# Optimizing a Trainium2 kernel written in Bass

```python
import jax, jax.numpy as jnp
from jax import lax
import numpy as np
import jax
import jax.numpy as jnp

D_MODEL = 1024
BATCH = 1
SEQ = 512
DEPTH = 2

A_HEADS = 16
A_KV_HEADS = 4
A_HEAD_DIM = 64
A_REP = A_HEADS // A_KV_HEADS
IDX_HEADS = 8
IDX_DIM = 64
IDX_TOPK_MAX = 256
Q_BLOCK = 128
A_Q = A_HEADS * A_HEAD_DIM
A_KV = A_KV_HEADS * A_HEAD_DIM
A_IN = A_Q + 2 * A_KV + IDX_HEADS * IDX_DIM + IDX_DIM + IDX_HEADS
A_SPLITS = (A_Q, A_Q + A_KV, A_Q + 2 * A_KV, A_Q + 2 * A_KV + IDX_HEADS * IDX_DIM,
            A_Q + 2 * A_KV + IDX_HEADS * IDX_DIM + IDX_DIM)

B_HEADS = 4
B_DK = D_MODEL // 2 // B_HEADS
B_DV = D_MODEL // B_HEADS
B_GATE_RANK = 16
B_GATE_TAU = 16.0
B_CHUNK = 64
B_QK = B_HEADS * B_DK
B_V = B_HEADS * B_DV
B_IN = 2 * B_QK + 2 * B_V + B_GATE_RANK
B_SPLITS = (B_QK, 2 * B_QK, 2 * B_QK + B_V, 2 * B_QK + 2 * B_V)

D_FF = 4 * D_MODEL

ROPE_THETA = 500000.0
ROT_DIM = A_HEAD_DIM // 4
LN_EPS = 1e-5
RMS_EPS = 1e-6
DN_ALPHA = (2 * DEPTH) ** 0.25
DN_BETA = (8 * DEPTH) ** -0.25
N_A_LAYERS = (DEPTH + 1) // 2
N_B_LAYERS = DEPTH // 2


def layer_norm(x, g, b):
    xf = x.astype(jnp.float32)
    mu = jnp.mean(xf, axis=-1, keepdims=True)
    var = jnp.mean(jnp.square(xf - mu), axis=-1, keepdims=True)
    return ((xf - mu) * lax.rsqrt(var + LN_EPS) * g + b).astype(x.dtype)

def rotary_tables(positions):
    inv = ROPE_THETA ** (-jnp.arange(0, ROT_DIM, 2, dtype=jnp.float32) / ROT_DIM)
    ang = positions.astype(jnp.float32)[..., None] * inv
    return jnp.cos(ang), jnp.sin(ang)

def partial_rotary(t, cos, sin):
    half = cos.shape[-1]
    shape = cos.shape[:2] + (1,) * (t.ndim - 3) + (half,)
    c = cos.reshape(shape)
    s = sin.reshape(shape)
    t1 = t[..., :half].astype(jnp.float32)
    t2 = t[..., half:2 * half].astype(jnp.float32)
    return jnp.concatenate([(t1 * c - t2 * s).astype(t.dtype),
                            (t2 * c + t1 * s).astype(t.dtype),
                            t[..., 2 * half:]], axis=-1)

def dsa_mixer(x, cos, sin, w_in, w_o):
    bsz, L, _ = x.shape
    top_k = min(IDX_TOPK_MAX, L // 4)
    proj = x @ w_in
    q, k, v, iq, ik, iw = jnp.split(proj, A_SPLITS, axis=-1)
    q = partial_rotary(q.reshape(bsz, L, A_HEADS, A_HEAD_DIM), cos, sin)
    k = partial_rotary(k.reshape(bsz, L, A_KV_HEADS, A_HEAD_DIM), cos, sin)
    v = v.reshape(bsz, L, A_KV_HEADS, A_HEAD_DIM)
    iq = partial_rotary(iq.reshape(bsz, L, IDX_HEADS, IDX_DIM), cos, sin)
    ik = partial_rotary(ik, cos, sin)
    iw = iw.astype(jnp.float32) * IDX_HEADS ** -0.5
    key_idx = jnp.arange(L)

    def block(i):
        start = i * Q_BLOCK
        q_idx = start + jnp.arange(Q_BLOCK)
        iq_b = lax.dynamic_slice_in_dim(iq, start, Q_BLOCK, axis=1)
        iw_b = lax.dynamic_slice_in_dim(iw, start, Q_BLOCK, axis=1)
        s = jnp.einsum('bqhd,bsd->bqhs', iq_b, ik, preferred_element_type=jnp.float32) * IDX_DIM ** -0.5
        score = jnp.einsum('bqh,bqhs->bqs', iw_b, jax.nn.relu(s))
        causal = key_idx[None, :] <= q_idx[:, None]
        score = jnp.where(causal[None], score, -jnp.inf)
        _, sel = lax.top_k(score, top_k)
        valid = sel <= q_idx[None, :, None]
        k_sel = jax.vmap(lambda kk, ii: kk[ii])(k, sel)
        v_sel = jax.vmap(lambda vv, ii: vv[ii])(v, sel)
        q_b = lax.dynamic_slice_in_dim(q, start, Q_BLOCK, axis=1).reshape(bsz, Q_BLOCK, A_KV_HEADS, A_REP, A_HEAD_DIM)
        logits = jnp.einsum('bqgrd,bqkgd->bqgrk', q_b, k_sel, preferred_element_type=jnp.float32) * A_HEAD_DIM ** -0.5
        logits = jnp.where(valid[:, :, None, None, :], logits, -jnp.inf)
        p = jax.nn.softmax(logits, axis=-1)
        o = jnp.einsum('bqgrk,bqkgd->bqgrd', p.astype(v.dtype), v_sel)
        return o.reshape(bsz, Q_BLOCK, A_Q)

    out = lax.map(block, jnp.arange(L // Q_BLOCK))
    out = out.transpose(1, 0, 2, 3).reshape(bsz, L, A_Q)
    return out @ w_o

def gla_mixer(x, w_in, w_a2, b_a, g_norm, w_o):
    bsz, L, _ = x.shape
    n_c = L // B_CHUNK
    proj = x @ w_in
    q, k, v, r, a_low = jnp.split(proj, B_SPLITS, axis=-1)
    log_a = jax.nn.log_sigmoid((a_low @ w_a2 + b_a).astype(jnp.float32)) / B_GATE_TAU

    def to_chunks(t, d):
        return t.astype(jnp.float32).reshape(bsz, n_c, B_CHUNK, B_HEADS, d).transpose(1, 0, 3, 2, 4)

    qc = to_chunks(q, B_DK) * B_DK ** -0.5
    kc = to_chunks(k, B_DK)
    vc = to_chunks(v, B_DV)
    gc = to_chunks(log_a, B_DK)
    mask = jnp.tril(jnp.ones((B_CHUNK, B_CHUNK), dtype=bool))

    def step(state, inp):
        qi, ki, vi, gi = inp
        b = jnp.cumsum(gi, axis=2)
        b_last = b[:, :, -1:, :]
        diff = jnp.where(mask[None, None, :, :, None], b[:, :, :, None, :] - b[:, :, None, :, :], -jnp.inf)
        attn = jnp.einsum('bhid,bhjd,bhijd->bhij', qi, ki, jnp.exp(diff))
        intra = jnp.einsum('bhij,bhje->bhie', attn, vi)
        inter = jnp.einsum('bhid,bhde->bhie', qi * jnp.exp(b), state)
        new_state = jnp.exp(b_last)[:, :, 0, :, None] * state + jnp.einsum('bhjd,bhje->bhde', ki * jnp.exp(b_last - b), vi)
        return new_state, intra + inter

    state0 = jnp.zeros((bsz, B_HEADS, B_DK, B_DV), jnp.float32)
    _, outs = lax.scan(step, state0, (qc, kc, vc, gc))
    o = outs.transpose(1, 0, 3, 2, 4).reshape(bsz, L, B_HEADS, B_DV)
    o = o * lax.rsqrt(jnp.mean(jnp.square(o), axis=-1, keepdims=True) + RMS_EPS) * g_norm
    gate = jax.nn.silu(r.astype(jnp.float32).reshape(bsz, L, B_HEADS, B_DV))
    y = (o * gate).reshape(bsz, L, B_V).astype(x.dtype)
    return y @ w_o

def squared_relu_mlp(x, w_up, w_down):
    return jnp.square(jax.nn.relu(x @ w_up)) @ w_down

def first_inputs(seed: int = 0) -> dict:
    key = jax.random.key(seed)
    ks = jax.random.split(key, 16)
    f32 = jnp.float32

    def nrm(k, shape, fan_in, scale=1.0):
        return jax.random.normal(k, shape, f32) * (scale * fan_in ** -0.5)

    x = jax.random.normal(ks[0], (BATCH, SEQ, D_MODEL), f32)
    positions = jnp.broadcast_to(jnp.arange(SEQ, dtype=jnp.int32), (BATCH, SEQ))
    a_w_in = nrm(ks[1], (N_A_LAYERS, D_MODEL, A_IN), D_MODEL)
    a_w_o = nrm(ks[2], (N_A_LAYERS, A_Q, D_MODEL), A_Q, DN_BETA)
    b_w_in = nrm(ks[3], (N_B_LAYERS, D_MODEL, B_IN), D_MODEL)
    b_w_a2 = nrm(ks[4], (N_B_LAYERS, B_GATE_RANK, B_QK), B_GATE_RANK)
    b_b_a = 0.1 * jax.random.normal(ks[5], (N_B_LAYERS, B_QK), f32)
    b_g_norm = 1.0 + 0.02 * jax.random.normal(ks[6], (N_B_LAYERS, B_DV), f32)
    b_w_o = nrm(ks[7], (N_B_LAYERS, B_V, D_MODEL), B_V, DN_BETA)
    ln_mix_g = 1.0 + 0.02 * jax.random.normal(ks[8], (DEPTH, D_MODEL), f32)
    ln_mix_b = 0.02 * jax.random.normal(ks[9], (DEPTH, D_MODEL), f32)
    mlp_w_up = nrm(ks[10], (DEPTH, D_MODEL, D_FF), D_MODEL)
    mlp_w_down = nrm(ks[11], (DEPTH, D_FF, D_MODEL), D_FF, DN_BETA)
    ln_mlp_g = 1.0 + 0.02 * jax.random.normal(ks[12], (DEPTH, D_MODEL), f32)
    ln_mlp_b = 0.02 * jax.random.normal(ks[13], (DEPTH, D_MODEL), f32)
    return {'x': x, 'positions': positions, 'a_w_in': a_w_in, 'a_w_o': a_w_o,
            'b_w_in': b_w_in, 'b_w_a2': b_w_a2, 'b_b_a': b_b_a, 'b_g_norm': b_g_norm, 'b_w_o': b_w_o,
            'ln_mix_g': ln_mix_g, 'ln_mix_b': ln_mix_b, 'mlp_w_up': mlp_w_up, 'mlp_w_down': mlp_w_down,
            'ln_mlp_g': ln_mlp_g, 'ln_mlp_b': ln_mlp_b}

def first_block(x, positions, a_w_in, a_w_o, b_w_in, b_w_a2, b_b_a, b_g_norm, b_w_o,
              ln_mix_g, ln_mix_b, mlp_w_up, mlp_w_down, ln_mlp_g, ln_mlp_b):
    cos, sin = rotary_tables(positions)
    h = x
    for i in range(DEPTH):
        j = i // 2
        if i % 2 == 0:
            mix = dsa_mixer(h, cos, sin, a_w_in[j], a_w_o[j])
        else:
            mix = gla_mixer(h, b_w_in[j], b_w_a2[j], b_b_a[j], b_g_norm[j], b_w_o[j])
        h = layer_norm(DN_ALPHA * h + mix, ln_mix_g[i], ln_mix_b[i])
        h = layer_norm(DN_ALPHA * h + squared_relu_mlp(h, mlp_w_up[i], mlp_w_down[i]), ln_mlp_g[i], ln_mlp_b[i])
    return h


DEPTH_2 = 1

GRID_W = 64
EPS = 1e-6
ATTN_HEADS = 8
ATTN_KV_HEADS = 2
ATTN_HEAD_DIM = 64
ATTN_WIDTH = ATTN_HEADS * ATTN_HEAD_DIM
KV_WIDTH = ATTN_KV_HEADS * ATTN_HEAD_DIM
ROPE_THETA_2 = 10000.0
MLSTM_HEADS = 4
MLSTM_HEAD_DIM = 128
MLSTM_WIDTH = MLSTM_HEADS * MLSTM_HEAD_DIM
MLSTM_CHUNK = 64
CONV_WIDTH = 5
N_GATES = 4 * MLSTM_HEADS
FORGET_BIAS_LO = 3.0
FORGET_BIAS_HI = 6.0
MIX_WIDTH = ATTN_WIDTH + MLSTM_WIDTH
IN_PROJ_WIDTH = ATTN_WIDTH + 2 * KV_WIDTH + 4 * MLSTM_WIDTH + N_GATES
FFN_HIDDEN = 256 * ((8 * D_MODEL + 3 * 256 - 1) // (3 * 256))


def rms_norm(x, g):
    xf = x.astype(jnp.float32)
    y = xf * lax.rsqrt(jnp.mean(xf * xf, axis=-1, keepdims=True) + EPS)
    return (y * g.astype(jnp.float32)).astype(x.dtype)

def modulate(h, shift, scale):
    return h * (1.0 + scale[:, None, :]) + shift[:, None, :]

def axial_rope_tables(seq):
    rows = seq // GRID_W
    row = jnp.repeat(jnp.arange(rows, dtype=jnp.float32), GRID_W)
    col = jnp.tile(jnp.arange(GRID_W, dtype=jnp.float32), rows)
    axis_dim = ATTN_HEAD_DIM // 2
    inv_freq = ROPE_THETA_2 ** (-jnp.arange(0, axis_dim, 2, dtype=jnp.float32) / axis_dim)
    ang_row = row[:, None] * inv_freq[None, :]
    ang_col = col[:, None] * inv_freq[None, :]
    return (jnp.cos(ang_row), jnp.sin(ang_row), jnp.cos(ang_col), jnp.sin(ang_col))

def rotate_pairs(x, cos, sin):
    x1, x2 = jnp.split(x, 2, axis=-1)
    cos = cos[:, None, :]
    sin = sin[:, None, :]
    return jnp.concatenate([x1 * cos - x2 * sin, x2 * cos + x1 * sin], axis=-1)

def apply_axial_rope(x, tables):
    cos_r, sin_r, cos_c, sin_c = tables
    x_row, x_col = jnp.split(x.astype(jnp.float32), 2, axis=-1)
    out = jnp.concatenate([rotate_pairs(x_row, cos_r, sin_r), rotate_pairs(x_col, cos_c, sin_c)], axis=-1)
    return out.astype(x.dtype)

def axial_gqa_attention(q, k, v, q_g, k_g, tables):
    B, S, _ = q.shape
    G = ATTN_HEADS // ATTN_KV_HEADS
    q = q.reshape(B, S, ATTN_HEADS, ATTN_HEAD_DIM)
    k = k.reshape(B, S, ATTN_KV_HEADS, ATTN_HEAD_DIM)
    v = v.reshape(B, S, ATTN_KV_HEADS, ATTN_HEAD_DIM)
    q = apply_axial_rope(rms_norm(q, q_g), tables)
    k = apply_axial_rope(rms_norm(k, k_g), tables)
    n_blocks = S // Q_BLOCK
    qb = q.reshape(B, n_blocks, Q_BLOCK, ATTN_KV_HEADS, G, ATTN_HEAD_DIM).transpose(1, 0, 3, 4, 2, 5)
    kt = k.transpose(0, 2, 1, 3)
    vt = v.transpose(0, 2, 1, 3)
    scale = ATTN_HEAD_DIM ** -0.5

    def one_block(q_blk):
        s = jnp.einsum('bkgqd,bksd->bkgqs', q_blk, kt).astype(jnp.float32) * scale
        p = jax.nn.softmax(s, axis=-1).astype(vt.dtype)
        return jnp.einsum('bkgqs,bksd->bkgqd', p, vt)

    o = lax.map(one_block, qb)
    return o.transpose(1, 0, 4, 2, 3, 5).reshape(B, S, ATTN_WIDTH)

def mlstm_chunkwise(q, k, v, i_pre, log_f):
    B, H, S, D = q.shape
    L = MLSTM_CHUNK
    nc = S // L

    def to_chunks(a):
        return jnp.moveaxis(a.reshape((B, H, nc, L) + a.shape[3:]), 2, 0)

    xs = (to_chunks(q), to_chunks(k), to_chunks(v), to_chunks(i_pre), to_chunks(log_f))
    tril = jnp.tril(jnp.ones((L, L), dtype=bool))

    def step(carry, chunk):
        C, n, m = carry
        qc, kc, vc, ic, fc = chunk
        b = jnp.cumsum(fc, axis=-1)
        g = b[..., -1]
        d = b[..., :, None] - b[..., None, :] + ic[..., None, :]
        d = jnp.where(tril, d, -jnp.inf)
        m_inter = b + m[..., None]
        m_t = jnp.maximum(m_inter, jnp.max(d, axis=-1))
        w_inter = jnp.exp(m_inter - m_t)
        p = jnp.exp(d - m_t[..., None])
        s = jnp.einsum('bhtd,bhsd->bhts', qc, kc) * p
        num = w_inter[..., None] * jnp.einsum('bhvd,bhtd->bhtv', C, qc) + jnp.einsum('bhts,bhsv->bhtv', s, vc)
        den = w_inter * jnp.einsum('bhd,bhtd->bht', n, qc) + jnp.sum(s, axis=-1)
        h = num / jnp.maximum(jnp.abs(den), jnp.exp(-m_t))[..., None]
        a = g[..., None] - b + ic
        m_new = jnp.maximum(g + m, jnp.max(a, axis=-1))
        decay = jnp.exp(g + m - m_new)
        w = jnp.exp(a - m_new[..., None])
        C = decay[..., None, None] * C + jnp.einsum('bhs,bhsv,bhsd->bhvd', w, vc, kc)
        n = decay[..., None] * n + jnp.einsum('bhs,bhsd->bhd', w, kc)
        return (C, n, m_new), h

    init = (jnp.zeros((B, H, D, D), jnp.float32), jnp.zeros((B, H, D), jnp.float32), jnp.zeros((B, H), jnp.float32))
    _, h = lax.scan(step, init, xs)
    return jnp.moveaxis(h, 0, 2).reshape(B, H, S, D)

def centred_depthwise_conv(x, w, b):
    ch = x.shape[-1]
    y = lax.conv_general_dilated(x, w[:, None, :].astype(x.dtype), window_strides=(1,),
                                 padding=[(CONV_WIDTH // 2, CONV_WIDTH // 2)],
                                 dimension_numbers=('NWC', 'WIO', 'NWC'), feature_group_count=ch)
    return y + b.astype(x.dtype)

def bidirectional_mlstm(qk_pre, v, o_pre, gate_pre, conv_w, conv_b, gate_b, norm_g):
    B, S, _ = v.shape
    qk = jax.nn.silu(centred_depthwise_conv(qk_pre, conv_w, conv_b))
    q, k = jnp.split(qk, 2, axis=-1)

    def heads(a):
        return a.astype(jnp.float32).reshape(B, S, MLSTM_HEADS, MLSTM_HEAD_DIM).transpose(0, 2, 1, 3)

    qh = heads(q)
    kh = heads(k) * MLSTM_HEAD_DIM ** -0.5
    vh = heads(v)
    g = (gate_pre.astype(jnp.float32) + gate_b.astype(jnp.float32)).reshape(B, S, 4, MLSTM_HEADS)
    g = g.transpose(2, 0, 3, 1)
    i_fw, f_fw, i_bw, f_bw = g[0], g[1], g[2], g[3]
    h_fw = mlstm_chunkwise(qh, kh, vh, i_fw, jax.nn.log_sigmoid(f_fw))
    flip = lambda a: jnp.flip(a, axis=2)
    h_bw = flip(mlstm_chunkwise(flip(qh), flip(kh), flip(vh), flip(i_bw), flip(jax.nn.log_sigmoid(f_bw))))
    h = (h_fw + h_bw).transpose(0, 2, 1, 3)
    h = h * lax.rsqrt(jnp.mean(h * h, axis=-1, keepdims=True) + EPS)
    h = h * norm_g.astype(jnp.float32).reshape(MLSTM_HEADS, MLSTM_HEAD_DIM)
    h = h.reshape(B, S, MLSTM_WIDTH) * jax.nn.sigmoid(o_pre.astype(jnp.float32))
    return h.astype(v.dtype)

def second_inputs(seed: int = 0) -> dict:
    key = jax.random.key(seed)
    ks = jax.random.split(key, 18)
    nrm = lambda k, shape, s: jax.random.normal(k, shape, jnp.float32) * s
    gain = lambda k, shape: 1.0 + nrm(k, shape, 0.02)
    f_bias = jnp.linspace(FORGET_BIAS_LO, FORGET_BIAS_HI, MLSTM_HEADS, dtype=jnp.float32)
    gate_offset = jnp.zeros((4, MLSTM_HEADS), jnp.float32).at[1].set(f_bias).at[3].set(f_bias)
    gate_b = (nrm(ks[10], (DEPTH_2, 4, MLSTM_HEADS), 0.1) + gate_offset).reshape(DEPTH_2, N_GATES)
    return {
        'x': nrm(ks[0], (BATCH, SEQ, D_MODEL), 1.0),
        'c': nrm(ks[1], (BATCH, D_MODEL), 1.0),
        'w_ada': nrm(ks[2], (DEPTH_2, D_MODEL, 6 * D_MODEL), D_MODEL ** -0.5),
        'b_ada': nrm(ks[3], (DEPTH_2, 6 * D_MODEL), 0.02),
        'norm_mix_g': gain(ks[4], (DEPTH_2, D_MODEL)),
        'w_in': nrm(ks[5], (DEPTH_2, D_MODEL, IN_PROJ_WIDTH), D_MODEL ** -0.5),
        'q_norm_g': gain(ks[6], (DEPTH_2, ATTN_HEAD_DIM)),
        'k_norm_g': gain(ks[7], (DEPTH_2, ATTN_HEAD_DIM)),
        'conv_w': nrm(ks[8], (DEPTH_2, CONV_WIDTH, 2 * MLSTM_WIDTH), CONV_WIDTH ** -0.5),
        'conv_b': nrm(ks[9], (DEPTH_2, 2 * MLSTM_WIDTH), 0.02),
        'gate_b': gate_b,
        'mlstm_norm_g': gain(ks[11], (DEPTH_2, MLSTM_WIDTH)),
        'w_out': nrm(ks[12], (DEPTH_2, MIX_WIDTH, D_MODEL), MIX_WIDTH ** -0.5),
        'norm_ffn_g': gain(ks[13], (DEPTH_2, D_MODEL)),
        'w_gate': nrm(ks[14], (DEPTH_2, D_MODEL, FFN_HIDDEN), D_MODEL ** -0.5),
        'w_up': nrm(ks[15], (DEPTH_2, D_MODEL, FFN_HIDDEN), D_MODEL ** -0.5),
        'w_down': nrm(ks[16], (DEPTH_2, FFN_HIDDEN, D_MODEL), FFN_HIDDEN ** -0.5),
        'final_norm_g': gain(ks[17], (D_MODEL,)),
    }

def second_block(x, c, w_ada, b_ada, norm_mix_g, w_in, q_norm_g, k_norm_g, conv_w, conv_b, gate_b,
              mlstm_norm_g, w_out, norm_ffn_g, w_gate, w_up, w_down, final_norm_g):
    S = x.shape[1]
    tables = axial_rope_tables(S)
    cond = jax.nn.silu(c)
    splits = [ATTN_WIDTH,
              ATTN_WIDTH + KV_WIDTH,
              ATTN_WIDTH + 2 * KV_WIDTH,
              ATTN_WIDTH + 2 * KV_WIDTH + 2 * MLSTM_WIDTH,
              ATTN_WIDTH + 2 * KV_WIDTH + 3 * MLSTM_WIDTH,
              ATTN_WIDTH + 2 * KV_WIDTH + 4 * MLSTM_WIDTH]
    for l in range(DEPTH_2):
        mod = cond @ w_ada[l] + b_ada[l]
        sh1, sc1, g1, sh2, sc2, g2 = jnp.split(mod, 6, axis=-1)
        h = modulate(rms_norm(x, norm_mix_g[l]), sh1, sc1)
        proj = h @ w_in[l]
        q_a, k_a, v_a, qk_m, v_m, o_m, gates = jnp.split(proj, splits, axis=-1)
        y_attn = axial_gqa_attention(q_a, k_a, v_a, q_norm_g[l], k_norm_g[l], tables)
        y_mem = bidirectional_mlstm(qk_m, v_m, o_m, gates, conv_w[l], conv_b[l], gate_b[l], mlstm_norm_g[l])
        mix = jnp.concatenate([y_attn, y_mem], axis=-1) @ w_out[l]
        x = x + g1[:, None, :] * mix
        h = modulate(rms_norm(x, norm_ffn_g[l]), sh2, sc2)
        ffn = (jax.nn.silu(h @ w_gate[l]) * (h @ w_up[l])) @ w_down[l]
        x = x + g2[:, None, :] * ffn
    return rms_norm(x, final_norm_g)


def setup_inputs(seed=0):
    out = dict(first_inputs(seed))
    for name, value in second_inputs(seed + 1).items():
        if name != "x":
            out[name + "_2"] = value
    return out


def reference(
    x, positions, a_w_in, a_w_o, b_w_in, b_w_a2, b_b_a, b_g_norm, b_w_o, ln_mix_g, ln_mix_b,
    mlp_w_up, mlp_w_down, ln_mlp_g, ln_mlp_b, c_2, w_ada_2, b_ada_2, norm_mix_g_2, w_in_2,
    q_norm_g_2, k_norm_g_2, conv_w_2, conv_b_2, gate_b_2, mlstm_norm_g_2, w_out_2, norm_ffn_g_2,
    w_gate_2, w_up_2, w_down_2, final_norm_g_2,
):
    x = first_block(
        x, positions, a_w_in, a_w_o, b_w_in, b_w_a2, b_b_a, b_g_norm, b_w_o, ln_mix_g, ln_mix_b,
        mlp_w_up, mlp_w_down, ln_mlp_g, ln_mlp_b,
    )
    return second_block(
        x, c_2, w_ada_2, b_ada_2, norm_mix_g_2, w_in_2, q_norm_g_2, k_norm_g_2, conv_w_2,
        conv_b_2, gate_b_2, mlstm_norm_g_2, w_out_2, norm_ffn_g_2, w_gate_2, w_up_2, w_down_2,
        final_norm_g_2,
    )


_drawn_inputs = setup_inputs


def setup_inputs(seed=0):
    import zlib

    import numpy as np

    out = dict(_drawn_inputs(seed))
    spreads = {}
    factors = {'b_b_a': 5.668,
     'b_g_norm': 8.0,
     'norm_mix_g_2': 8.0,
     'q_norm_g_2': 8.0,
     'k_norm_g_2': 8.0,
     'conv_b_2': 200.0,
     'mlstm_norm_g_2': 31.79,
     'norm_ffn_g_2': 11.503,
     'final_norm_g_2': 22.954}
    for name, (base, spread) in spreads.items():
        noise = np.random.default_rng([zlib.crc32(name.encode()), seed]).standard_normal(out[name].shape)
        drawn = base * np.exp(spread * noise) if base else spread * noise
        out[name] = jnp.asarray(drawn.astype(out[name].dtype))
    for name, factor in factors.items():
        out[name] = (out[name] * factor).astype(out[name].dtype)
    return out
```

```python
from contextlib import ExitStack

import numpy as np
import concourse.bass as bass
from concourse import mybir

F = mybir.dt.float32
R = mybir.dt.float32r
I32 = mybir.dt.int32
U8 = mybir.dt.uint8
ALU = mybir.AluOpType
ACT = mybir.ActivationFunctionType
AX = mybir.AxisListType.X

P = 128
T = 4
SEQ = 512
D = 1024
ALPHA = 4.0 ** 0.25
BIG = 1e30
NRAW = 3
NHL = 2
CH = 2048
LEVELS = [64, 32, 16, 8, 4, 2, 1]

C_ID, C_CB, C_CBT, C_ONE, C_SEL, C_INV, C_RC, C_RS = 0, 128, 256, 384, 512, 1024, 1032, 1288
C_END = 1544


def constants():
    c = np.zeros((P, C_END), np.float32)
    i = np.arange(P)
    c[:, C_ID:C_ID + P] = np.eye(P)
    c[:, C_CB:C_CB + P] = np.where(i[None, :] > i[:, None], -BIG, 0.0)
    c[:, C_CBT:C_CBT + P] = np.where(i[None, :] < i[:, None], -BIG, 0.0)
    c[:, C_ONE:C_ONE + P] = 1.0
    for h in range(4):
        c[h, C_SEL + h * P:C_SEL + (h + 1) * P] = -1.0
    c[:, C_INV:C_INV + 8] = np.float32(500000.0) ** (-np.arange(0, 16, 2, dtype=np.float32) / np.float32(16))
    inv = np.float32(10000.0) ** (-np.arange(0, 32, 2, dtype=np.float32) / np.float32(32))
    for t in range(T):
        tok = t * P + i
        ar = (tok // 64).astype(np.float32)[:, None] * inv[None, :]
        ac = (tok % 64).astype(np.float32)[:, None] * inv[None, :]
        c[:, C_RC + t * 64:C_RC + t * 64 + 64] = np.concatenate([np.cos(ar), np.cos(ar), np.cos(ac), np.cos(ac)], 1)
        c[:, C_RS + t * 64:C_RS + t * 64 + 64] = np.concatenate([-np.sin(ar), np.sin(ar), -np.sin(ac), np.sin(ac)], 1)
    m = np.zeros((P, 8, P), np.float32)
    for n, s in enumerate(LEVELS):
        j, k = i[:, None], i[None, :]
        m[:, n, :] = (j // (2 * s) == k // (2 * s)) & (j % (2 * s) < s) & (k % (2 * s) >= s)
    m[:, 7, :] = np.eye(P)
    return c, m.reshape(P, 8 * P)


class Line:

    def __init__(self, sem):
        self.sem, self.n, self.todo, self.seen = sem, 0, [], {}

    def put(self, after, fn, mark=True):
        for tok in after:
            if tok is None:
                continue
            sem, v = tok
            if self.seen.get(sem.name, 0) < v:
                self.seen[sem.name] = v
                self.todo.append(lambda e, s=sem, v=v: e.wait_ge(s, v))
        if not mark:
            self.todo.append(fn)
            return None
        self.n += 1
        self.todo.append(lambda e: fn(e).then_inc(self.sem, 1))
        return (self.sem, self.n)

    def last(self):
        return (self.sem, self.n)


def program(nc, x, positions, a_w_in, a_w_o, b_w_in, b_w_a2, b_b_a, b_g_norm, b_w_o, ln_mix_g, ln_mix_b,
            mlp_w_up, mlp_w_down, ln_mlp_g, ln_mlp_b, c_2, w_ada_2, b_ada_2, norm_mix_g_2, w_in_2, q_norm_g_2,
            k_norm_g_2, conv_w_2, conv_b_2, gate_b_2, mlstm_norm_g_2, w_out_2, norm_ffn_g_2, w_gate_2, w_up_2,
            w_down_2, final_norm_g_2, cst, lmask, cols, posn, out, dbg=None):
    ctx = ExitStack()
    with ctx:
        def sb(name, shape, dt=F):
            return ctx.enter_context(nc.sbuf_tensor(name, shape, dt))

        def sem(name):
            return ctx.enter_context(nc.semaphore(name))

        h = sb("h", [P, T, D])
        xh = sb("xh", [P, 8, SEQ], R)
        xl = sb("xl", [P, 8, SEQ], R)
        raw = sb("raw", [P, NRAW, CH])
        wh = sb("wh", [P, NHL, CH], R)
        wl = sb("wl", [P, NHL, CH], R)
        uh = sb("uh", [P, 2, 4, SEQ], R)
        ul = sb("ul", [P, 2, 4, SEQ], R)
        C = sb("C", [P, C_END])
        LM = sb("LM", [P, 8 * P], U8)
        gb = sb("gb", [P, 2048])
        A = sb("A", [P, 13344])
        small = sb("small", [P, 256])
        stats = sb("stats", [P, T, 2, 6])
        mv = sb("mv", [P, T, 2])
        rsv = sb("rsv", [P, 32])
        rsy = sb("rsy", [P, 32])
        rsa = sb("rsa", [P, 32])
        posi = sb("posi", [P, T], I32)
        bank = [ctx.enter_context(nc.psum_tensor(f"bank{i}", [P, 512], F)) for i in range(8)]

        PE, DVE, ACTE, POOL, SP = (Line(sem(n)) for n in ("s_pe", "s_dve", "s_act", "s_pool", "s_sp"))
        s_raw = [sem(f"s_raw{i}") for i in range(NRAW)]
        s_in = sem("s_in")
        s_gb = sem("s_gb")
        s_acc = sem("s_acc")
        s_out = sem("s_out")
        s_dbg = sem("s_dbg")

        ident = C[:, C_ID:C_ID + P]
        ones = C[:, C_ONE:C_ONE + P]
        CB = C[:, C_CB:C_CB + P]
        CBT = C[:, C_CBT:C_CBT + P]
        dumps = [0]

        def dump(name, ap, after):
            if dbg is None or name not in dbg:
                return
            dst = dbg[name]
            SP.put(after, lambda e: e.dma_start(dst, ap).then_inc(s_dbg, 16), mark=False)
            dumps[0] += 1
            SP.todo.append(lambda e, v=16 * dumps[0]: e.wait_ge(s_dbg, v))

        bfree = [None] * 8
        bnext = [0]

        held = set()

        def take(hold=False):
            while bnext[0] in held:
                bnext[0] = (bnext[0] + 1) % 8
            b = bnext[0]
            bnext[0] = (b + 1) % 8
            if hold:
                held.add(b)
            return b

        def v(fn, after=()):
            return DVE.put(after, fn)

        def a(fn, after=()):
            return ACTE.put(after, fn)

        def g(fn, after=()):
            return POOL.put(after, fn)

        def mm(out_, l, r, start, stop, after=(), mark=False):
            return PE.put(after, lambda e: e.matmul(out_, l, r, start=start, stop=stop), mark)

        def mm_group(out_, pairs, after=(), mark=True):
            tok = None
            for i, (l, r) in enumerate(pairs):
                tok = mm(out_, l, r, i == 0, i == len(pairs) - 1, after if i == 0 else (), mark and i == len(pairs) - 1)
            return tok

        def tr(out_, in_, idn, after=(), mark=False):
            return PE.put(after, lambda e: e.transpose(out_, in_, idn), mark)

        n_in = [0]

        def load(dst, src):
            n_in[0] += 1
            SP.put((), lambda e: e.dma_start(dst, src).then_inc(s_in, 16), mark=False)

        def col(n, w):
            return small[:, n:n + w]

        load(posi[:, :], posn)
        load(C[:, :], cst)
        for t in range(T):
            load(h[:, t, :], x[0, t * P:(t + 1) * P, :])
        load(A[:, 12288:13312], lmask)
        load(col(0, 80), cols)
        BA, CC, GM, GF, CVB = col(0, 4), col(8, 8), col(16, 8), col(24, 8), col(72, 8)
        CW = col(32, 40).rearrange("p (w k) -> p w k", k=8)
        GB = col(80, 16)
        load(GB, gate_b_2[0].partition_broadcast(P))
        SH1, SC1, SH2, SC2 = col(96, 8), col(104, 8), col(112, 8), col(120, 8)
        CS1, CS2 = col(128, 8), col(136, 8)
        S0 = (s_in, 16 * n_in[0])

        v(lambda e: e.tensor_copy(LM[:, :], A[:, 12288:13312]), [S0])

        chunks = []

        def plan(w, r0, nk, c0, nc_):
            chunks.append((w[r0:r0 + nk * P, c0:c0 + nc_].rearrange("(k p) n -> p k n", p=P), nk, nc_))

        def plan_tok(w, c0, n):
            if n <= 256:
                plan(w, 0, 8, c0, n)
            else:
                plan(w, 0, 4, c0, n)
                plan(w, 512, 4, c0, n)

        wa, wb, w2 = a_w_in[0], b_w_in[0], w_in_2[0]

        def plan_mlp(i):
            for n in range(9):
                if n < 8:
                    plan(mlp_w_up[i], 0, 8, n * 512, 256)
                    plan(mlp_w_up[i], 0, 8, n * 512 + 256, 256)
                if n > 0:
                    for c in range(2):
                        plan(mlp_w_down[i], (n - 1) * 512, 4, c * 512, 512)

        plan_tok(wa, 1536, 512)
        plan_tok(wa, 2048, 72)
        plan_tok(wa, 1024, 512)
        plan_tok(wa, 0, 512)
        plan_tok(wa, 512, 512)
        plan_tok(a_w_o[0], 0, 512)
        plan_tok(a_w_o[0], 512, 512)
        plan_mlp(0)
        plan(wb, 0, 8, 3072, 16)
        for n in range(4):
            plan(wb, 0, 8, n * 256, 256)
        for n in range(4):
            plan_tok(wb, 1024 + 512 * n, 512)
        plan_tok(b_w_o[0], 0, 512)
        plan_tok(b_w_o[0], 512, 512)
        plan_mlp(1)
        plan_ada = []

        def ada_plan(r):
            for k in range(8):
                plan(w_ada_2[0], k * P, 1, r * 2048, 2048)

        ada_plan(0)
        plan_tok(w2, 0, 512)
        plan_tok(w2, 512, 256)
        for n in range(4):
            plan(w2, 0, 8, 768 + n * 256, 256)
        plan_tok(w2, 1792, 512)
        plan_tok(w2, 2816, 16)
        ada_plan(1)
        ada_plan(2)
        plan_tok(w2, 2304, 512)
        plan_tok(w_out_2[0], 0, 512)
        plan_tok(w_out_2[0], 512, 512)
        FG = [(0, 4), (4, 4), (8, 4), (12, 4), (16, 4), (20, 2)]
        for n in range(len(FG) + 1):
            if n < len(FG):
                f0, nf = FG[n]
                for q in range(nf // 2):
                    plan(w_gate_2[0], 0, 8, (f0 + 2 * q) * P, 256)
                    plan(w_up_2[0], 0, 8, (f0 + 2 * q) * P, 256)
            if n > 0:
                f0, nf = FG[n - 1]
                for c in range(2):
                    plan(w_down_2[0], f0 * P, nf, c * 512, 512)

        used = [0]
        prepped = [0]
        loaded = [0]
        raw_free = [None] * NRAW
        hl_free = [None] * NHL
        ready = {}
        is_ada = set()
        pos = 0
        for n, (src, nk, ncol) in enumerate(chunks):
            if nk == 1:
                is_ada.add(n)

        def fetch(i):
            if i >= len(chunks):
                return
            src, nk, ncol = chunks[i]
            s = i % NRAW
            dst = raw[:, s, 0:nk * ncol].rearrange("p (k n) -> p k n", k=nk)
            SP.put([raw_free[s]], lambda e: e.dma_start(dst, src).then_inc(s_raw[s], 16), mark=False)

        def landed(i):
            return (s_raw[i % NRAW], 16 * (i // NRAW + 1))

        slot_of = {}
        nsplit = [0]

        def split_chunk(i):
            if i >= len(chunks) or i in is_ada:
                return
            src, nk, ncol = chunks[i]
            r, n = i % NRAW, nk * ncol
            s = nsplit[0] % NHL
            nsplit[0] += 1
            slot_of[i] = s
            t1 = a(lambda e: e.activation(wh[:, s, 0:n], raw[:, r, 0:n], ACT.Copy), [landed(i), hl_free[s]])
            t2 = v(lambda e: e.tensor_tensor(wl[:, s, 0:n], raw[:, r, 0:n], wh[:, s, 0:n].bitcast(F), ALU.subtract),
                   [landed(i), t1])
            raw_free[r] = t2
            ready[i] = t2
            fetch(i + NRAW)

        def next_chunk():
            i = used[0]
            used[0] += 1
            while prepped[0] <= i + 1 and prepped[0] < len(chunks):
                if prepped[0] in is_ada:
                    break
                split_chunk(prepped[0])
                prepped[0] += 1
            src, nk, ncol = chunks[i]
            s = slot_of[i]
            H = wh[:, s, 0:nk * ncol].rearrange("p (k n) -> p k n", k=nk)
            L = wl[:, s, 0:nk * ncol].rearrange("p (k n) -> p k n", k=nk)
            return H, L, ready[i], s, nk, ncol

        def next_ada():
            i = used[0]
            used[0] += 1
            assert i in is_ada
            prepped[0] = max(prepped[0], i + 1)
            return i

        for i in range(NRAW):
            fetch(i)

        def gemm_tok(n, hi, lo, ready_x, evac):
            bs = [take() for _ in range(T)]
            k0 = 0
            rx = ready_x
            while k0 < 8:
                H, L, rw, s, nk, ncol = next_chunk()
                assert ncol == n, (ncol, n)
                for t in range(T):
                    for k in range(nk):
                        kk = k0 + k
                        X, Y = hi[:, kk, t * P:(t + 1) * P], lo[:, kk, t * P:(t + 1) * P]
                        o = bank[bs[t]][:, 0:n]
                        first, end = kk == 0, kk == 7
                        mm(o, X, H[:, k, :], first, False, [rw, rx, bfree[bs[t]]] if first else [rw])
                        mm(o, X, L[:, k, :], False, False)
                        tok = mm(o, Y, H[:, k, :], False, end, mark=(k == nk - 1))
                    if end:
                        bfree[bs[t]] = evac(t, bank[bs[t]][:, 0:n], tok)
                hl_free[s] = PE.last()
                k0 += nk

        def gemm_T(hi, lo, ready_x, evac, width=P):
            H, L, rw, s, nk, ncol = next_chunk()
            assert nk == 8
            toks = []
            for j in range(max(1, ncol // P)):
                w = min(P, ncol)
                b = take()
                o = bank[b][0:w, :]
                for k in range(8):
                    c = slice(j * P, j * P + w)
                    mm(o, H[:, k, c], hi[:, k, :], k == 0, False, [rw, ready_x, bfree[b]] if k == 0 else ())
                    mm(o, L[:, k, c], hi[:, k, :], False, False)
                    tok = mm(o, H[:, k, c], lo[:, k, :], False, k == 7, mark=(k == 7))
                toks.append((j, b, o, tok))
            hl_free[s] = PE.last()
            for j, b, o, tok in toks:
                bfree[b] = evac(j, o, tok)

        def split(src, dh, dl, after):
            t1 = a(lambda e: e.activation(dh, src, ACT.Copy), after)
            return v(lambda e: e.tensor_tensor(dl, src, dh.bitcast(F), ALU.subtract), [t1])

        def to_T(src, toks, scale=None, shift=None, tmp=None):
            last = None
            for k in range(8):
                b = take()
                for t in range(T):
                    tok = tr(bank[b][:, t * P:(t + 1) * P], src[:, t, k * P:(k + 1) * P], ident,
                             [bfree[b], toks[t]], mark=(t == T - 1))
                if scale is None:
                    last = bfree[b] = split(bank[b][:, :], xh[:, k, :], xl[:, k, :], [tok])
                else:
                    m = tmp[k % 2]
                    t1 = v(lambda e, b=b, m=m, k=k: e.tensor_scalar(m, bank[b][:, :], scale[:, k:k + 1],
                                                                  shift[:, k:k + 1], ALU.mult, ALU.add), [tok, last])
                    bfree[b] = t1
                    last = split(m, xh[:, k, :], xl[:, k, :], [t1, tok])
            return last

        def rsqrt(dst, src, n, scale, eps, after):
            vv, yy, aa = rsv[:, 0:n], rsy[:, 0:n], rsa[:, 0:n]
            t1 = v(lambda e: e.tensor_scalar(vv, src, scale, eps, ALU.mult, ALU.add), after)
            t2 = a(lambda e: e.activation(yy, vv, ACT.Ln), [t1])
            t3 = a(lambda e: e.activation(yy, yy, ACT.Exp, scale=-0.5), [t2])
            t4 = v(lambda e: e.tensor_tensor(aa, yy, yy, ALU.mult), [t3])
            t5 = v(lambda e: e.tensor_tensor(aa, aa, vv, ALU.mult), [t4])
            t6 = v(lambda e: e.tensor_scalar(aa, aa, -0.5, 1.5, ALU.mult, ALU.add), [t5])
            return v(lambda e: e.tensor_tensor(dst, yy, aa, ALU.mult), [t6])

        ngb = [0]

        def load_gb(dst, src, after):
            ngb[0] += 1
            POOL.put(after, lambda e: e.dma_start(dst, src).then_inc(s_gb, 16), mark=False)
            return (s_gb, 16 * ngb[0])

        def layer_norm(gd, bd, ht):
            free = [DVE.last(), ACTE.last(), PE.last()]
            load_gb(gb[:, 0:D], gd.partition_broadcast(P), free)
            tg = load_gb(gb[:, D:2 * D], bd.partition_broadcast(P), ())
            for t in range(T):
                for q in range(2):
                    ts = v(lambda e, t=t, q=q: e.bn_stats(stats[:, t, q, :], h[:, t, q * 512:(q + 1) * 512]), [ht[t]])
                ts = v(lambda e, t=t: e.bn_aggr(mv[:, t, :], stats[:, t, :, :].rearrange("p a b -> p (a b)")), [ts])
            rs = small[:, 144:148]
            tr_ = rsqrt(rs, mv[:, :, 1], T, 1.0, 1e-5, [ts])
            toks = []
            for t in range(T):
                t1 = v(lambda e, t=t: e.scalar_tensor_tensor(h[:, t, :], h[:, t, :], mv[:, t, 0:1], gb[:, 0:D],
                                                            ALU.subtract, ALU.mult), [tg, tr_])
                toks.append(v(lambda e, t=t: e.scalar_tensor_tensor(h[:, t, :], h[:, t, :], rs[:, t:t + 1],
                                                                   gb[:, D:2 * D], ALU.mult, ALU.add), [t1]))
            return toks

        def residual_out(hi_ready, ht):
            toks = [None] * T
            for c in range(2):
                def evac(t, ps, tok, c=c):
                    hv = h[:, t, c * 512:(c + 1) * 512]
                    toks[t] = v(lambda e: e.scalar_tensor_tensor(hv, hv, ALPHA, ps, ALU.mult, ALU.add),
                                [tok, ht[t]])
                    return toks[t]
                gemm_tok(512, xh, xl, hi_ready, evac)
            return toks

        u_free = [None, None]

        def down(n, nf, u_ready, evac):
            bsel = n % 2
            for c in range(2):
                H, L, rw, s, nk, ncol = next_chunk()
                assert nk == nf
                for t in range(T):
                    b = take()
                    for f in range(nf):
                        X = uh[:, bsel, f, t * P:(t + 1) * P]
                        Y = ul[:, bsel, f, t * P:(t + 1) * P]
                        mm(bank[b][:, :], X, H[:, f, :], f == 0, False, [rw, u_ready, bfree[b]] if f == 0 else ())
                        mm(bank[b][:, :], X, L[:, f, :], False, False)
                        tok = mm(bank[b][:, :], Y, H[:, f, :], False, f == nf - 1, mark=(f == nf - 1))
                    bfree[b] = evac(n, t, c, bank[b][:, :], tok)
                hl_free[s] = PE.last()
            u_free[bsel] = PE.last()

        def mlp(x_ready, ht):
            toks = [None] * T
            urdy = {}
            rb = A[:, 0:2048].rearrange("p (n s) -> p n s", n=4)
            prev = [None] * 4

            def evac_down(n, t, c, ps, tok):
                hv = h[:, t, c * 512:(c + 1) * 512]
                if n == 0:
                    toks[t] = v(lambda e: e.scalar_tensor_tensor(hv, hv, ALPHA, ps, ALU.mult, ALU.add), [tok, ht[t]])
                else:
                    toks[t] = v(lambda e: e.tensor_tensor(hv, hv, ps, ALU.add), [tok, toks[t]])
                return toks[t]

            for n in range(9):
                if n < 8:
                    for q in range(2):
                        def evac(j, ps, tok, q=q, n=n):
                            i = 2 * q + j
                            r = rb[:, i, :]
                            t1 = a(lambda e: e.activation(r, ps, ACT.Relu), [tok, prev[i]])
                            t2 = v(lambda e: e.tensor_tensor(r, r, r, ALU.mult), [t1])
                            prev[i] = urdy[n] = split(r, uh[:, n % 2, i, :], ul[:, n % 2, i, :], [t2, u_free[n % 2]])
                            return t1
                        gemm_T(xh, xl, x_ready, evac)
                if n > 0:
                    down(n - 1, 4, urdy[n - 1], evac_down)
            return toks

        pf = small[:, 148:152]
        ang = small[:, 152:184]
        nn = small[:, 184:216]
        rot = sb("rot", [P, 2, T, 16])
        cosd, sind = rot[:, 0, :, :], rot[:, 1, :, :]
        t0 = v(lambda e: e.tensor_copy(pf, posi[:, :]), [S0])
        a3 = ang.rearrange("p (t k) -> p t k", t=T)
        n3 = nn.rearrange("p (t k) -> p t k", t=T)
        t0 = v(lambda e: e.tensor_tensor(a3, pf.unsqueeze(2).broadcast_to([P, T, 8]),
                                         C[:, C_INV:C_INV + 8].unsqueeze(1).broadcast_to([P, T, 8]), ALU.mult), [t0])
        MAGIC = 12582912.0
        t0 = v(lambda e: e.tensor_scalar(nn, ang, float(np.float32(1 / (2 * np.pi))), MAGIC, ALU.mult, ALU.add), [t0])
        t0 = v(lambda e: e.tensor_scalar(nn, nn, MAGIC, None, ALU.subtract), [t0])
        c1 = 6.28125
        c2 = float(np.float32(np.round((2 * np.pi - c1) * 2 ** 21) / 2 ** 21))
        c3 = float(np.float32(2 * np.pi - c1 - c2))
        for cc in (c1, c2, c3):
            t0 = v(lambda e, cc=cc: e.scalar_tensor_tensor(ang, nn, -cc, ang, ALU.mult, ALU.add), [t0])
        t0 = v(lambda e: e.tensor_scalar(ang, ang, 3.1415925, -3.1415925, ALU.min, ALU.max), [t0])
        t1 = a(lambda e: e.activation(sind[:, :, 8:16], a3, ACT.Sin), [t0])
        t2 = a(lambda e: e.activation(n3, a3, ACT.Sin, scale=0.5), [t0, t1])
        t3 = v(lambda e: e.tensor_tensor(nn, nn, nn, ALU.mult), [t2])
        t3 = v(lambda e: e.tensor_scalar(cosd[:, :, 0:8], n3, -2.0, 1.0, ALU.mult, ALU.add), [t3])
        t3 = v(lambda e: e.tensor_scalar(cosd[:, :, 8:16], n3, -2.0, 1.0, ALU.mult, ALU.add), [t3])
        rot_ready = v(lambda e: e.tensor_scalar(sind[:, :, 0:8], sind[:, :, 8:16], -1.0, None, ALU.mult), [t1])

        def rotary(view, nh, after):
            ta = gb[:, 0:nh * 16 * T].rearrange("p (t g k) -> p t g k", t=T, k=16)
            tb = gb[:, 512:512 + nh * 16 * T].rearrange("p (t g k) -> p t g k", t=T, k=16)
            cv = cosd.unsqueeze(2).broadcast_to([P, T, nh, 16])
            sv = sind.unsqueeze(2).broadcast_to([P, T, nh, 16])
            x1 = v(lambda e: e.tensor_tensor(ta, view[:, :, :, 0:16], cv, ALU.mult), after)
            x2 = v(lambda e: e.tensor_tensor(tb[:, :, :, 0:8], view[:, :, :, 8:16], sv[:, :, :, 0:8], ALU.mult), after)
            x3 = v(lambda e: e.tensor_tensor(tb[:, :, :, 8:16], view[:, :, :, 0:8], sv[:, :, :, 8:16], ALU.mult), after)
            return v(lambda e: e.tensor_tensor(view[:, :, :, 0:16], ta, tb, ALU.add), [x1, x2, x3])

        def turn(view, nt, dst, after, scale=None):
            last = []
            for j in range(nt):
                b = take()
                for t in range(T):
                    tok = tr(bank[b][:, t * P:(t + 1) * P], view[:, t, j * P:(j + 1) * P], ident,
                             [bfree[b]] + list(after), mark=(t == T - 1))
                d = dst[:, j, :]
                bfree[b] = a(lambda e, b=b, d=d: e.activation(d, bank[b][:, :], ACT.Copy), [tok])
                last.append(bfree[b])
            return last[-1]

        xr = to_T(h, [S0] * T)

        qT = A[:, 0:4096].rearrange("p (j s) -> p j s", j=8)
        iqT = A[:, 0:2048].rearrange("p (j s) -> p j s", j=4)
        ikT = A[:, 2048:2560].rearrange("p (j s) -> p j s", j=1)
        kT = A[:, 4096:6144].rearrange("p (j s) -> p j s", j=4)
        vt = A[:, 6144:7168].rearrange("p (t n) -> p t n", t=T)
        bias = A[:, 7168:9216].rearrange("p (t n) -> p t n", t=T)
        tmp = A[:, 9216:11264].rearrange("p (t n) -> p t n", t=T)
        kd = A[:, 11264:13312].rearrange("p (t n) -> p t n", t=T)
        iw = sb("iw", [P, T, 8])

        ev = []

        def ev_tmp(t, ps, tok):
            k = a(lambda e: e.activation(tmp[:, t, :], ps, ACT.Copy), [tok])
            ev.append(k)
            return k

        gemm_tok(512, xh, xl, xr, ev_tmp)
        rt = rotary(tmp.rearrange("p t (g k) -> p t g k", k=64), 8, [rot_ready, ev[-1]])
        iq_ready = turn(tmp, 4, iqT, [rt])

        kd1 = kd[:, :, 0:128]
        ev = []

        def ev_ik(t, ps, tok):
            for q in range(2):
                a(lambda e, q=q: e.activation(kd1[:, t, q * 64:(q + 1) * 64], ps[:, 0:64], ACT.Copy), [tok])
            k = a(lambda e: e.activation(iw[:, t, :], ps[:, 64:72], ACT.Copy, scale=8.0 ** -0.5))
            ev.append(k)
            return k

        gemm_tok(72, xh, xl, xr, ev_ik)
        iw_ready = ev[-1]
        rt = rotary(kd1.rearrange("p t (g k) -> p t g k", k=64), 2, [ev[-1]])
        ik_ready = turn(kd1, 1, ikT, [rt])

        cur = gb[:, 1024:1536]
        rel = [gb[:, 1536:2048], gb[:, 512:1024]]
        rel_free = [None, None]
        n_rel = 0
        sc_done = {}
        for t in range(1, T):
            n = P * (t + 1)
            prev_t = None
            for hh in range(8):
                b = take()
                half = slice(64 * (hh % 2), 64 * (hh % 2) + 64)
                tok = mm(bank[b][:, 0:n], iqT[half, hh // 2, t * P:(t + 1) * P], ikT[half, 0, 0:n], True, True,
                         [bfree[b], iq_ready, ik_ready], True)
                r = rel[n_rel % 2]
                t1 = a(lambda e, b=b, n=n, r=r: e.activation(r[:, 0:n], bank[b][:, 0:n], ACT.Relu, scale=0.125),
                       [tok, rel_free[n_rel % 2], rt])
                bfree[b] = t1
                s_ = bias[:, t, 0:n]
                w_ = iw[:, t, hh:hh + 1]
                if hh == 0:
                    prev_t = v(lambda e, s_=s_, r=r, n=n, w_=w_: e.tensor_scalar(s_, r[:, 0:n], w_, None, ALU.mult),
                               [t1, iw_ready])
                else:
                    prev_t = v(lambda e, s_=s_, r=r, n=n, w_=w_: e.scalar_tensor_tensor(
                        s_, r[:, 0:n], w_, s_, ALU.mult, ALU.add), [t1, prev_t])
                rel_free[n_rel % 2] = prev_t
                n_rel += 1
            sd = bias[:, t, t * P:(t + 1) * P]
            sc_done[t] = v(lambda e, sd=sd: e.tensor_tensor(sd, sd, CB, ALU.add), [prev_t])
        dump("iqT", iqT, [iq_ready])
        dump("ikT", ikT, [ik_ready])
        dump("score", bias[:, 3, :], [sc_done[3]])
        m8 = sb("m8", [P, 8])
        bias_ready = [None] * T
        tk = None

        def top_k(t):
            n = P * (t + 1)
            s_ = bias[:, t, 0:n]
            w_ = cur[:, 0:n]
            k = sc_done[t]
            src = s_
            for r in range(16):
                k = v(lambda e, src=src: e.max(m8[:, :], src), [k])
                k = v(lambda e, src=src, w_=w_: e.match_replace(w_, m8[:, :], src, -3e38), [k])
                src = w_
            k = v(lambda e: e.tensor_tensor(s_, w_, s_, ALU.is_equal), [k])
            return v(lambda e: e.tensor_scalar(s_, s_, -BIG, None, ALU.mult), [k])

        ev = []

        def ev_kv(t, ps, tok):
            kv_ = kd[:, t, :].rearrange("p (g q k) -> p g q k", g=4, q=2)
            pk = ps[:, 0:256].rearrange("p (g k) -> p g k", g=4)
            for q in range(2):
                a(lambda e, q=q: e.activation(kv_[:, :, q, :], pk, ACT.Copy), [tok, ik_ready])
            k = a(lambda e: e.activation(vt[:, t, :], ps[:, 256:512], ACT.Copy))
            ev.append(k)
            return k

        gemm_tok(512, xh, xl, xr, ev_kv)
        v_ready = ev[-1]
        rt = rotary(kd.rearrange("p t (g k) -> p t g k", k=64), 8, [ev[-1], DVE.last()])
        k_ready = turn(kd, 4, kT, [rt])
        for c in range(2):
            ev = []

            def ev_q(t, ps, tok):
                k = a(lambda e: e.activation(tmp[:, t, :], ps, ACT.Copy), [tok, PE.last() if t < 0 else None])
                ev.append(k)
                return k

            gemm_tok(512, xh, xl, xr, ev_q)
            rt = rotary(tmp.rearrange("p t (g k) -> p t g k", k=64), 8, [ev[-1]])
            q_ready = turn(tmp, 4, qT[:, 4 * c:4 * c + 4, :], [rt])
        tb0 = v(lambda e: e.tensor_copy(bias[:, 0, 0:P], CB))
        bias_ready[0] = tb0
        for t in range(1, T):
            bias_ready[t] = top_k(t)
        dump("bias", bias[:, 3, :], [bias_ready[3]])

        dump("qT", qT, [q_ready])
        dump("kT", kT, [k_ready])
        NPB = 3
        att = sb("att", [P, 4, 16, T])
        soft_n = [0]

        def attend(name, PB_, PTs, qv, kv_, vv_, nheads, grp, causal, ready_, emit_o):
            mx, nmx, sm, rc = (att[:, q, 0:nheads, :] for q in range(4))
            pfree = [None] * NPB
            ptfree = None
            ob = None
            for hd in range(nheads):
                half = slice(64 * (hd % 2), 64 * (hd % 2) + 64)
                gk = hd // grp
                pt_banks = {}
                pt_tok = {}
                bt = [take(True) for _ in range(T)]
                order = list(range(T))
                for t in order:
                    n = P * (t + 1) if causal else SEQ
                    i = soft_n[0] % NPB
                    soft_n[0] += 1
                    pb = PB_[i]
                    b = take()
                    tok = mm(bank[b][:, 0:n], qv[half, hd // 2, t * P:(t + 1) * P], kv_[half, gk, 0:n], True, True,
                             [bfree[b]] + ready_, True)
                    mxc, nmc = mx[:, hd, t:t + 1], nmx[:, hd, t:t + 1]
                    if causal:
                        t1 = v(lambda e, b=b, n=n, t=t, pb=pb, mxc=mxc: e.tensor_tensor_reduce(
                            pb[:, 0:n], bank[b][:, 0:n], bias[:, t, 0:n], 0.125, -3e38, ALU.add, ALU.max, mxc),
                            [tok, pfree[i], bias_ready[t]])
                        bfree[b] = t1
                        t2 = v(lambda e, mxc=mxc, nmc=nmc: e.tensor_scalar(nmc, mxc, -1.0, None, ALU.mult), [t1])
                        t3 = a(lambda e, pb=pb, n=n, nmc=nmc, hd=hd, t=t: e.activation(
                            pb[:, 0:n], pb[:, 0:n], ACT.Exp, bias=nmc, accum_out=sm[:, hd, t:t + 1]), [t2])
                    else:
                        t1 = v(lambda e, b=b, mxc=mxc: e.reduce_max(mxc, bank[b][:, :], AX), [tok])
                        t2 = v(lambda e, mxc=mxc, nmc=nmc: e.tensor_scalar(nmc, mxc, -0.125, None, ALU.mult), [t1])
                        t3 = a(lambda e, b=b, pb=pb, nmc=nmc, hd=hd, t=t: e.activation(
                            pb[:, :], bank[b][:, :], ACT.Exp, bias=nmc, scale=0.125, accum_out=sm[:, hd, t:t + 1]),
                            [t2, pfree[i]])
                        bfree[b] = t3
                    t4 = v(lambda e, hd=hd, t=t: e.reciprocal(rc[:, hd, t:t + 1], sm[:, hd, t:t + 1]), [t3])
                    t5 = g(lambda e, pb=pb, n=n, hd=hd, t=t: e.tensor_scalar(
                        pb[:, 0:n], pb[:, 0:n], rc[:, hd, t:t + 1], None, ALU.mult), [t4, t3])
                    for kb in range(n // P):
                        o = bank[bt[kb]][:, t * P:(t + 1) * P]
                        pt_tok[kb] = tr(o, pb[:, kb * P:(kb + 1) * P], ident, [bfree[bt[kb]], t5], mark=True)
                    pfree[i] = PE.last()
                pt_r = []
                for kb in range(T):
                    c0 = kb * P if causal else 0
                    d, s_ = PTs[:, kb, c0:SEQ], bank[bt[kb]][:, c0:SEQ]
                    if kb % 2:
                        k = v(lambda e, d=d, s_=s_: e.tensor_copy(d, s_), [pt_tok[kb], ptfree])
                    else:
                        k = a(lambda e, d=d, s_=s_: e.activation(d, s_, ACT.Copy), [pt_tok[kb], ptfree])
                    bfree[bt[kb]] = k
                    held.discard(bt[kb])
                    pt_r.append(k)
                if hd % 2 == 0:
                    ob = take(True)
                for kb in range(T):
                    c0 = kb * P if causal else 0
                    tok = mm(bank[ob][half, c0:SEQ], vv_(kb, gk), PTs[:, kb, c0:SEQ], kb == 0, kb == T - 1,
                             [pt_r[kb], bfree[ob] if hd % 2 == 0 else None], mark=(kb == T - 1))
                ptfree = tok
                if hd % 2:
                    held.discard(ob)
                    bfree[ob] = emit_o(hd // 2, bank[ob][:, :], tok)

        oo = []

        def emit_a(j, ps, tok):
            k = split(ps, xh[:, j, :], xl[:, j, :], [tok])
            oo.append(k)
            return k

        PBa = [A[:, 11264 + 512 * i:11776 + 512 * i] for i in range(NPB)]
        attend("a", PBa, tmp, qT, kT, lambda kb, gk: vt[:, kb, gk * 64:gk * 64 + 64], 16, 4, True,
               [q_ready, k_ready, v_ready], emit_a)
        ht = residual_out(oo[-1], [S0] * T)
        ht = layer_norm(ln_mix_g[0], ln_mix_b[0], ht)
        dump("h1", h[:, :, :], [ht[-1]])
        xr = to_T(h, ht)
        ht = mlp(xr, ht)
        ht = layer_norm(ln_mlp_g[0], ln_mlp_b[0], ht)
        dump("h2", h[:, :, :], [ht[-1]])

        xr = to_T(h, ht)
        gq = A[:, 0:2048].rearrange("p (h s) -> p h s", h=4)
        gk_ = A[:, 2048:4096].rearrange("p (h s) -> p h s", h=4)
        gv = A[:, 4096:8192].rearrange("p (t n) -> p t n", t=T)
        bb = A[:, 8192:10240].rearrange("p (h s) -> p h s", h=4)
        EE = A[:, 10240:10752].rearrange("p (h s) -> p h s", h=4)
        QS = A[:, 10752:11264].rearrange("p (h s) -> p h s", h=4)
        KS = A[:, 11264:11776].rearrange("p (h s) -> p h s", h=4)
        AT = A[:, 11776:12288].rearrange("p (h s) -> p h s", h=4)
        KD = A[:, 12288:12800].rearrange("p (h s) -> p h s", h=4)
        QE = gb[:, 0:512].rearrange("p (h s) -> p h s", h=4)
        KDT = gb[:, 512:1024].rearrange("p (h s) -> p h s", h=4)
        ST = gb[:, 1024:2048].rearrange("p (h n) -> p h n", h=4)
        zz = A[:, 4096:6144].rearrange("p (h s) -> p h s", h=4)
        z2 = A[:, 6144:8192].rearrange("p (h s) -> p h s", h=4)
        alow = A[0:16, 12288:12800]
        wa2 = A[0:16, 12800:13312]
        ta2 = load_gb(wa2, b_w_a2[0], [PE.last(), DVE.last(), ACTE.last()])
        al = []

        def ev_al(j, ps, tok):
            al.append(a(lambda e: e.activation(alow, ps, ACT.Copy), [tok]))
            return al[-1]

        gemm_T(xh, xl, xr, ev_al)
        zt = None
        for q in range(4):
            b = take()
            tok = mm(bank[b][:, :], wa2[:, q * P:(q + 1) * P], alow, True, True, [al[0], ta2, bfree[b]], True)
            bfree[b] = v(lambda e, b=b, q=q: e.tensor_scalar(zz[:, q, :], bank[b][:, :], BA[:, q:q + 1], None, ALU.add),
                         [tok, S0])
        zt = DVE.last()
        t1 = a(lambda e: e.activation(z2, zz, ACT.Abs), [zt])
        t1 = a(lambda e: e.activation(z2, z2, ACT.Exp, scale=-1.0), [t1])
        t1 = v(lambda e: e.tensor_scalar(z2, z2, 1.0, None, ALU.add), [t1])
        t1 = a(lambda e: e.activation(z2, z2, ACT.Ln), [t1])
        t1 = v(lambda e: e.scalar_tensor_tensor(zz, zz, 0.0, z2, ALU.min, ALU.subtract), [t1])
        for q in range(4):
            for c in range(4):
                b_ready = v(lambda e, q=q, c=c: e.tensor_tensor_scan(
                    bb[:, q, c * P:(c + 1) * P], ones, zz[:, q, c * P:(c + 1) * P], 0.0, ALU.mult, ALU.add), [t1])
        dump("bb", bb, [b_ready])
        qk_r = []
        for n in range(4):
            def ev_qk(j, ps, tok, n=n):
                i = 2 * n + j
                dst = gq[:, i, :] if i < 4 else gk_[:, i - 4, :]
                sc = 128.0 ** -0.5 if i < 4 else 1.0
                qk_r.append(a(lambda e: e.activation(dst, ps, ACT.Copy, scale=sc), [tok]))
                return qk_r[-1]
            gemm_T(xh, xl, xr, ev_qk)
        for n in range(2):
            def ev_v(t, ps, tok, n=n):
                vr = a(lambda e: e.activation(gv[:, t, n * 512:(n + 1) * 512], ps, ACT.Copy), [tok, b_ready])
                qk_r.append(vr)
                return vr
            gemm_tok(512, xh, xl, xr, ev_v)
        qkv = qk_r[-1]
        ssq = sb("ssq", [P, T, 4])
        ebl = sb("ebl", [P, 4])
        st_ready = None
        o_done = []
        for c in range(4):
            cs = slice(c * P, (c + 1) * P)
            at = None
            for n, s in list(enumerate(LEVELS)) + [(7, 0)]:
                b = take()
                if s:
                    nb = 64 // s

                    def blk(x4):
                        return x4.rearrange("p h (n two s) -> p h n two s", two=2, s=s)

                    bv = blk(bb[:, :, cs])
                    ref = bv[:, :, :, 0, s - 1:s].broadcast_to([P, 4, nb, s])
                    ev4, qs4, ks4 = blk(EE), blk(QS), blk(KS)
                    qv4, kv4 = blk(gq[:, :, cs]), blk(gk_[:, :, cs])
                    for hh in range(1):
                        t1 = v(lambda e, ev4=ev4, bv=bv, ref=ref: e.tensor_tensor(
                            ev4[:, :, :, 1, :], bv[:, :, :, 1, :], ref, ALU.subtract), [b_ready, DVE.last(), ACTE.last()])
                        t2 = v(lambda e, ev4=ev4, bv=bv, ref=ref: e.tensor_tensor(
                            ev4[:, :, :, 0, :], ref, bv[:, :, :, 0, :], ALU.subtract), [b_ready])
                    t3 = a(lambda e: e.activation(EE, EE, ACT.Exp, scale=0.0625), [t2])
                    if n == 0:
                        for X in (QS, KS):
                            src = gq if X is QS else gk_
                            t4 = v(lambda e, X=X, src=src, cs=cs: e.tensor_copy(X, src[:, :, cs]), [qkv, PE.last()])
                    t5 = v(lambda e, qs4=qs4, qv4=qv4, ev4=ev4: e.tensor_tensor(
                        qs4[:, :, :, 1, :], qv4[:, :, :, 1, :], ev4[:, :, :, 1, :], ALU.mult), [t3, DVE.last(), PE.last()])
                    t6 = v(lambda e, ks4=ks4, kv4=kv4, ev4=ev4: e.tensor_tensor(
                        ks4[:, :, :, 0, :], kv4[:, :, :, 0, :], ev4[:, :, :, 0, :], ALU.mult), [t3])
                    for q in range(4):
                        tok = mm(bank[b][:, q * P:(q + 1) * P], KS[:, q, :], QS[:, q, :], True, True,
                                 [bfree[b], t6], q == 3)
                else:
                    for q in range(4):
                        tok = mm(bank[b][:, q * P:(q + 1) * P], gk_[:, q, cs], gq[:, q, cs], True, True,
                                 [bfree[b], qkv], q == 3)
                if n == 0:
                    at = v(lambda e: e.memset(AT, 0.0), [PE.last()])
                mk = LM[:, n * P:(n + 1) * P].unsqueeze(1).broadcast_to([P, 4, P])
                pv = bank[b][:, :].rearrange("p (h s) -> p h s", h=4)
                at = v(lambda e, mk=mk, pv=pv: e.copy_predicated(AT, mk, pv), [tok, at])
                bfree[b] = at
            if c == 0:
                dump("AT", AT, [at])
            t1 = a(lambda e, cs=cs: e.activation(QE, bb[:, :, cs], ACT.Exp, scale=0.0625), [at, PE.last()])
            qe = v(lambda e, cs=cs: e.tensor_tensor(QE, QE, gq[:, :, cs], ALU.mult), [t1])
            bl = bb[:, :, c * P + 127:c * P + 128]
            t1 = v(lambda e, cs=cs, bl=bl: e.tensor_tensor(KDT, bl.broadcast_to([P, 4, P]), bb[:, :, cs], ALU.subtract),
                   [qe])
            t1 = a(lambda e: e.activation(KDT, KDT, ACT.Exp, scale=0.0625), [t1])
            te = a(lambda e, bl=bl: e.activation(ebl[:, :].unsqueeze(2), bl, ACT.Exp, scale=0.0625), [st_ready])
            kdt = v(lambda e, cs=cs: e.tensor_tensor(KDT, KDT, gk_[:, :, cs], ALU.mult), [t1])
            b = take()
            for q in range(4):
                tok = tr(bank[b][:, q * P:(q + 1) * P], KDT[:, q, :], ident, [bfree[b], kdt], q == 3)
            bfree[b] = kdr = a(lambda e, b=b: e.activation(
                KD, bank[b][:, :].rearrange("p (h s) -> p h s", h=4), ACT.Copy), [tok])
            ob = [take(), take()]
            for q in range(4):
                o = bank[ob[q // 2]][:, (q % 2) * 256:(q % 2) * 256 + 256]
                prs = [(AT[:, q, :], gv[:, c, q * 256:(q + 1) * 256])]
                if c:
                    prs.append((QE[:, q, :], ST[:, q, :]))
                otok = mm_group(o, prs, [bfree[ob[q // 2]], at, qe, st_ready])
            sbk = [take(), take()]
            if c < 3:
                for q in range(4):
                    o = bank[sbk[q // 2]][:, (q % 2) * 256:(q % 2) * 256 + 256]
                    stok = mm_group(o, [(KD[:, q, :], gv[:, c, q * 256:(q + 1) * 256])], [bfree[sbk[q // 2]], kdr])
                for q in range(4):
                    o = bank[sbk[q // 2]][:, (q % 2) * 256:(q % 2) * 256 + 256]
                    if c == 0:
                        st_ready = v(lambda e, q=q, o=o: e.tensor_copy(ST[:, q, :], o), [stok])
                    else:
                        st_ready = v(lambda e, q=q, o=o: e.scalar_tensor_tensor(
                            ST[:, q, :], ST[:, q, :], ebl[:, q:q + 1], o, ALU.mult, ALU.add), [stok, te])
                    bfree[sbk[q // 2]] = st_ready
            last_pe = PE.last()
            for q in range(4):
                o = bank[ob[q // 2]][:, (q % 2) * 256:(q % 2) * 256 + 256]
                dst = gv[:, c, q * 256:(q + 1) * 256]
                k1 = a(lambda e, dst=dst, o=o: e.activation(dst, o, ACT.Copy), [otok, last_pe])
                k2 = a(lambda e, dst=dst, q=q, c=c: e.activation(
                    EE.rearrange("p h s -> p (h s)")[:, 0:256], dst, ACT.Square, accum_out=ssq[:, c, q:q + 1]), [k1, at])
                bfree[ob[q // 2]] = k1
            o_done.append(k2)
        dump("go", gv, [o_done[-1]])
        rs = small[:, 216:232]
        rr = rsqrt(rs, ssq[:, :, :].rearrange("p t h -> p (t h)"), 16, 1.0 / 256, 1e-6, [o_done[-1]])
        gnb = gb[:, 0:256]
        tg = load_gb(gnb, b_g_norm[0].partition_broadcast(P), [PE.last(), DVE.last(), ACTE.last()])
        yt = [None] * T
        for t in range(T):
            for q in range(4):
                o = gv[:, t, q * 256:(q + 1) * 256]
                yt[t] = v(lambda e, o=o, t=t, q=q: e.scalar_tensor_tensor(
                    o, o, rs[:, t * 4 + q:t * 4 + q + 1], gnb, ALU.mult, ALU.mult), [tg, rr])
        sg = [gb[:, 512:1024], gb[:, 1024:1536]]
        sgf = [None, None]
        ns = [0]

        def gate_with(dst, ps, tok, after, silu):
            i = ns[0] % 2
            ns[0] += 1
            e_ = sg[i]
            k1 = a(lambda e: e.activation(e_, ps, ACT.Exp, scale=-1.0), [tok, sgf[i]])
            k2 = v(lambda e: e.tensor_scalar(e_, e_, 1.0, None, ALU.add), [k1])
            k3 = v(lambda e: e.reciprocal(e_, e_), [k2])
            if silu:
                k4 = v(lambda e: e.tensor_tensor(dst, dst, ps, ALU.mult), [after, k1])
            else:
                k4 = after
            k5 = v(lambda e: e.tensor_tensor(dst, dst, e_, ALU.mult), [k3, k4])
            sgf[i] = k5
            return k5

        for n in range(2):
            def ev_r(t, ps, tok, n=n):
                yt[t] = gate_with(gv[:, t, n * 512:(n + 1) * 512], ps, tok, yt[t], True)
                return yt[t]
            gemm_tok(512, xh, xl, xr, ev_r)
        dump("gy", gv, [yt[-1]])
        xr = to_T(gv, yt)
        ht = residual_out(xr, ht)
        ht = layer_norm(ln_mix_g[1], ln_mix_b[1], ht)
        dump("h3", h[:, :, :], [ht[-1]])
        xr = to_T(h, ht)
        ht = mlp(xr, ht)
        ht = layer_norm(ln_mlp_g[1], ln_mlp_b[1], ht)
        dump("h4", h[:, :, :], [ht[-1]])

        cond = small[:, 232:240]
        t1 = a(lambda e: e.activation(cond, CC, ACT.Exp, scale=-1.0), [S0])
        t1 = v(lambda e: e.tensor_scalar(cond, cond, 1.0, None, ALU.add), [t1])
        t1 = v(lambda e: e.reciprocal(cond, cond), [t1])
        cond_ready = v(lambda e: e.tensor_tensor(cond, cond, CC, ALU.mult), [t1])
        acc = A[:, 4096:6144]
        G1, G2 = A[:, 6144:7168], A[:, 7168:8192]
        nacc = [0]

        def ada(r, cols, rows):
            free = [PE.last(), DVE.last(), ACTE.last()]
            k = v(lambda e: e.memset(acc, 0.0), free)
            nacc[0] += 1
            POOL.put([k], lambda e: e.dma_start(acc[0:1, :], b_ada_2[0:1, r * 2048:(r + 1) * 2048]).then_inc(s_acc, 16),
                     mark=False)
            k = (s_acc, 16 * nacc[0])
            for kt in range(8):
                i = next_ada()
                rw = raw[:, i % NRAW, :]
                k = v(lambda e, rw=rw, kt=kt: e.scalar_tensor_tensor(acc, rw, cond[:, kt:kt + 1], acc, ALU.mult, ALU.add),
                      [landed(i), k, cond_ready])
                raw_free[i % NRAW] = k
                fetch(i + NRAW)
            last = None
            for c0, dst in cols:
                b = take()
                for j in range(8):
                    tok = mm(bank[b][:, j:j + 1], acc[:, c0 + j * P:c0 + (j + 1) * P], ones[:, 0:1], True, True,
                             [bfree[b], k], j == 7)
                last = bfree[b] = v(lambda e, b=b, dst=dst: e.tensor_copy(dst, bank[b][:, 0:8]), [tok])
            for c0, dst in rows:
                for j in range(2):
                    b = take()
                    tok = mm(bank[b][:, :], ones, acc[:, c0 + j * 512:c0 + (j + 1) * 512], True, True, [bfree[b], k], True)
                    last = bfree[b] = v(lambda e, b=b, dst=dst, j=j: e.tensor_copy(dst[:, j * 512:(j + 1) * 512],
                                                                                   bank[b][:, :]), [tok])
            return last

        md = ada(0, [(0, SH1), (1024, SC1)], [])
        t1 = v(lambda e: e.tensor_scalar(CS1, SC1, 1.0, None, ALU.add), [md])
        cs1 = v(lambda e: e.tensor_tensor(CS1, CS1, GM, ALU.mult), [t1])

        def rms_rows(dst, ht):
            sq = gb[:, 0:1024]
            k = DVE.last()
            for t in range(T):
                k = a(lambda e, t=t: e.activation(sq, h[:, t, :], ACT.Square, accum_out=ssq[:, t, 0:1]), [ht[t], k])
            rs_ = small[:, 144:148]
            k = rsqrt(rs_, ssq[:, :, 0], T, 1.0 / D, 1e-6, [k])
            return [v(lambda e, t=t: e.tensor_scalar(dst[:, t, :], h[:, t, :], rs_[:, t:t + 1], None, ALU.mult), [k])
                    for t in range(T)]

        xn = A[:, 0:4096].rearrange("p (t n) -> p t n", t=T)
        nt = rms_rows(xn, ht)
        xr = to_T(xn, nt, CS1, SH1, [gb[:, 1024:1536], gb[:, 1536:2048]])

        y = A[:, 0:4096].rearrange("p (t n) -> p t n", t=T)
        qT2 = A[:, 4096:6144].rearrange("p (j s) -> p j s", j=4)
        kT2 = A[:, 6144:7168].rearrange("p (j s) -> p j s", j=2)
        v2 = A[:, 7168:7680].rearrange("p (t n) -> p t n", t=T)
        tm = A[:, 7680:9728].rearrange("p (t n) -> p t n", t=T)
        tm2 = A[:, 9728:11776].rearrange("p (t n) -> p t n", t=T)
        kd2 = A[:, 11776:12800].rearrange("p (t n) -> p t n", t=T)
        gqn, gkn = gb[:, 0:64], gb[:, 64:128]
        load_gb(gqn, q_norm_g_2[0].partition_broadcast(P), [DVE.last(), ACTE.last(), PE.last()])
        tgq = load_gb(gkn, k_norm_g_2[0].partition_broadcast(P), ())
        s32 = sb("s32", [P, 32])

        def norm_rope(x4, w4, nh, gain, after):
            k = v(lambda e: e.tensor_tensor(w4.rearrange("p t g k -> p (t g k)"), x4.rearrange("p t g k -> p (t g k)"),
                                            x4.rearrange("p t g k -> p (t g k)"), ALU.mult), after)
            k = v(lambda e: e.tensor_reduce(s32[:, 0:T * nh].rearrange("p (t g) -> p t g", t=T), w4, AX, ALU.add), [k])
            k = rsqrt(s32[:, 0:T * nh], s32[:, 0:T * nh], T * nh, 1.0 / 64, 1e-6, [k])
            rsb = s32[:, 0:T * nh].rearrange("p (t g) -> p t g", t=T).unsqueeze(3).broadcast_to([P, T, nh, 64])
            k = v(lambda e: e.tensor_tensor(x4, x4, rsb, ALU.mult), [k])
            gn = gain.unsqueeze(1).broadcast_to([P, T * nh, 64])
            x3 = x4.rearrange("p t g k -> p (t g) k")
            k = v(lambda e: e.tensor_tensor(x3, x3, gn, ALU.mult), [k, tgq])
            for t in range(T):
                rcv = C[:, C_RC + t * 64:C_RC + t * 64 + 64].unsqueeze(1).broadcast_to([P, nh, 64])
                rsv_ = C[:, C_RS + t * 64:C_RS + t * 64 + 64].rearrange("p (r a k) -> p r a k", r=2, a=2)
                xv = x4[:, t].rearrange("p g (r a k) -> p g r a k", r=2, a=2)
                wv = w4[:, t].rearrange("p g (r a k) -> p g r a k", r=2, a=2)
                k1 = k
                for q in range(2):
                    sv = rsv_[:, :, q, :].unsqueeze(1).broadcast_to([P, nh, 2, 16])
                    k1 = v(lambda e, wv=wv, xv=xv, sv=sv, q=q: e.tensor_tensor(wv[:, :, :, q, :], xv[:, :, :, 1 - q, :], sv,
                                                                             ALU.mult), [k])
                k2 = v(lambda e, t=t, rcv=rcv: e.tensor_tensor(x4[:, t], x4[:, t], rcv, ALU.mult), [k1])
                k3 = v(lambda e, t=t: e.tensor_tensor(x4[:, t], x4[:, t], w4[:, t], ALU.add), [k1, k2])
            return k3

        ev = []

        def ev_q2(t, ps, tok):
            ev.append(a(lambda e: e.activation(tm[:, t, :], ps, ACT.Copy), [tok, md]))
            return ev[-1]

        gemm_tok(512, xh, xl, xr, ev_q2)
        k = norm_rope(tm.rearrange("p t (g k) -> p t g k", k=64), tm2.rearrange("p t (g k) -> p t g k", k=64), 8, gqn,
                      [ev[-1]])
        q2r = turn(tm, 4, qT2, [k])
        ev = []

        def ev_k2(t, ps, tok):
            kk = kd2[:, t, :].rearrange("p (g q k) -> p g q k", g=2, q=2)
            pk = ps[:, 0:128].rearrange("p (g k) -> p g k", g=2)
            for q in range(2):
                a(lambda e, q=q: e.activation(kk[:, :, q, :], pk, ACT.Copy), [tok])
            ev.append(a(lambda e: e.activation(v2[:, t, :], ps[:, 128:256], ACT.Copy), [tok]))
            return ev[-1]

        gemm_tok(256, xh, xl, xr, ev_k2)
        w4 = A[:, 9728:10752].rearrange("p (t g k) -> p t g k", t=T, k=64)
        k = norm_rope(kd2.rearrange("p t (g k) -> p t g k", k=64), w4, 4, gkn, [ev[-1]])
        k2r = turn(kd2, 2, kT2, [k])
        v2r = ev[-1]
        dump("qT2", qT2, [q2r])
        dump("kT2", kT2, [k2r])
        yT = [uh[:, j // 2 % 2, 0, :] for j in range(4)]
        y2 = []
        oT2 = A[:, 11776:12288]
        yparts = []

        def emit_2(j, ps, tok):
            k = a(lambda e: e.activation(oT2, ps, ACT.Copy), [tok, PE.last(), k2r])
            b = take()
            for t in range(T):
                tk2 = tr(bank[b][:, t * P:(t + 1) * P], oT2[:, t * P:(t + 1) * P], ident, [bfree[b], k], t == T - 1)
            bfree[b] = a(lambda e, b=b, j=j: e.activation(
                y[:, :, j * P:(j + 1) * P], bank[b][:, :].rearrange("p (t n) -> p t n", t=T), ACT.Copy), [tk2])
            y2.append(bfree[b])
            return k

        PB2 = [A[:, 7680 + 512 * i:8192 + 512 * i] for i in range(NPB)]
        attend("b", PB2, tm2, qT2, kT2, lambda kb, gk: v2[:, kb, gk * 64:gk * 64 + 64], 8, 4, False,
               [q2r, k2r, v2r], emit_2)
        dump("ya", y[:, :, 0:512], [y2[-1]])

        mqk = A[:, 4096:8192].rearrange("p (j s) -> p j s", j=8)
        vx = A[:, 8192:10272].rearrange("p (t h n) -> p t h n", t=T, h=4)
        STm = A[:, 10272:12320].rearrange("p (b s) -> p b s", b=T)
        Mr = [A[0:4, 12320:12832], A[0:4, 12832:13344]]
        pad = gb[:, 0:516]
        ya_ = gb[:, 516:1028]
        eb_ = gb[:, 1028:1540]
        kz = v(lambda e: e.memset(pad, 0.0), [y2[-1], tgq])
        kp = kz
        att_done = [y2[-1], PE.last(), DVE.last()]
        cvt = []
        for n in range(4):
            def ev_c(j, ps, tok, n=n):
                i = 2 * n + j
                k0 = a(lambda e: e.activation(pad[:, 2:514], ps, ACT.Copy), [tok, DVE.last()])
                k = v(lambda e: e.tensor_scalar(ya_, pad[:, 0:512], CW[:, 0, i:i + 1], CVB[:, i:i + 1], ALU.mult, ALU.add),
                      [k0, S0])
                for w in range(1, 5):
                    k = v(lambda e, w=w: e.scalar_tensor_tensor(ya_, pad[:, w:w + 512], CW[:, w, i:i + 1], ya_,
                                                               ALU.mult, ALU.add), [k])
                k1 = a(lambda e: e.activation(eb_, ya_, ACT.Exp, scale=-1.0), [k])
                k1 = v(lambda e: e.tensor_scalar(eb_, eb_, 1.0, None, ALU.add), [k1])
                k1 = v(lambda e: e.reciprocal(eb_, eb_), [k1])
                cvt.append(v(lambda e: e.tensor_tensor(mqk[:, i, :], ya_, eb_, ALU.mult), [k1] + att_done))
                return k0
            gemm_T(xh, xl, xr, ev_c)
        qk_ready = cvt[-1]
        kz = v(lambda e: e.memset(vx[:, :, :, 128:130], 1.0), att_done)
        ev = []

        def ev_v2(t, ps, tok):
            ev.append(a(lambda e: e.activation(vx[:, t, :, 0:128], ps.rearrange("p (h n) -> p h n", h=4), ACT.Copy),
                        [tok] + att_done))
            return ev[-1]

        gemm_tok(512, xh, xl, xr, ev_v2)
        vx_ready = ev[-1]
        gg = sb("gg", [P, T, 16])
        g2_ = sb("g2_", [P, T, 16])
        ev = []

        def ev_g(t, ps, tok):
            ev.append(v(lambda e: e.tensor_tensor(gg[:, t, :], ps, GB, ALU.add), [tok, S0]))
            return ev[-1]

        gemm_tok(16, xh, xl, xr, ev_g)
        gr = ev[-1]
        k = a(lambda e: e.activation(g2_[:, :, :], gg[:, :, :], ACT.Abs), [gr])
        k = a(lambda e: e.activation(g2_[:, :, :], g2_[:, :, :], ACT.Exp, scale=-1.0), [k])
        k = v(lambda e: e.tensor_scalar(g2_[:, :, :], g2_[:, :, :], 1.0, None, ALU.add), [k])
        k = a(lambda e: e.activation(g2_[:, :, :], g2_[:, :, :], ACT.Ln), [k])
        lf = v(lambda e: e.scalar_tensor_tensor(g2_[:, :, :], gg[:, :, :], 0.0, g2_[:, :, :], ALU.min, ALU.subtract), [k])
        acol = sb("acol", [P, 2, T, 4])
        ecol = sb("ecol", [P, 2, T, 4])
        ir, fr = STm[0:4, 0, :], STm[0:4, 1, :]
        onerow = STm[0:4, 2, :]
        k1r = v(lambda e: e.memset(onerow, 1.0), att_done)
        mrdy = []
        prev_k = None
        for d in range(2):
            bi, bf = take(), take()
            for t in range(T):
                tok = tr(bank[bi][0:4, t * P:(t + 1) * P], gg[:, t, 8 * d:8 * d + 4], ident, [bfree[bi], lf], t == T - 1)
            for t in range(T):
                tok2 = tr(bank[bf][0:4, t * P:(t + 1) * P], g2_[:, t, 8 * d + 4:8 * d + 8], ident, [bfree[bf], lf], t == T - 1)
            rv = (lambda ap: ap) if d == 0 else (lambda ap: ap[:, ::-1])
            ki = a(lambda e, bi=bi: e.activation(ir, bank[bi][0:4, :], ACT.Copy), [tok, prev_k] + att_done)
            kf = a(lambda e, bf=bf, d=d: e.activation(Mr[d], bank[bf][0:4, :], ACT.Copy), [tok2] + att_done)
            bfree[bi], bfree[bf] = ki, kf
            k = v(lambda e, rv=rv, d=d: e.tensor_tensor_scan(rv(fr), onerow, rv(Mr[d]), 0.0, ALU.mult, ALU.add),
                  [kf, k1r, prev_k])
            ka = v(lambda e: e.tensor_tensor(ir, ir, fr, ALU.subtract), [k, ki])
            km = v(lambda e, rv=rv, d=d: e.tensor_tensor_scan(rv(Mr[d]), rv(ir), rv(ir), 0.0, ALU.max, ALU.max), [ka])
            mrdy.append(km)
            kn = v(lambda e, d=d: e.tensor_tensor(fr, fr, Mr[d], ALU.add), [km])
            b = take()
            for t in range(T):
                tr(bank[b][:, t * 4:t * 4 + 4], ir[:, t * P:(t + 1) * P], ident[0:4, 0:4], [bfree[b], ka])
                tok = tr(bank[b][:, 16 + t * 4:20 + t * 4], fr[:, t * P:(t + 1) * P], ident[0:4, 0:4], [kn], t == T - 1)
            k1 = a(lambda e, b=b, d=d: e.activation(acol[:, d, :, :], bank[b][:, 0:16].rearrange("p (t h) -> p t h", t=T),
                                                 ACT.Copy), [tok])
            prev_k = bfree[b] = a(lambda e, b=b, d=d: e.activation(
                ecol[:, d, :, :], bank[b][:, 16:32].rearrange("p (t h) -> p t h", t=T), ACT.Exp, scale=-1.0), [tok])
        cols_ready = prev_k
        dump("acol", acol[:, :, :, :], [cols_ready])
        dump("ecol", ecol[:, :, :, :], [cols_ready])
        dump("mqk", mqk, [qk_ready])
        den = sb("den", [P, 4])
        Db = [gb[:, 512 * i:512 * (i + 1)] for i in range(4)]
        dfree = [cols_ready] * 4
        nd = [0]
        SCL = 128.0 ** -0.5
        st_free = cols_ready
        hmr = None
        for hh in range(4):
            for d in range(2):
                bM = take(True)
                mtok = mm(bank[bM][:, :], C[0:4, C_SEL + hh * P:C_SEL + (hh + 1) * P], Mr[d], True, True,
                          [bfree[bM], mrdy[d]], True)
                sr = []
                for sb_ in range(T):
                    c0, c1_ = (sb_ * P, SEQ) if d == 0 else (0, (sb_ + 1) * P)
                    n = c1_ - c0
                    i = nd[0] % 4
                    nd[0] += 1
                    dv = Db[i][:, 0:n]
                    k = v(lambda e, dv=dv, bM=bM, c0=c0, c1_=c1_, d=d, sb_=sb_, hh=hh: e.tensor_scalar(
                        dv, bank[bM][:, c0:c1_], acol[:, d, sb_, hh:hh + 1], 0.0, ALU.add, ALU.min),
                        [mtok, dfree[i], cols_ready])
                    bfree[bM] = k
                    dd = Db[i][:, 0:P] if d == 0 else Db[i][:, n - P:n]
                    mk = CBT if d == 0 else CB
                    k = v(lambda e, dd=dd, mk=mk: e.tensor_tensor(dd, dd, mk, ALU.add), [k])
                    k = a(lambda e, dv=dv: e.activation(dv, dv, ACT.Exp), [k])
                    b = take()
                    tok = mm(bank[b][:, 0:n], mqk[:, 4 + hh, sb_ * P:(sb_ + 1) * P], mqk[:, hh, c0:c1_], True, True,
                             [bfree[b], qk_ready], True)
                    k = v(lambda e, b=b, dv=dv, n=n, sb_=sb_, c0=c0, c1_=c1_: e.scalar_tensor_tensor(
                        STm[:, sb_, c0:c1_], bank[b][:, 0:n], SCL, dv, ALU.mult, ALU.mult), [tok, k, st_free])
                    bfree[b] = k
                    dfree[i] = k
                    sr.append(k)
                held.discard(bM)
                for t in range(T):
                    b = take()
                    src = range(0, t + 1) if d == 0 else range(t, T)
                    tok = mm_group(bank[b][:, 0:130], [(STm[:, q, t * P:(t + 1) * P], vx[:, q, hh, :]) for q in src],
                                   [bfree[b], sr[-1], vx_ready, kz])
                    dn = den[:, t:t + 1]
                    k = v(lambda e, dn=dn, b=b: e.tensor_scalar(dn, bank[b][:, 128:129], -1.0, None, ALU.mult), [tok])
                    k = v(lambda e, dn=dn, b=b: e.tensor_tensor(dn, dn, bank[b][:, 128:129], ALU.max), [k])
                    k = v(lambda e, dn=dn, d=d, t=t, hh=hh: e.tensor_tensor(dn, dn, ecol[:, d, t, hh:hh + 1], ALU.max), [k])
                    k = v(lambda e, dn=dn: e.reciprocal(dn, dn), [k])
                    yv = y[:, t, 512 + hh * P:512 + (hh + 1) * P]
                    if d == 0:
                        k = v(lambda e, yv=yv, b=b, dn=dn: e.tensor_scalar(yv, bank[b][:, 0:128], dn, None, ALU.mult), [k])
                    else:
                        k = v(lambda e, yv=yv, b=b, dn=dn: e.scalar_tensor_tensor(yv, bank[b][:, 0:128], dn, yv,
                                                                                ALU.mult, ALU.add), [k])
                    bfree[b] = k
                    hmr = k
                st_free = PE.last()
        dump("ym0", y[:, :, 512:1024], [hmr])
        sqb = STm.rearrange("p b s -> p (b s)")
        for t in range(T):
            for hh in range(4):
                k = a(lambda e, t=t, hh=hh: e.activation(sqb[:, 0:128], y[:, t, 512 + hh * P:512 + (hh + 1) * P], ACT.Square,
                                                      accum_out=ssq[:, t, hh:hh + 1]), [hmr, st_free, ACTE.last()])
        k = rsqrt(rs, ssq[:, :, :].rearrange("p t h -> p (t h)"), 16, 1.0 / 128, 1e-6, [k])
        gmb = gb[:, 0:512]
        tg = load_gb(gmb, mlstm_norm_g_2[0].partition_broadcast(P), [DVE.last(), ACTE.last(), PE.last()])
        ym = [None] * T
        for t in range(T):
            for hh in range(4):
                yv = y[:, t, 512 + hh * P:512 + (hh + 1) * P]
                ym[t] = v(lambda e, yv=yv, t=t, hh=hh: e.scalar_tensor_tensor(
                    yv, yv, rs[:, 4 * t + hh:4 * t + hh + 1], gmb[:, hh * P:(hh + 1) * P], ALU.mult, ALU.mult), [tg, k])
        md = ada(1, [(1024, SH2)], [(0, G1)])
        md = ada(2, [(0, SC2)], [(1024, G2)])
        t1 = v(lambda e: e.tensor_scalar(CS2, SC2, 1.0, None, ALU.add), [md])
        cs2 = v(lambda e: e.tensor_tensor(CS2, CS2, GF, ALU.mult), [t1])

        def ev_o(t, ps, tok):
            ym[t] = gate_with(y[:, t, 512:1024], ps, tok, ym[t], False)
            return ym[t]

        gemm_tok(512, xh, xl, xr, ev_o)
        dump("y", y, [ym[-1], y2[-1]])
        xr = to_T(y, ym)
        for c in range(2):
            def ev_w(t, ps, tok, c=c):
                m = gb[:, 1024 + 512 * (t % 2):1536 + 512 * (t % 2)]
                k = v(lambda e: e.tensor_tensor(m, ps, G1[:, c * 512:(c + 1) * 512], ALU.mult), [tok, md, DVE.last()])
                hv = h[:, t, c * 512:(c + 1) * 512]
                ht[t] = v(lambda e: e.tensor_tensor(hv, hv, m, ALU.add), [k, ht[t]])
                return ht[t]
            gemm_tok(512, xh, xl, xr, ev_w)
        dump("h5", h[:, :, :], [ht[-1]])
        nt = rms_rows(xn, ht)
        xr = to_T(xn, nt, CS2, SH2, [gb[:, 1024:1536], gb[:, 1536:2048]])
        facc = A[:, 8192:12288].rearrange("p (t n) -> p t n", t=T)
        ub = A[:, 0:4096].rearrange("p (i s) -> p i s", i=8)
        uf = [PE.last()] * 8
        ft = [None] * T
        urdy = {}
        nu = [0]

        def ev_down(n, t, c, ps, tok):
            fv = facc[:, t, c * 512:(c + 1) * 512]
            if n == 0:
                ft[t] = v(lambda e: e.tensor_copy(fv, ps), [tok])
            else:
                ft[t] = v(lambda e: e.tensor_tensor(fv, fv, ps, ALU.add), [tok, ft[t]])
            return ft[t]

        for n in range(len(FG) + 1):
            if n < len(FG):
                for q in range(FG[n][1] // 2):
                    gt = {}

                    def ev_gate(j, ps, tok):
                        i = 2 * (nu[0] % 4) + j
                        gx = ub[:, i, :]
                        k1 = a(lambda e: e.activation(gx, ps, ACT.Exp, scale=-1.0), [tok, uf[i]])
                        k2 = v(lambda e: e.tensor_scalar(gx, gx, 1.0, None, ALU.add), [k1])
                        k3 = v(lambda e: e.reciprocal(gx, gx), [k2])
                        gt[j] = v(lambda e: e.tensor_tensor(gx, gx, ps, ALU.mult), [k3])
                        return gt[j]

                    def ev_up(j, ps, tok, q=q, n=n):
                        i = 2 * (nu[0] % 4) + j
                        gx = ub[:, i, :]
                        k1 = v(lambda e: e.tensor_tensor(gx, gx, ps, ALU.mult), [tok, gt[j]])
                        fi = 2 * q + j
                        uf[i] = urdy[n] = split(gx, uh[:, n % 2, fi, :], ul[:, n % 2, fi, :], [k1, u_free[n % 2]])
                        return k1

                    gemm_T(xh, xl, xr, ev_gate)
                    gemm_T(xh, xl, xr, ev_up)
                    nu[0] += 1
            if n > 0:
                down(n - 1, FG[n - 1][1], urdy[n - 1], ev_down)
        fg = A[:, 0:1024]
        tg = load_gb(fg, final_norm_g_2.partition_broadcast(P), [DVE.last(), ACTE.last(), PE.last()])
        for t in range(T):
            k = v(lambda e, t=t: e.tensor_tensor(facc[:, t, :], facc[:, t, :], G2, ALU.mult), [ft[t]])
            ht[t] = v(lambda e, t=t: e.tensor_tensor(h[:, t, :], h[:, t, :], facc[:, t, :], ALU.add), [k, ht[t]])
        nt = rms_rows(facc, ht)
        n_out = 0
        for t in range(T):
            k = v(lambda e, t=t: e.tensor_tensor(facc[:, t, :], facc[:, t, :], fg, ALU.mult), [nt[t], tg])
            SP.put([k], lambda e, t=t: e.dma_start(out[0, t * P:(t + 1) * P, :], facc[:, t, :]).then_inc(s_out, 16),
                   mark=False)
        SP.put([(s_out, 16 * T)], lambda e: None, mark=False)
        assert used[0] == len(chunks), (used[0], len(chunks))

        block = ctx.enter_context(nc.Block())

        @block.sync
        def _(e):
            for f in SP.todo:
                f(e)

        @block.gpsimd
        def _(e):
            for f in POOL.todo:
                f(e)

        @block.scalar
        def _(e):
            for f in ACTE.todo:
                f(e)

        @block.tensor
        def _(e):
            for f in PE.todo:
                f(e)

        @block.vector
        def _(e):
            for f in DVE.todo:
                f(e)


NAMES = ["x", "positions", "a_w_in", "a_w_o", "b_w_in", "b_w_a2", "b_b_a", "b_g_norm", "b_w_o", "ln_mix_g", "ln_mix_b",
         "mlp_w_up", "mlp_w_down", "ln_mlp_g", "ln_mlp_b", "c_2", "w_ada_2", "b_ada_2", "norm_mix_g_2", "w_in_2",
         "q_norm_g_2", "k_norm_g_2", "conv_w_2", "conv_b_2", "gate_b_2", "mlstm_norm_g_2", "w_out_2", "norm_ffn_g_2",
         "w_gate_2", "w_up_2", "w_down_2", "final_norm_g_2"]


def packed(inputs):
    def by_part(a):
        return np.asarray(a).reshape(-1, P).T

    pad = np.zeros((P, 4), np.float32)
    cols = [by_part(inputs["b_b_a"]), pad, by_part(inputs["c_2"]), by_part(inputs["norm_mix_g_2"]),
            by_part(inputs["norm_ffn_g_2"]), by_part(inputs["conv_w_2"]), by_part(inputs["conv_b_2"])]
    return np.ascontiguousarray(np.concatenate(cols, 1)), np.ascontiguousarray(by_part(inputs["positions"]))


def kernel(**inputs):
    import concourse.bacc as bacc
    from concourse.bass_utils import run_bass_kernel_spmd

    nc = bacc.Bacc("TRN2", target_bir_lowering=False, num_devices=1)
    arrays, args = {}, []
    given = {n: np.ascontiguousarray(inputs[n]) for n in NAMES}
    given["cst"], given["lmask"] = constants()
    given["cols"], given["posn"] = packed(inputs)
    for name, arr in given.items():
        arrays["in_" + name] = arr
        args.append(nc.dram_tensor("in_" + name, arr.shape, mybir.dt.from_np(arr.dtype), kind="ExternalInput").ap())
    out = nc.dram_tensor("out_0", (1, SEQ, D), F, kind="ExternalOutput").ap()
    program(nc, *args, out)
    r = run_bass_kernel_spmd(nc, [arrays], core_ids=[0])
    return r.results[0]["out_0"]
```

```python
from contextlib import ExitStack

import numpy as np
import concourse.bass as bass
from concourse import mybir

F = mybir.dt.float32
R = mybir.dt.float32r
I32 = mybir.dt.int32
U8 = mybir.dt.uint8
ALU = mybir.AluOpType
ACT = mybir.ActivationFunctionType
AX = mybir.AxisListType.X

P = 128
T = 4
SEQ = 512
D = 1024
ALPHA = 4.0 ** 0.25
BIG = 1e30
NRAW = 3
NHL = 2
CH = 2048
LEVELS = [64, 32, 16, 8, 4, 2, 1]

C_ID, C_CB, C_CBT, C_ONE, C_INV, C_RC, C_RS = 0, 128, 256, 384, 512, 520, 776
C_END = 1032


def constants():
    c = np.zeros((P, C_END), np.float32)
    i = np.arange(P)
    c[:, C_ID:C_ID + P] = np.eye(P)
    c[:, C_CB:C_CB + P] = np.where(i[None, :] > i[:, None], -BIG, 0.0)
    c[:, C_CBT:C_CBT + P] = np.where(i[None, :] < i[:, None], -BIG, 0.0)
    c[:, C_ONE:C_ONE + P] = 1.0
    c[:, C_INV:C_INV + 8] = np.float32(500000.0) ** (-np.arange(0, 16, 2, dtype=np.float32) / np.float32(16))
    inv = np.float32(10000.0) ** (-np.arange(0, 32, 2, dtype=np.float32) / np.float32(32))
    for t in range(T):
        tok = t * P + i
        ar = (tok // 64).astype(np.float32)[:, None] * inv[None, :]
        ac = (tok % 64).astype(np.float32)[:, None] * inv[None, :]
        c[:, C_RC + t * 64:C_RC + t * 64 + 64] = np.concatenate([np.cos(ar), np.cos(ar), np.cos(ac), np.cos(ac)], 1)
        c[:, C_RS + t * 64:C_RS + t * 64 + 64] = np.concatenate([-np.sin(ar), np.sin(ar), -np.sin(ac), np.sin(ac)], 1)
    m = np.zeros((P, 8, P), np.float32)
    for n, s in enumerate(LEVELS):
        j, k = i[:, None], i[None, :]
        m[:, n, :] = (j // (2 * s) == k // (2 * s)) & (j % (2 * s) < s) & (k % (2 * s) >= s)
    m[:, 7, :] = np.eye(P)
    return c, m.reshape(P, 8 * P)


class Line:

    def __init__(self, sem):
        self.sem, self.n, self.todo, self.seen = sem, 0, [], {}

    def put(self, after, fn, mark=True):
        for tok in after:
            if tok is None:
                continue
            sem, v = tok
            if self.seen.get(sem.name, 0) < v:
                self.seen[sem.name] = v
                self.todo.append(lambda e, s=sem, v=v: e.wait_ge(s, v))
        if not mark:
            self.todo.append(fn)
            return None
        self.n += 1
        self.todo.append(lambda e: fn(e).then_inc(self.sem, 1))
        return (self.sem, self.n)

    def last(self):
        return (self.sem, self.n)


def program(nc, x, positions, a_w_in, a_w_o, b_w_in, b_w_a2, b_b_a, b_g_norm, b_w_o, ln_mix_g, ln_mix_b,
            mlp_w_up, mlp_w_down, ln_mlp_g, ln_mlp_b, c_2, w_ada_2, b_ada_2, norm_mix_g_2, w_in_2, q_norm_g_2,
            k_norm_g_2, conv_w_2, conv_b_2, gate_b_2, mlstm_norm_g_2, w_out_2, norm_ffn_g_2, w_gate_2, w_up_2,
            w_down_2, final_norm_g_2, cst, lmask, cols, posn, out, dbg=None):
    ctx = ExitStack()
    with ctx:
        def sb(name, shape, dt=F):
            return ctx.enter_context(nc.sbuf_tensor(name, shape, dt))

        def sem(name):
            return ctx.enter_context(nc.semaphore(name))

        h = sb("h", [P, T, D])
        xh = sb("xh", [P, 8, SEQ], R)
        xl = sb("xl", [P, 8, SEQ], R)
        raw = sb("raw", [P, NRAW, CH])
        wh = sb("wh", [P, NHL, CH], R)
        wl = sb("wl", [P, NHL, CH], R)
        uh = sb("uh", [P, 2, 4, SEQ], R)
        ul = sb("ul", [P, 2, 4, SEQ], R)
        C = sb("C", [P, C_END])
        LM = sb("LM", [P, 8 * P], U8)
        gb = sb("gb", [P, 2048])
        A = sb("A", [P, 13344])
        small = sb("small", [P, 576])
        stats = sb("stats", [P, T, 2, 6])
        mv = sb("mv", [P, T, 2])
        rsv = sb("rsv", [P, 64])
        rsy = sb("rsy", [P, 64])
        rsa = sb("rsa", [P, 64])
        posi = sb("posi", [P, T], I32)
        bank = [ctx.enter_context(nc.psum_tensor(f"bank{i}", [P, 512], F)) for i in range(8)]

        PE, DVE, ACTE, POOL, SP = (Line(sem(n)) for n in ("s_pe", "s_dve", "s_act", "s_pool", "s_sp"))
        s_raw = [sem(f"s_raw{i}") for i in range(NRAW)]
        s_in = sem("s_in")
        s_gb = sem("s_gb")
        s_acc = sem("s_acc")
        s_out = sem("s_out")
        s_dbg = sem("s_dbg")

        ident = C[:, C_ID:C_ID + P]
        ones = C[:, C_ONE:C_ONE + P]
        CB = C[:, C_CB:C_CB + P]
        CBT = C[:, C_CBT:C_CBT + P]
        dumps = [0]

        def dump(name, ap, after):
            if dbg is None or name not in dbg:
                return
            dst = dbg[name]
            SP.put(after, lambda e: e.dma_start(dst, ap).then_inc(s_dbg, 16), mark=False)
            dumps[0] += 1
            SP.todo.append(lambda e, v=16 * dumps[0]: e.wait_ge(s_dbg, v))

        bfree = [None] * 8
        bnext = [0]

        held = set()

        def take(hold=False):
            while bnext[0] in held:
                bnext[0] = (bnext[0] + 1) % 8
            b = bnext[0]
            bnext[0] = (b + 1) % 8
            if hold:
                held.add(b)
            return b

        def v(fn, after=()):
            return DVE.put(after, fn)

        def a(fn, after=()):
            return ACTE.put(after, fn)

        def g(fn, after=()):
            return POOL.put(after, fn)

        def mm(out_, l, r, start, stop, after=(), mark=False):
            return PE.put(after, lambda e: e.matmul(out_, l, r, start=start, stop=stop), mark)

        def mm_group(out_, pairs, after=(), mark=True):
            tok = None
            for i, (l, r) in enumerate(pairs):
                tok = mm(out_, l, r, i == 0, i == len(pairs) - 1, after if i == 0 else (), mark and i == len(pairs) - 1)
            return tok

        def tr(out_, in_, idn, after=(), mark=False):
            return PE.put(after, lambda e: e.transpose(out_, in_, idn), mark)

        n_in = [0]

        def load(dst, src):
            n_in[0] += 1
            SP.put((), lambda e: e.dma_start(dst, src).then_inc(s_in, 16), mark=False)

        def col(n, w):
            return small[:, n:n + w]

        load(posi[:, :], posn)
        load(C[:, :], cst)
        for t in range(T):
            load(h[:, t, :], x[0, t * P:(t + 1) * P, :])
        load(A[:, 12288:13312], lmask)
        load(col(0, 80), cols[:, 0:80])
        load(col(256, 64), cols[:, 80:144])
        load(col(448, 48), cols[:, 144:192])
        BADA = col(448, 48)
        BA, CC, GM, GF, CVB = col(0, 4), col(8, 8), col(16, 8), col(24, 8), col(72, 8)
        CW = col(32, 40).rearrange("p (w k) -> p w k", k=8)
        GB = col(80, 16)
        load(GB, gate_b_2[0].partition_broadcast(P))
        SH1, SC1, SH2, SC2 = col(96, 8), col(104, 8), col(112, 8), col(120, 8)
        GC1, GC2 = col(240, 8), col(248, 8)
        LNC = {(n, i): col(256 + 16 * j + 8 * i, 8) for j, n in enumerate(("mg", "mb", "fg", "fb")) for i in range(2)}
        CS1, CS2 = col(128, 8), col(136, 8)
        S0 = (s_in, 16 * n_in[0])

        v(lambda e: e.tensor_copy(LM[:, :], A[:, 12288:13312]), [S0])

        chunks = []

        def plan(w, r0, nk, c0, nc_):
            chunks.append((w[r0:r0 + nk * P, c0:c0 + nc_].rearrange("(k p) n -> p k n", p=P), nk, nc_))

        def plan_tok(w, c0, n):
            if n <= 256:
                plan(w, 0, 8, c0, n)
            else:
                plan(w, 0, 4, c0, n)
                plan(w, 512, 4, c0, n)

        def plan_pair(w):
            for r0 in (0, 512):
                for c0 in (0, 512):
                    plan(w, r0, 4, c0, 512)

        wa, wb, w2 = a_w_in[0], b_w_in[0], w_in_2[0]

        ada_of = {}

        def plan_ada(n):
            ada_of[len(chunks)] = n
            plan(w_ada_2[0], (n % 8) * P, 1, (n // 8) * 2048, 2048)

        def plan_mlp(i):
            for n in range(9):
                if n < 8:
                    for q in range(2):
                        plan(mlp_w_up[i], 0, 8, n * 512 + q * 256, 256)
                        if i == 0:
                            plan_ada(2 * n + q)
                        elif q == 0:
                            plan_ada(16 + n)
                if n > 0:
                    for c in range(2):
                        plan(mlp_w_down[i], (n - 1) * 512, 4, c * 512, 512)

        plan_tok(wa, 1536, 512)
        plan_tok(wa, 2048, 72)
        plan_tok(wa, 1024, 512)
        plan_tok(wa, 0, 512)
        plan_tok(wa, 512, 512)
        plan_pair(a_w_o[0])
        plan_mlp(0)
        plan(wb, 0, 8, 3072, 16)
        for n in range(4):
            plan(wb, 0, 8, n * 256, 256)
        for n in range(4):
            plan_tok(wb, 1024 + 512 * n, 512)
        plan_pair(b_w_o[0])
        plan_mlp(1)
        plan_tok(w2, 0, 512)
        plan_tok(w2, 512, 256)
        for n in range(4):
            plan(w2, 0, 8, 768 + n * 256, 256)
        plan_tok(w2, 1792, 512)
        plan_tok(w2, 2816, 16)
        core2 = [len(chunks)]
        plan_tok(w2, 2304, 512)
        plan_pair(w_out_2[0])
        FG = [(0, 2), (2, 4), (6, 4), (10, 4), (14, 4), (18, 4)]
        for n in range(len(FG) + 1):
            if n < len(FG):
                f0, nf = FG[n]
                for q in range(nf // 2):
                    plan(w_gate_2[0], 0, 8, (f0 + 2 * q) * P, 256)
                    plan(w_up_2[0], 0, 8, (f0 + 2 * q) * P, 256)
            if n > 0:
                f0, nf = FG[n - 1]
                for c in range(2):
                    plan(w_down_2[0], f0 * P, nf, c * 512, 512)

        used = [0]
        prepped = [0]
        loaded = [0]
        raw_free = [None] * NRAW
        hl_free = [None] * NHL
        ready = {}
        waiting = []
        limit = [core2[0]]

        def fetch(i):
            if i >= len(chunks):
                return
            if i >= limit[0]:
                waiting.append(i)
                return
            src, nk, ncol = chunks[i]
            s = i % NRAW
            dst = raw[:, s, 0:nk * ncol].rearrange("p (k n) -> p k n", k=nk)
            SP.put([raw_free[s]], lambda e: e.dma_start(dst, src).then_inc(s_raw[s], 16), mark=False)

        def release(after):
            limit[0] = len(chunks)
            for s in range(NRAW):
                raw_free[s] = None
            SP.put(after, lambda e: None, mark=False)
            for i in list(waiting):
                fetch(i)

        def landed(i):
            return (s_raw[i % NRAW], 16 * (i // NRAW + 1))

        slot_of = {}
        nsplit = [0]

        def split_chunk(i, later=False):
            if i in ada_of:
                ada(i, ada_of[i])
                return
            src, nk, ncol = chunks[i]
            r, n = i % NRAW, nk * ncol
            s = nsplit[0] % NHL
            nsplit[0] += 1
            slot_of[i] = s
            t1 = a(lambda e: e.activation(wh[:, s, 0:n], raw[:, r, 0:n], ACT.Copy), [landed(i), hl_free[s]])

            def low():
                t2 = v(lambda e: e.tensor_tensor(wl[:, s, 0:n], raw[:, r, 0:n], wh[:, s, 0:n].bitcast(F), ALU.subtract),
                       [landed(i), t1])
                raw_free[r] = t2
                ready[i] = t2
                fetch(i + NRAW)

            if later:
                return low
            low()

        def prep_ahead():
            i = prepped[0]
            assert i == used[0] and i not in ada_of
            if i >= limit[0]:
                return lambda: None
            prepped[0] += 1
            return split_chunk(i, True)

        def next_chunk(look=True):
            i = used[0]
            while i in ada_of:
                i += 1
            used[0] = i + 1
            ahead = i + 1 if look else i
            while ahead in ada_of:
                ahead += 1
            while prepped[0] <= ahead and prepped[0] < len(chunks):
                if prepped[0] < limit[0]:
                    split_chunk(prepped[0])
                elif prepped[0] == i or limit[0] == len(chunks):
                    raise AssertionError
                else:
                    break
                prepped[0] += 1
            src, nk, ncol = chunks[i]
            s = slot_of[i]
            H = wh[:, s, 0:nk * ncol].rearrange("p (k n) -> p k n", k=nk)
            L = wl[:, s, 0:nk * ncol].rearrange("p (k n) -> p k n", k=nk)
            return H, L, ready[i], s, nk, ncol

        cond = small[:, 232:240]
        t1 = a(lambda e: e.activation(cond, CC, ACT.Exp, scale=-1.0), [S0])
        t1 = v(lambda e: e.tensor_scalar(cond, cond, 1.0, None, ALU.add), [t1])
        t1 = v(lambda e: e.reciprocal(cond, cond), [t1])
        cond_ready = v(lambda e: e.tensor_tensor(cond, cond, CC, ALU.mult), [t1])
        acc = A[:, 4096:6144]
        s_k = [None]
        mod_cols = [SH1, SC1, GC1, SH2, SC2, GC2]

        def ada(i, n):
            r, kt = n // 8, n % 8
            rw = raw[:, i % NRAW, :]
            if kt == 0:
                k = v(lambda e: e.tensor_scalar(acc, rw, cond[:, 0:1], None, ALU.mult), [landed(i), PE.last(), cond_ready])
            else:
                k = v(lambda e: e.scalar_tensor_tensor(acc, rw, cond[:, kt:kt + 1], acc, ALU.mult, ALU.add),
                      [landed(i), s_k[0]])
            s_k[0] = raw_free[i % NRAW] = k
            fetch(i + NRAW)
            if kt == 7:
                owed.append((r, k))

        owed = []

        def ada_sum():
            while owed:
                r, k = owed.pop()
                b = take()
                for j in range(16):
                    tok = mm(bank[b][:, j:j + 1], acc[:, j * P:(j + 1) * P], ones[:, 0:1], True, True, [bfree[b], k], j == 15)
                for q in range(2):
                    dst, bc = mod_cols[2 * r + q], BADA[:, 16 * r + 8 * q:16 * r + 8 * q + 8]
                    bfree[b] = v(lambda e, dst=dst, q=q, bc=bc: e.tensor_tensor(dst, bank[b][:, 8 * q:8 * q + 8], bc,
                                                                               ALU.add), [tok])

        for i in range(NRAW):
            fetch(i)

        background = []

        def tick(n=1):
            for _ in range(n):
                for job in list(background):
                    if next(job, background) is background:
                        background.remove(job)

        def drain():
            while background:
                tick()

        def as_list(r):
            return r if isinstance(r, list) else [r] * 8

        def gemm_tok(n, hi, lo, ready_x, evac, ticks=0):
            bs = [take(True) for _ in range(T)]
            k0 = 0
            rx = as_list(ready_x)
            while k0 < 8:
                H, L, rw, s, nk, ncol = next_chunk()
                assert ncol == n, (ncol, n)
                for t in range(T):
                    for k in range(nk):
                        kk = k0 + k
                        X, Y = hi[:, kk, t * P:(t + 1) * P], lo[:, kk, t * P:(t + 1) * P]
                        o = bank[bs[t]][:, 0:n]
                        first, end = kk == 0, kk == 7
                        mm(o, X, H[:, k, :], first, False, [rw, rx[kk], bfree[bs[t]]] if first else [rw, rx[kk]])
                        mm(o, X, L[:, k, :], False, False)
                        tok = mm(o, Y, H[:, k, :], False, end, mark=(k == nk - 1))
                    if end:
                        bfree[bs[t]] = evac(t, bank[bs[t]][:, 0:n], tok)
                        held.discard(bs[t])
                    tick(ticks)
                hl_free[s] = PE.last()
                k0 += nk

        def panel_pair(X, Y, nk, out_of, first, after, evac):
            W = [next_chunk(), next_chunk(False)]
            assert W[0][4] == nk
            late = None
            for t in range(T):
                toks = []
                for c in range(2):
                    H, L, rw = W[c][0:3]
                    b = out_of(t, c)
                    for k in range(nk):
                        o = bank[b][:, :]
                        mm(o, X(k, t), H[:, k, :], first and k == 0, False, [rw, bfree[b]] + after(k) if k == 0 else after(k))
                        mm(o, X(k, t), L[:, k, :], False, False)
                        tok = mm(o, Y(k, t), H[:, k, :], False, k == nk - 1, mark=(k == nk - 1))
                    toks.append((b, tok))
                if t == T - 1:
                    for c in range(2):
                        hl_free[W[c][3]] = PE.last()
                    if prepped[0] < len(chunks):
                        late = prep_ahead()
                for c, (b, tok) in enumerate(toks):
                    bfree[b] = evac(t, c, bank[b][:, :], tok)
                    held.discard(b)
            if late:
                late()

        def gemm_pair(hi, lo, ready_x, evac):
            bs = [[take(True) for c in range(2)] for t in range(T)]
            rx = as_list(ready_x)
            for c in range(2):
                H, L, rw, s, nk, ncol = next_chunk()
                for t in range(T):
                    for k in range(nk):
                        X, Y = hi[:, k, t * P:(t + 1) * P], lo[:, k, t * P:(t + 1) * P]
                        o = bank[bs[t][c]][:, :]
                        mm(o, X, H[:, k, :], k == 0, False, [rw, rx[k], bfree[bs[t][c]]] if k == 0 else [rx[k]])
                        mm(o, X, L[:, k, :], False, False)
                        mm(o, Y, H[:, k, :], False, False, mark=(k == nk - 1 and t == T - 1))
                hl_free[s] = PE.last()
            panel_pair(lambda k, t: hi[:, 4 + k, t * P:(t + 1) * P], lambda k, t: lo[:, 4 + k, t * P:(t + 1) * P], 4,
                       lambda t, c: bs[t][c], False, lambda k: [rx[4 + k]], evac)

        def gemm_T(hi, lo, ready_x, evac, ticks=0):
            H, L, rw, s, nk, ncol = next_chunk()
            assert nk == 8
            rx = as_list(ready_x)
            for j in range(max(1, ncol // P)):
                w = min(P, ncol)
                b = take()
                o = bank[b][0:w, :]
                for k in range(8):
                    c = slice(j * P, j * P + w)
                    mm(o, H[:, k, c], hi[:, k, :], k == 0, False, [rw, rx[k], bfree[b]] if k == 0 else [rx[k]])
                    mm(o, L[:, k, c], hi[:, k, :], False, False)
                    tok = mm(o, H[:, k, c], lo[:, k, :], False, k == 7, mark=(k == 7))
                if (j + 1) * P >= ncol:
                    hl_free[s] = PE.last()
                bfree[b] = evac(j, o, tok)
                tick(ticks)

        def split(src, dh, dl, after):
            t1 = a(lambda e: e.activation(dh, src, ACT.Copy), after)
            return v(lambda e: e.tensor_tensor(dl, src, dh.bitcast(F), ALU.subtract), [t1])

        mid = [A[:, 12288:12800], A[:, 12800:13312]]

        def to_T(src, toks, scale=None, shift=None, cols_ready=None):
            bs = [take(True) for _ in range(8)]
            out_ = []
            mf = [None, None]
            for t in range(T):
                for k in range(8):
                    tok = tr(bank[bs[k]][:, t * P:(t + 1) * P], src[:, t, k * P:(k + 1) * P], ident,
                             [bfree[bs[k]], toks[t]], mark=(t == T - 1))
                    if t < T - 1:
                        continue
                    ps = bank[bs[k]][:, :]
                    if scale is None:
                        t2 = bfree[bs[k]] = split(ps, xh[:, k, :], xl[:, k, :], [tok])
                    else:
                        m = mid[k % 2]
                        t1 = a(lambda e, ps=ps, m=m, k=k: e.activation(m, ps, ACT.Identity, bias=shift[:, k:k + 1],
                                                                       scale=scale[:, k:k + 1]), [tok, mf[k % 2], cols_ready])
                        bfree[bs[k]] = t1
                        if k % 2:
                            t2 = v(lambda e, m=m, k=k: e.tensor_copy(xh[:, k, :], m), [t1])
                        else:
                            t2 = a(lambda e, m=m, k=k: e.activation(xh[:, k, :], m, ACT.Copy), [t1])
                        t2 = mf[k % 2] = v(lambda e, m=m, k=k: e.tensor_tensor(xl[:, k, :], m, xh[:, k, :].bitcast(F),
                                                                               ALU.subtract), [t1, t2])
                    out_.append(t2)
            held.difference_update(bs)
            return out_

        def rsqrt(dst, src, n, scale, eps, after, c0=0):
            vv, yy, aa = rsv[:, c0:c0 + n], rsy[:, c0:c0 + n], rsa[:, c0:c0 + n]
            k = v(lambda e: e.tensor_scalar(vv, src, scale, eps, ALU.mult, ALU.add), after)
            k = v(lambda e: e.tensor_scalar(yy.bitcast(I32), vv.bitcast(I32), -0.5, 1597463007.0, ALU.mult, ALU.add), [k])
            for q in range(3):
                if n == 1:
                    k = v(lambda e: e.scalar_tensor_tensor(aa, yy, yy, vv, ALU.mult, ALU.mult), [k])
                else:
                    k = v(lambda e: e.tensor_tensor(aa, yy, yy, ALU.mult), [k])
                    k = v(lambda e: e.tensor_tensor(aa, aa, vv, ALU.mult), [k])
                k = v(lambda e: e.tensor_scalar(aa, aa, -0.5, 1.5, ALU.mult, ALU.add), [k])
                k = v(lambda e, q=q: e.tensor_tensor(dst if q == 2 else yy, yy, aa, ALU.mult), [k])
            return k

        ngb = [0]

        def load_gb(dst, src, after):
            ngb[0] += 1
            POOL.put(after, lambda e: e.dma_start(dst, src).then_inc(s_gb, 16), mark=False)
            return (s_gb, 16 * ngb[0])

        ln_rs = small[:, 144:148]
        mrs = small[:, 500:504]

        def ln_stats(t, q, tok):
            return v(lambda e: e.bn_stats(stats[:, t, q, :], h[:, t, q * 512:(q + 1) * 512]), [tok])

        def ln_rows(t, tok):
            ts = v(lambda e: e.bn_aggr(mv[:, t, :], stats[:, t, :, :].rearrange("p a b -> p (a b)")), [tok])
            k = rsqrt(ln_rs[:, t:t + 1], mv[:, t, 1:2], 1, 1.0, 1e-5, [ts], 32 + t)
            k = v(lambda e: e.scalar_tensor_tensor(mrs[:, t:t + 1], mv[:, t, 0:1], -1.0, ln_rs[:, t:t + 1],
                                                   ALU.mult, ALU.mult), [k])
            return a(lambda e: e.activation(h[:, t, :], h[:, t, :], ACT.Identity, bias=mrs[:, t:t + 1],
                                            scale=ln_rs[:, t:t + 1]), [k, tok])

        def ln_load(gd, bd):
            free = [POOL.last()]
            load_gb(gb[:, 0:D], gd.partition_broadcast(P), free + [DVE.last(), ACTE.last(), PE.last()])
            return load_gb(gb[:, D:2 * D], bd.partition_broadcast(P), ())

        def ln_finish(nt, tg, gain, shift):
            xr_ = to_T(h, nt, gain, shift)
            read = PE.last()
            toks = []
            for t in range(T):
                k = g(lambda e, t=t: e.tensor_tensor(h[:, t, :], h[:, t, :], gb[:, 0:D], ALU.mult), [tg, read, nt[t]])
                toks.append(g(lambda e, t=t: e.tensor_tensor(h[:, t, :], h[:, t, :], gb[:, D:2 * D], ALU.add), [k]))
            return xr_, toks

        def residual_out(hi_ready, ht):
            toks = [None] * T

            def evac(t, c, ps, tok):
                hv = h[:, t, c * 512:(c + 1) * 512]
                k = v(lambda e: e.scalar_tensor_tensor(hv, hv, ALPHA, ps, ALU.mult, ALU.add), [tok, ht[t]])
                toks[t] = ln_stats(t, c, k)
                if c:
                    toks[t] = ln_rows(t, toks[t])
                return k

            gemm_pair(xh, xl, hi_ready, evac)
            return toks

        u_free = [None, None]

        def down(n, nf, u_ready, evac, last=False):
            bsel = n % 2
            if last:
                panel_pair(lambda f, t: uh[:, bsel, f, t * P:(t + 1) * P], lambda f, t: ul[:, bsel, f, t * P:(t + 1) * P], nf,
                           lambda t, c: take(), True, lambda f: [u_ready], lambda t, c, ps, tok: evac(n, t, c, ps, tok))
                ada_sum()
                u_free[bsel] = PE.last()
                return
            for c in range(2):
                H, L, rw, s, nk, ncol = next_chunk()
                assert nk == nf
                for t in range(T):
                    b = take()
                    for f in range(nf):
                        X = uh[:, bsel, f, t * P:(t + 1) * P]
                        Y = ul[:, bsel, f, t * P:(t + 1) * P]
                        mm(bank[b][:, :], X, H[:, f, :], f == 0, False, [rw, u_ready, bfree[b]] if f == 0 else ())
                        mm(bank[b][:, :], X, L[:, f, :], False, False)
                        tok = mm(bank[b][:, :], Y, H[:, f, :], False, f == nf - 1, mark=(f == nf - 1))
                    bfree[b] = evac(n, t, c, bank[b][:, :], tok)
                hl_free[s] = PE.last()
            ada_sum()
            u_free[bsel] = PE.last()

        def mlp(x_ready, ht, finish=None):
            toks = [None] * T
            urdy = {}
            rb = A[:, 0:2048].rearrange("p (n s) -> p n s", n=4)
            prev = [None] * 4

            def evac_down(n, t, c, ps, tok):
                hv = h[:, t, c * 512:(c + 1) * 512]
                if n == 0:
                    toks[t] = v(lambda e: e.scalar_tensor_tensor(hv, hv, ALPHA, ps, ALU.mult, ALU.add), [tok, ht[t]])
                else:
                    toks[t] = v(lambda e: e.tensor_tensor(hv, hv, ps, ALU.add), [tok, toks[t]])
                k = toks[t]
                if n == 7:
                    toks[t] = ln_stats(t, c, k)
                    if c:
                        toks[t] = (finish or ln_rows)(t, toks[t])
                return k

            for n in range(9):
                if n < 8:
                    for q in range(2):
                        def evac(j, ps, tok, q=q, n=n):
                            i = 2 * q + j
                            r = rb[:, i, :]
                            t1 = a(lambda e: e.activation(r, ps, ACT.Relu), [tok, prev[i]])
                            t2 = v(lambda e: e.tensor_tensor(r, r, r, ALU.mult), [t1])
                            prev[i] = urdy[n] = split(r, uh[:, n % 2, i, :], ul[:, n % 2, i, :], [t2, u_free[n % 2]])
                            return t1
                        gemm_T(xh, xl, x_ready, evac)
                if n > 0:
                    down(n - 1, 4, urdy[n - 1], evac_down, n == 8)
            return toks

        pf = small[:, 148:152]
        ang = small[:, 152:184]
        nn = small[:, 184:216]
        rot = sb("rot", [P, 2, T, 16])
        cosd, sind = rot[:, 0, :, :], rot[:, 1, :, :]
        t0 = v(lambda e: e.tensor_copy(pf, posi[:, :]), [S0])
        a3 = ang.rearrange("p (t k) -> p t k", t=T)
        n3 = nn.rearrange("p (t k) -> p t k", t=T)
        t0 = v(lambda e: e.tensor_tensor(a3, pf.unsqueeze(2).broadcast_to([P, T, 8]),
                                         C[:, C_INV:C_INV + 8].unsqueeze(1).broadcast_to([P, T, 8]), ALU.mult), [t0])
        MAGIC = 12582912.0
        t0 = v(lambda e: e.tensor_scalar(nn, ang, float(np.float32(1 / (2 * np.pi))), MAGIC, ALU.mult, ALU.add), [t0])
        t0 = v(lambda e: e.tensor_scalar(nn, nn, MAGIC, None, ALU.subtract), [t0])
        c1 = 6.28125
        c2 = float(np.float32(np.round((2 * np.pi - c1) * 2 ** 21) / 2 ** 21))
        c3 = float(np.float32(2 * np.pi - c1 - c2))
        for cc in (c1, c2, c3):
            t0 = v(lambda e, cc=cc: e.scalar_tensor_tensor(ang, nn, -cc, ang, ALU.mult, ALU.add), [t0])
        t0 = v(lambda e: e.tensor_scalar(ang, ang, 3.1415925, -3.1415925, ALU.min, ALU.max), [t0])
        t1 = a(lambda e: e.activation(sind[:, :, 8:16], a3, ACT.Sin), [t0])
        t2 = a(lambda e: e.activation(n3, a3, ACT.Sin, scale=0.5), [t0, t1])
        t3 = v(lambda e: e.tensor_tensor(nn, nn, nn, ALU.mult), [t2])
        t3 = v(lambda e: e.tensor_scalar(cosd[:, :, 0:8], n3, -2.0, 1.0, ALU.mult, ALU.add), [t3])
        t3 = v(lambda e: e.tensor_scalar(cosd[:, :, 8:16], n3, -2.0, 1.0, ALU.mult, ALU.add), [t3])
        rot_ready = v(lambda e: e.tensor_scalar(sind[:, :, 0:8], sind[:, :, 8:16], -1.0, None, ALU.mult), [t1])

        def rotary(view, nh, after):
            ta = gb[:, 0:nh * 16 * T].rearrange("p (t g k) -> p t g k", t=T, k=16)
            tb = gb[:, 512:512 + nh * 16 * T].rearrange("p (t g k) -> p t g k", t=T, k=16)
            cv = cosd.unsqueeze(2).broadcast_to([P, T, nh, 16])
            sv = sind.unsqueeze(2).broadcast_to([P, T, nh, 16])
            x1 = v(lambda e: e.tensor_tensor(ta, view[:, :, :, 0:16], cv, ALU.mult), after)
            x2 = v(lambda e: e.tensor_tensor(tb[:, :, :, 0:8], view[:, :, :, 8:16], sv[:, :, :, 0:8], ALU.mult), after)
            x3 = v(lambda e: e.tensor_tensor(tb[:, :, :, 8:16], view[:, :, :, 0:8], sv[:, :, :, 8:16], ALU.mult), after)
            return v(lambda e: e.tensor_tensor(view[:, :, :, 0:16], ta, tb, ALU.add), [x1, x2, x3])

        def turn(view, nt, dst, after, scale=None):
            last = []
            for j in range(nt):
                b = take()
                for t in range(T):
                    tok = tr(bank[b][:, t * P:(t + 1) * P], view[:, t, j * P:(j + 1) * P], ident,
                             [bfree[b]] + list(after), mark=(t == T - 1))
                d = dst[:, j, :]
                bfree[b] = a(lambda e, b=b, d=d: e.activation(d, bank[b][:, :], ACT.Copy), [tok])
                last.append(bfree[b])
            return last[-1]

        xr = to_T(h, [S0] * T)

        qT = A[:, 0:4096].rearrange("p (j s) -> p j s", j=8)
        iqT = A[:, 0:2048].rearrange("p (j s) -> p j s", j=4)
        ikT = A[:, 2048:2560].rearrange("p (j s) -> p j s", j=1)
        kT = A[:, 4096:6144].rearrange("p (j s) -> p j s", j=4)
        vt = A[:, 6144:7168].rearrange("p (t n) -> p t n", t=T)
        bias = A[:, 7168:9216].rearrange("p (t n) -> p t n", t=T)
        tmp = A[:, 9216:11264].rearrange("p (t n) -> p t n", t=T)
        kd = A[:, 11264:13312].rearrange("p (t n) -> p t n", t=T)
        iw = sb("iw", [P, T, 8])

        ev = []

        def ev_tmp(t, ps, tok):
            k = a(lambda e: e.activation(tmp[:, t, :], ps, ACT.Copy), [tok])
            ev.append(k)
            return k

        gemm_tok(512, xh, xl, xr, ev_tmp)
        riq = rotary(tmp.rearrange("p t (g k) -> p t g k", k=64), 8, [rot_ready, ev[-1]])
        kd1 = gb[:, 1536:2048].rearrange("p (t n) -> p t n", t=T)
        ev = []

        def ev_ik(t, ps, tok):
            for q in range(2):
                a(lambda e, q=q: e.activation(kd1[:, t, q * 64:(q + 1) * 64], ps[:, 0:64], ACT.Copy), [tok])
            k = a(lambda e: e.activation(iw[:, t, :], ps[:, 64:72], ACT.Copy, scale=8.0 ** -0.5))
            ev.append(k)
            return k

        gemm_tok(72, xh, xl, xr, ev_ik)
        iw_ready = ev[-1]
        iq_ready = turn(tmp, 4, iqT, [riq])
        rt = rotary(kd1.rearrange("p t (g k) -> p t g k", k=64), 2, [ev[-1], riq])
        ik_ready = turn(kd1, 1, ikT, [rt])

        cur = gb[:, 1024:1536]
        rel = [A[:, 11264 + 512 * i:11776 + 512 * i] for i in range(4)]
        rel_free = [None] * 4
        n_rel = 0
        sc_done = {}
        for t in range(1, T):
            n = P * (t + 1)
            prev_t = None
            for hh in range(8):
                b = take()
                half = slice(64 * (hh % 2), 64 * (hh % 2) + 64)
                tok = mm(bank[b][:, 0:n], iqT[half, hh // 2, t * P:(t + 1) * P], ikT[half, 0, 0:n], True, True,
                         [bfree[b], iq_ready, ik_ready], True)
                i = n_rel % 4
                r = rel[i]
                t1 = a(lambda e, b=b, n=n, r=r: e.activation(r[:, 0:n], bank[b][:, 0:n], ACT.Relu, scale=0.125),
                       [tok, rel_free[i]])
                bfree[b] = t1
                s_ = bias[:, t, 0:n]
                w_ = iw[:, t, hh:hh + 1]
                if hh == 0:
                    prev_t = v(lambda e, s_=s_, r=r, n=n, w_=w_: e.tensor_scalar(s_, r[:, 0:n], w_, None, ALU.mult),
                               [t1, iw_ready])
                else:
                    prev_t = v(lambda e, s_=s_, r=r, n=n, w_=w_: e.scalar_tensor_tensor(
                        s_, r[:, 0:n], w_, s_, ALU.mult, ALU.add), [t1, prev_t])
                rel_free[i] = prev_t
                n_rel += 1
            sd = bias[:, t, t * P:(t + 1) * P]
            sc_done[t] = v(lambda e, sd=sd: e.tensor_tensor(sd, sd, CB, ALU.add), [prev_t])
        scored = sc_done[T - 1]
        m8 = sb("m8", [P, 8])
        bias_ready = [None] * T
        bias_ready[0] = v(lambda e: e.tensor_copy(bias[:, 0, 0:P], CB))

        def top_k():
            for t in range(1, T):
                n = P * (t + 1)
                s_ = bias[:, t, 0:n]
                w_ = cur[:, 0:n]
                k = sc_done[t]
                src = s_
                for r in range(16):
                    k = v(lambda e, src=src: e.max(m8[:, :], src), [k])
                    k = v(lambda e, src=src, w_=w_: e.match_replace(w_, m8[:, :], src, -3e38), [k])
                    src = w_
                    yield
                k = v(lambda e, s_=s_, w_=w_: e.tensor_tensor(s_, w_, s_, ALU.is_equal), [k])
                bias_ready[t] = v(lambda e, s_=s_: e.tensor_scalar(s_, s_, -BIG, None, ALU.mult), [k])

        background.append(top_k())
        ev = []

        def ev_kv(t, ps, tok):
            kv_ = kd[:, t, :].rearrange("p (g q k) -> p g q k", g=4, q=2)
            pk = ps[:, 0:256].rearrange("p (g k) -> p g k", g=4)
            for q in range(2):
                a(lambda e, q=q: e.activation(kv_[:, :, q, :], pk, ACT.Copy), [tok, scored])
            k = a(lambda e: e.activation(vt[:, t, :], ps[:, 256:512], ACT.Copy))
            ev.append(k)
            return k

        gemm_tok(512, xh, xl, xr, ev_kv, 2)
        v_ready = ev[-1]
        rk = rotary(kd.rearrange("p t (g k) -> p t g k", k=64), 8, [ev[-1], ik_ready, DVE.last()])
        for c in range(2):
            ev = []

            def ev_q(t, ps, tok):
                k = a(lambda e: e.activation(tmp[:, t, :], ps, ACT.Copy), [tok])
                ev.append(k)
                return k

            gemm_tok(512, xh, xl, xr, ev_q, 2)
            if c == 0:
                k_ready = turn(kd, 4, kT, [rk])
            rt = rotary(tmp.rearrange("p t (g k) -> p t g k", k=64), 8, [ev[-1], rk])
            q_ready = turn(tmp, 4, qT[:, 4 * c:4 * c + 4, :], [rt])
        drain()

        att = sb("att", [P, 3, 16, T])

        def attend(bufs, PTs, qv, kv_, vv_, nheads, grp, causal, ready_, emit_o):
            nmx, sm, rc = (att[:, q, 0:nheads, :] for q in range(3))
            N = nheads * T
            NB = len(bufs)
            bfr = [None] * NB
            st = [{} for _ in range(N)]
            pt_tok = {}
            pt_free = [None] * len(PTs)
            ob = [None]

            def scores_(i):
                hd, t = i // T, i % T
                half = slice(64 * (hd % 2), 64 * (hd % 2) + 64)
                n = P * (t + 1) if causal else SEQ
                b = take()
                pb = bufs[i % NB][:, 0:n]
                nm = nmx[:, hd, t:t + 1]
                tok = mm(bank[b][:, 0:n], qv[half, hd // 2, t * P:(t + 1) * P], kv_[half, hd // grp, 0:n], True, True,
                         [bfree[b]] + ready_, True)
                if causal:
                    k = v(lambda e: e.tensor_tensor_reduce(pb, bank[b][:, 0:n], bias[:, t, 0:n], -0.125, 3e38,
                                                           ALU.add, ALU.min, nm), [tok, bfr[i % NB], bias_ready[t]])
                else:
                    k = v(lambda e: e.tensor_scalar(pb, bank[b][:, 0:n], -0.125, 3e38, ALU.mult, ALU.min, accum_out=nm),
                          [tok, bfr[i % NB]])
                bfree[b] = k
                st[i]["e"] = a(lambda e: e.activation(pb, pb, ACT.Exp, bias=nm, scale=-1.0,
                                                      accum_out=sm[:, hd, t:t + 1]), [k])

            def norm_(i):
                hd, t = i // T, i % T
                n = P * (t + 1) if causal else SEQ
                pb = bufs[i % NB][:, 0:n]
                k = v(lambda e: e.reciprocal(rc[:, hd, t:t + 1], sm[:, hd, t:t + 1]), [st[i]["e"]])
                st[i]["n"] = v(lambda e: e.tensor_scalar(pb, pb, rc[:, hd, t:t + 1], None, ALU.mult), [k])

            def turn_(i):
                hd, t = i // T, i % T
                n = P * (t + 1) if causal else SEQ
                pb = bufs[i % NB]
                b = take()
                for kb in range(n // P):
                    tok = tr(bank[b][:, kb * P:(kb + 1) * P], pb[:, kb * P:(kb + 1) * P], ident,
                             [bfree[b], st[i]["n"]], mark=(kb == n // P - 1))
                bfr[i % NB] = tok
                d = PTs[hd % len(PTs)][:, 0:n // P, t * P:(t + 1) * P]
                s_ = bank[b][:, 0:n].rearrange("p (k q) -> p k q", q=P)
                after = [tok, pt_free[hd % len(PTs)]]
                if i % 2:
                    k = v(lambda e: e.tensor_copy(d, s_), after)
                else:
                    k = a(lambda e: e.activation(d, s_, ACT.Copy), after)
                bfree[b] = k
                pt_tok[i] = k

            def out_(hd):
                half = slice(64 * (hd % 2), 64 * (hd % 2) + 64)
                PT = PTs[hd % len(PTs)]
                if hd % 2 == 0:
                    ob[0] = take(True)
                o = bank[ob[0]]
                for kb in range(T):
                    c0 = kb * P if causal else 0
                    tok = mm(o[half, c0:SEQ], vv_(kb, hd // grp), PT[:, kb, c0:SEQ], kb == 0, kb == T - 1,
                             [pt_tok[hd * T + q] for q in range(T)] + [bfree[ob[0]] if hd % 2 == 0 else None],
                             mark=(kb == T - 1))
                pt_free[hd % len(PTs)] = tok
                if hd % 2:
                    held.discard(ob[0])
                    bfree[ob[0]] = emit_o(hd // 2, o[:, :], tok)

            for i in range(N + 5):
                if i < N:
                    scores_(i)
                if 0 <= i - 1 < N:
                    norm_(i - 1)
                if 0 <= i - 2 < N:
                    turn_(i - 2)
                if i >= 4 and (i - 4) % T == T - 1 and (i - 4) // T < nheads:
                    out_((i - 4) // T)
                yield

        oo = []

        def emit_a(j, ps, tok):
            k = split(ps, xh[:, j, :], xl[:, j, :], [tok])
            oo.append(k)
            return k

        assert k_ready and q_ready
        bufs = [gb[:, 512 * i:512 * (i + 1)] for i in range(4)]
        for _ in attend(bufs, [tmp, kd], qT, kT, lambda kb, gk: vt[:, kb, gk * 64:gk * 64 + 64], 16, 4, True,
                        [q_ready, k_ready, v_ready], emit_a):
            pass
        tg = ln_load(ln_mix_g[0], ln_mix_b[0])
        nt = residual_out(oo, [S0] * T)
        xr, ht = ln_finish(nt, tg, LNC["mg", 0], LNC["mb", 0])
        tg = ln_load(ln_mlp_g[0], ln_mlp_b[0])
        nt = mlp(xr, ht)
        wa2 = A[0:16, 2048:2560]
        ta2 = load_gb(wa2, b_w_a2[0], [PE.last(), tg])
        xr, ht = ln_finish(nt, tg, LNC["fg", 0], LNC["fb", 0])

        gq = A[:, 0:2048].rearrange("p (h s) -> p h s", h=4)
        gk_ = A[:, 2048:4096].rearrange("p (h s) -> p h s", h=4)
        gv = A[:, 4096:8192].rearrange("p (t n) -> p t n", t=T)
        bb = A[:, 8192:10240].rearrange("p (h s) -> p h s", h=4)
        wb = [A[:, 10240 + 512 * i:10752 + 512 * i].rearrange("p (h s) -> p h s", h=4) for i in range(4)]
        ATs = [x_.rearrange("p (h s) -> p h s", h=4) for x_ in (A[:, 12288:12800], A[:, 12800:13312], gb[:, 0:512],
                                                              gb[:, 512:1024])]
        ST = gb[:, 1024:2048].rearrange("p (h n) -> p h n", h=4)
        zz = A[:, 4096:6144].rearrange("p (h s) -> p h s", h=4)
        z2 = A[:, 6144:8192].rearrange("p (h s) -> p h s", h=4)
        alow = A[0:16, 12288:12800]
        al = []

        def ev_al(j, ps, tok):
            al.append(a(lambda e: e.activation(alow, ps, ACT.Copy), [tok]))
            return al[-1]

        gemm_T(xh, xl, xr, ev_al)
        zt = None
        for q in range(4):
            b = take()
            tok = mm(bank[b][:, :], wa2[:, q * P:(q + 1) * P], alow, True, True, [al[0], ta2, bfree[b]], True)
            bfree[b] = v(lambda e, b=b, q=q: e.tensor_scalar(zz[:, q, :], bank[b][:, :], BA[:, q:q + 1], None, ALU.add),
                         [tok, S0])
        zt = DVE.last()
        t1 = a(lambda e: e.activation(z2, zz, ACT.Abs), [zt])
        t1 = a(lambda e: e.activation(z2, z2, ACT.Exp, scale=-1.0), [t1])
        t1 = v(lambda e: e.tensor_scalar(z2, z2, 1.0, None, ALU.add), [t1])
        t1 = a(lambda e: e.activation(z2, z2, ACT.Ln), [t1])
        t1 = v(lambda e: e.scalar_tensor_tensor(zz, zz, 0.0, z2, ALU.min, ALU.subtract), [t1])
        for q in range(4):
            for c in range(4):
                b_ready = v(lambda e, q=q, c=c: e.tensor_tensor_scan(
                    bb[:, q, c * P:(c + 1) * P], ones, zz[:, q, c * P:(c + 1) * P], 0.0, ALU.mult, ALU.add), [t1])
        qk_r = []
        for n in range(4):
            def ev_qk(j, ps, tok, n=n):
                i = 2 * n + j
                dst = gq[:, i, :] if i < 4 else gk_[:, i - 4, :]
                sc = 128.0 ** -0.5 if i < 4 else 1.0
                qk_r.append(a(lambda e: e.activation(dst, ps, ACT.Copy, scale=sc), [tok]))
                return qk_r[-1]
            gemm_T(xh, xl, xr, ev_qk)
        ssq = sb("ssq", [P, T, 4])
        ebl = sb("ebl", [P, 4, 4])
        qk_done = qk_r[-1]
        gb_free = [POOL.last(), DVE.last()]
        at = [None] * 4

        def levels():
            units = [(c, n) for c in range(4) for n in range(8)]
            st = [{} for _ in units]
            wfree = [None] * 4

            def blk(x4, s):
                return x4.rearrange("p h (n two s) -> p h n two s", two=2, s=s)

            def sub_(i):
                c, n = units[i]
                if n == 7:
                    return
                s = LEVELS[n]
                cs = slice(c * P, (c + 1) * P)
                bv = blk(bb[:, :, cs], s)
                ref = bv[:, :, :, 0, s - 1:s].broadcast_to([P, 4, 64 // s, s])
                w_ = blk(wb[i % 4], s)
                k = [wfree[i % 4], b_ready]
                g(lambda e: e.tensor_tensor(w_[:, :, :, 1, :], bv[:, :, :, 1, :], ref, ALU.subtract), k)
                k = g(lambda e: e.tensor_tensor(w_[:, :, :, 0, :], ref, bv[:, :, :, 0, :], ALU.subtract), k)
                st[i]["e"] = a(lambda e: e.activation(wb[i % 4], wb[i % 4], ACT.Exp, scale=0.0625), [k])

            def mul_(i):
                c, n = units[i]
                if n == 7:
                    return
                s = LEVELS[n]
                cs = slice(c * P, (c + 1) * P)
                w_, q4, k4 = blk(wb[i % 4], s), blk(gq[:, :, cs], s), blk(gk_[:, :, cs], s)
                v(lambda e: e.tensor_tensor(w_[:, :, :, 1, :], w_[:, :, :, 1, :], q4[:, :, :, 1, :], ALU.mult),
                  [st[i]["e"], qk_done])
                st[i]["m"] = v(lambda e: e.tensor_tensor(w_[:, :, :, 0, :], w_[:, :, :, 0, :], k4[:, :, :, 0, :],
                                                         ALU.mult), [st[i]["e"], qk_done])

            def pe_(i):
                c, n = units[i]
                cs = slice(c * P, (c + 1) * P)
                b = take(True)
                for q in range(4):
                    l, r = (gk_[:, q, cs], gq[:, q, cs]) if n == 7 else (wb[i % 4][:, q, :], wb[i % 4][:, q, :])
                    tok = mm(bank[b][:, q * P:(q + 1) * P], l, r, True, True,
                             [bfree[b], qk_done if n == 7 else st[i]["m"]], q == 3)
                wfree[i % 4] = tok
                st[i]["p"], st[i]["b"] = tok, b

            def put_(i):
                c, n = units[i]
                b = st[i]["b"]
                AT = ATs[c]
                if n == 0:
                    at[c] = v(lambda e: e.memset(AT, 0.0), gb_free + [al[0], ta2, PE.last()])
                mk = LM[:, n * P:(n + 1) * P].unsqueeze(1).broadcast_to([P, 4, P])
                pv = bank[b][:, :].rearrange("p (h s) -> p h s", h=4)
                at[c] = bfree[b] = v(lambda e: e.copy_predicated(AT, mk, pv), [st[i]["p"], at[c]])
                held.discard(b)

            N = len(units)
            for i in range(N + 4):
                if i < N:
                    sub_(i)
                if 0 <= i - 2 < N:
                    mul_(i - 2)
                if 0 <= i - 3 < N:
                    pe_(i - 3)
                if 0 <= i - 4 < N:
                    put_(i - 4)
                yield

        background.append(levels())
        for n in range(2):
            def ev_v(t, ps, tok, n=n):
                vr = a(lambda e: e.activation(gv[:, t, n * 512:(n + 1) * 512], ps, ACT.Copy), [tok, b_ready])
                qk_r.append(vr)
                return vr
            gemm_tok(512, xh, xl, xr, ev_v, 2)
        drain()
        qkv = qk_r[-1]
        st_ready = None
        o_done = []
        lvl = [PE.last()]
        ch = [{} for _ in range(4)]

        def decays(c):
            cs = slice(c * P, (c + 1) * P)
            QE, KD = wb[c % 2], wb[2 + c % 2]
            prev_ = [lvl[0]] if c < 2 else [ch[c - 2]["o"], ch[c - 2]["s"], ch[c - 2]["sq"]]
            t1 = a(lambda e: e.activation(QE, bb[:, :, cs], ACT.Exp, scale=0.0625), prev_)
            ch[c]["q"] = v(lambda e: e.tensor_tensor(QE, QE, gq[:, :, cs], ALU.mult), [t1])
            bl = bb[:, :, c * P + 127:c * P + 128]
            t1 = v(lambda e: e.tensor_tensor(KD, bl.broadcast_to([P, 4, P]), bb[:, :, cs], ALU.subtract), prev_)
            t1 = a(lambda e: e.activation(KD, KD, ACT.Exp, scale=0.0625), [t1])
            ch[c]["l"] = a(lambda e: e.activation(ebl[:, c, :].unsqueeze(2), bl, ACT.Exp, scale=0.0625))
            t1 = v(lambda e: e.tensor_tensor(KD, KD, gk_[:, :, cs], ALU.mult), [t1])
            b = take()
            for q in range(4):
                tok = tr(bank[b][:, q * P:(q + 1) * P], KD[:, q, :], ident, [bfree[b], t1], q == 3)
            bfree[b] = ch[c]["k"] = a(lambda e: e.activation(
                KD, bank[b][:, :].rearrange("p (h s) -> p h s", h=4), ACT.Copy), [tok])

        decays(0)
        for c in range(4):
            if c < 3:
                decays(c + 1)
            QE, KD, AT = wb[c % 2], wb[2 + c % 2], ATs[c]
            sbk = []
            stok = None
            if c < 3:
                sbk = [take(True), take(True)]
                for q in range(4):
                    o = bank[sbk[q // 2]][:, (q % 2) * 256:(q % 2) * 256 + 256]
                    stok = mm_group(o, [(KD[:, q, :], gv[:, c, q * 256:(q + 1) * 256])],
                                    [bfree[sbk[q // 2]], ch[c]["k"], qkv])
            ch[c]["s"] = stok
            ob = [take(True), take(True)]
            for q in range(4):
                o = bank[ob[q // 2]][:, (q % 2) * 256:(q % 2) * 256 + 256]
                prs = [(AT[:, q, :], gv[:, c, q * 256:(q + 1) * 256])]
                if c:
                    prs.append((QE[:, q, :], ST[:, q, :]))
                otok = mm_group(o, prs, [bfree[ob[q // 2]], at[c], ch[c]["q"], st_ready, qkv])
            ch[c]["o"] = otok
            for q in range(4 if c < 3 else 0):
                o = bank[sbk[q // 2]][:, (q % 2) * 256:(q % 2) * 256 + 256]
                if c == 0:
                    st_ready = v(lambda e, q=q, o=o: e.tensor_copy(ST[:, q, :], o), [stok] + gb_free)
                else:
                    st_ready = v(lambda e, q=q, o=o, c=c: e.scalar_tensor_tensor(
                        ST[:, q, :], ST[:, q, :], ebl[:, c, q:q + 1], o, ALU.mult, ALU.add), [stok, otok, ch[c]["l"]])
                bfree[sbk[q // 2]] = st_ready
            held.difference_update(sbk)
            junk = QE.rearrange("p h s -> p (h s)")[:, 0:256]
            for q in range(4):
                o = bank[ob[q // 2]][:, (q % 2) * 256:(q % 2) * 256 + 256]
                dst = gv[:, c, q * 256:(q + 1) * 256]
                k1 = a(lambda e, dst=dst, o=o: e.activation(dst, o, ACT.Copy), [otok])
                k2 = a(lambda e, dst=dst, q=q, c=c, junk=junk: e.activation(
                    junk, dst, ACT.Square, accum_out=ssq[:, c, q:q + 1]), [k1, ACTE.last()])
                bfree[ob[q // 2]] = k1
            held.difference_update(ob)
            ch[c]["sq"] = k2
            o_done.append(k2)
        rs = small[:, 216:232]
        rr = rsqrt(rs, ssq[:, :, :].rearrange("p t h -> p (t h)"), 16, 1.0 / 256, 1e-6, [o_done[-1]])
        gnb = gb[:, 0:256]
        tg = load_gb(gnb, b_g_norm[0].partition_broadcast(P), [PE.last(), DVE.last(), ACTE.last()])
        yt = [None] * T
        for t in range(T):
            for q in range(4):
                o = gv[:, t, q * 256:(q + 1) * 256]
                yt[t] = v(lambda e, o=o, t=t, q=q: e.scalar_tensor_tensor(
                    o, o, rs[:, t * 4 + q:t * 4 + q + 1], gnb, ALU.mult, ALU.mult), [tg, rr])
        sg = [gb[:, 512:1024], gb[:, 1024:1536]]
        sgf = [None, None]
        sg_free = [PE.last(), DVE.last()]
        ns = [0]

        def gate_with(dst, ps, tok, after, silu):
            i = ns[0] % 2
            ns[0] += 1
            e_ = sg[i]
            k1 = a(lambda e: e.activation(e_, ps, ACT.Silu if silu else ACT.Sigmoid), [tok, sgf[i]] + sg_free)
            k5 = v(lambda e: e.tensor_tensor(dst, dst, e_, ALU.mult), [k1, after])
            sgf[i] = k5
            return k1, k5

        for n in range(2):
            def ev_r(t, ps, tok, n=n):
                k1, yt[t] = gate_with(gv[:, t, n * 512:(n + 1) * 512], ps, tok, yt[t], True)
                return k1
            gemm_tok(512, xh, xl, xr, ev_r)
        xr = to_T(gv, yt)
        tg = ln_load(ln_mix_g[1], ln_mix_b[1])
        nt = residual_out(xr, ht)
        xr, ht = ln_finish(nt, tg, LNC["mg", 1], LNC["mb", 1])

        def rms_sum(t, tok, junk):
            return a(lambda e: e.activation(junk, h[:, t, :], ACT.Square, accum_out=ssq[:, t, 0:1]), [tok, ACTE.last()])

        def rms_root(t, k):
            return rsqrt(ln_rs[:, t:t + 1], ssq[:, t, 0:1], 1, 1.0 / D, 1e-6, [k], 32 + t)

        def rms_row(t, dst, k):
            k = rms_root(t, k)
            return a(lambda e: e.activation(dst[:, t, :], h[:, t, :], ACT.Copy, scale=ln_rs[:, t:t + 1]), [k])

        xn = A[:, 6144:10240].rearrange("p (t n) -> p t n", t=T)
        tg = ln_load(ln_mlp_g[1], ln_mlp_b[1])
        xn_t = [None] * T
        sq_t = [None] * T

        gain_t = [None] * T

        def shift3(t):
            ht2[t] = v(lambda e: e.tensor_tensor(h[:, t, :], h[:, t, :], gb[:, D:2 * D], ALU.add), [gain_t[t]])
            sq_t[t] = rms_sum(t, ht2[t], A[:, 10240:11264])

        def finish3(t, tok):
            k = ln_rows(t, tok)
            e_ = v if t == T - 1 else g
            if t:
                shift3(t - 1)
            if t > 1:
                xn_t[t - 2] = rms_row(t - 2, xn, sq_t[t - 2])
            gain_t[t] = e_(lambda e: e.tensor_tensor(h[:, t, :], h[:, t, :], gb[:, 0:D], ALU.mult), [k, tg])
            return gain_t[t]

        ht2 = [None] * T
        nt = mlp(xr, ht, finish3)
        ht = ht2
        md = DVE.last()
        t1 = v(lambda e: e.tensor_scalar(CS1, SC1, 1.0, None, ALU.add), [md])
        cs1 = v(lambda e: e.tensor_tensor(CS1, CS1, GM, ALU.mult), [t1])
        t1 = v(lambda e: e.tensor_scalar(CS2, SC2, 1.0, None, ALU.add), [md])
        cs2 = v(lambda e: e.tensor_tensor(CS2, CS2, GF, ALU.mult), [t1])
        shift3(T - 1)
        for t in (T - 2, T - 1):
            xn_t[t] = rms_row(t, xn, sq_t[t])
        xr = to_T(xn, xn_t, CS1, SH1, cs1)

        ym = A[:, 0:2048].rearrange("p (t n) -> p t n", t=T)
        qT2 = A[:, 2048:4096].rearrange("p (j s) -> p j s", j=4)
        kT2 = A[:, 4096:5120].rearrange("p (j s) -> p j s", j=2)
        v2 = A[:, 5120:5632].rearrange("p (t n) -> p t n", t=T)
        mqk = A[:, 5632:9728].rearrange("p (j s) -> p j s", j=8)
        vx = A[:, 9728:11808].rearrange("p (t h n) -> p t h n", t=T, h=4)
        tm = A[:, 9728:11776].rearrange("p (t n) -> p t n", t=T)
        tm2 = A[:, 0:2048].rearrange("p (t n) -> p t n", t=T)
        kd2 = A[:, 11808:12832].rearrange("p (t n) -> p t n", t=T)
        gqn, gkn = col(320, 64), col(384, 64)
        load_gb(gqn, q_norm_g_2[0].partition_broadcast(P), [md])
        tgq = load_gb(gkn, k_norm_g_2[0].partition_broadcast(P), ())
        s32 = sb("s32", [P, 32])

        def norm_rope(x4, w4, nh, gain, after, done):
            k = v(lambda e: e.tensor_tensor(w4.rearrange("p t g k -> p (t g k)"), x4.rearrange("p t g k -> p (t g k)"),
                                            x4.rearrange("p t g k -> p (t g k)"), ALU.mult), after)
            k = v(lambda e: e.tensor_reduce(s32[:, 0:T * nh].rearrange("p (t g) -> p t g", t=T), w4, AX, ALU.add), [k])
            yield
            k = rsqrt(s32[:, 0:T * nh], s32[:, 0:T * nh], T * nh, 1.0 / 64, 1e-6, [k])
            yield
            rsb = s32[:, 0:T * nh].rearrange("p (t g) -> p t g", t=T).unsqueeze(3).broadcast_to([P, T, nh, 64])
            k = v(lambda e: e.tensor_tensor(x4, x4, rsb, ALU.mult), [k])
            yield
            gn = gain.unsqueeze(1).broadcast_to([P, T * nh, 64])
            x3 = x4.rearrange("p t g k -> p (t g) k")
            k = v(lambda e: e.tensor_tensor(x3, x3, gn, ALU.mult), [k, tgq])
            for t in range(T):
                yield
                rcv = C[:, C_RC + t * 64:C_RC + t * 64 + 64].unsqueeze(1).broadcast_to([P, nh, 64])
                rsv_ = C[:, C_RS + t * 64:C_RS + t * 64 + 64].rearrange("p (r a k) -> p r a k", r=2, a=2)
                xv = x4[:, t].rearrange("p g (r a k) -> p g r a k", r=2, a=2)
                wv = w4[:, t].rearrange("p g (r a k) -> p g r a k", r=2, a=2)
                for q in range(2):
                    sv = rsv_[:, :, q, :].unsqueeze(1).broadcast_to([P, nh, 2, 16])
                    k1 = v(lambda e, wv=wv, xv=xv, sv=sv, q=q: e.tensor_tensor(wv[:, :, :, q, :], xv[:, :, :, 1 - q, :], sv,
                                                                             ALU.mult), [k])
                k2 = v(lambda e, t=t, rcv=rcv: e.tensor_tensor(x4[:, t], x4[:, t], rcv, ALU.mult), [k1])
                k3 = v(lambda e, t=t: e.tensor_tensor(x4[:, t], x4[:, t], w4[:, t], ALU.add), [k1, k2])
            done.append(k3)

        ev = []

        def ev_q2(t, ps, tok):
            ev.append(a(lambda e: e.activation(tm[:, t, :], ps, ACT.Copy), [tok]))
            return ev[-1]

        gemm_tok(512, xh, xl, xr, ev_q2)
        qd, kdn = [], []
        background.append(norm_rope(tm.rearrange("p t (g k) -> p t g k", k=64), tm2.rearrange("p t (g k) -> p t g k", k=64),
                                    8, gqn, [ev[-1]], qd))
        evk = []

        def ev_k2(t, ps, tok):
            kk = kd2[:, t, :].rearrange("p (g q k) -> p g q k", g=2, q=2)
            pk = ps[:, 0:128].rearrange("p (g k) -> p g k", g=2)
            for q in range(2):
                a(lambda e, q=q: e.activation(kk[:, :, q, :], pk, ACT.Copy), [tok])
            evk.append(a(lambda e: e.activation(v2[:, t, :], ps[:, 128:256], ACT.Copy), [tok]))
            return evk[-1]

        gemm_tok(256, xh, xl, xr, ev_k2, 1)

        def rope_k():
            while not qd:
                yield
            yield from norm_rope(kd2.rearrange("p t (g k) -> p t g k", k=64),
                                 A[:, 0:1024].rearrange("p (t g k) -> p t g k", t=T, k=64), 4, gkn, [evk[-1], qd[0]], kdn)

        background.append(rope_k())
        pads = [gb[:, 0:516], gb[:, 514:1030]]
        kz = v(lambda e: e.memset(gb[:, 0:1030], 0.0), [ht[-1]])
        pfr = [kz, kz]
        cvt = []
        for n in range(4):
            def ev_c(j, ps, tok, n=n):
                i = 2 * n + j
                pad, y_ = pads[i % 2], mqk[:, i, :]
                k0 = a(lambda e: e.activation(pad[:, 2:514], ps, ACT.Copy), [tok, pfr[i % 2]])
                k = v(lambda e: e.tensor_scalar(y_, pad[:, 0:512], CW[:, 0, i:i + 1], CVB[:, i:i + 1], ALU.mult, ALU.add),
                      [k0, S0])
                for w in range(1, 5):
                    k = v(lambda e, w=w: e.scalar_tensor_tensor(y_, pad[:, w:w + 512], CW[:, w, i:i + 1], y_,
                                                               ALU.mult, ALU.add), [k])
                pfr[i % 2] = k
                cvt.append(a(lambda e: e.activation(y_, y_, ACT.Silu), [k]))
                return k0
            gemm_T(xh, xl, xr, ev_c, 2)
        drain()
        qk_ready = cvt[-1]
        q2r = turn(tm, 4, qT2, qd)
        k2r = turn(kd2, 2, kT2, kdn)
        v2r = evk[-1]
        gg = sb("gg", [P, T, 16])
        g2_ = sb("g2_", [P, T, 16])
        ev = []

        def ev_v2(t, ps, tok):
            ev.append(a(lambda e: e.activation(vx[:, t, :, 0:128], ps.rearrange("p (h n) -> p h n", h=4), ACT.Copy),
                        [tok, q2r]))
            return ev[-1]

        kz = v(lambda e: e.memset(vx[:, :, :, 128:130], 1.0), [PE.last()])
        gemm_tok(512, xh, xl, xr, ev_v2)
        vx_ready = ev[-1]
        ev = []

        def ev_g(t, ps, tok):
            ev.append(v(lambda e: e.tensor_tensor(gg[:, t, :], ps, GB, ALU.add), [tok, S0]))
            return ev[-1]

        gemm_tok(16, xh, xl, xr, ev_g)
        gr = ev[-1]
        core0 = [DVE.last(), ACTE.last(), PE.last()]
        rawf = raw[:, :, :].rearrange("p a n -> p (a n)")
        STm = rawf[:, 2048:4096].rearrange("p (b s) -> p b s", b=T)
        PTs = [rawf[:, 0:2048].rearrange("p (b s) -> p b s", b=T), gb[:, 0:2048].rearrange("p (b s) -> p b s", b=T)]
        PB2 = [rawf[:, 4096 + 512 * i:4608 + 512 * i] for i in range(3)]
        Dd = rawf[:, 5632:6144]
        Db = [A[:, 11808:12320], A[:, 12320:12832]]
        acol = sb("acol", [P, 2, T, 4])
        ecol = sb("ecol", [P, 2, T, 4])
        den = sb("den", [P, 2, 2, 2])
        Mr = [A[32 * d:32 * d + 4, 12832:13344] for d in range(2)]
        SCL = 128.0 ** -0.5
        hm = [None]

        def memory():
            k = a(lambda e: e.activation(g2_[:, :, :], gg[:, :, :], ACT.Abs), [gr])
            k = a(lambda e: e.activation(g2_[:, :, :], g2_[:, :, :], ACT.Exp, scale=-1.0), [k])
            k = v(lambda e: e.tensor_scalar(g2_[:, :, :], g2_[:, :, :], 1.0, None, ALU.add), [k])
            k = a(lambda e: e.activation(g2_[:, :, :], g2_[:, :, :], ACT.Ln), [k])
            lf = v(lambda e: e.scalar_tensor_tensor(g2_[:, :, :], gg[:, :, :], 0.0, g2_[:, :, :], ALU.min, ALU.subtract),
                   [k])
            yield
            mrdy = [None, None]
            cols = [None, None]

            def gates(d):
                p = slice(32 * d, 32 * d + 4)
                ir, fr, onerow = STm[p, 0, :], STm[p, 1, :], STm[p, 2, :]
                rv = (lambda ap: ap) if d == 0 else (lambda ap: ap[:, ::-1])
                k1r = v(lambda e: e.memset(onerow, 1.0), core0)
                bi, bf = take(), take()
                for t in range(T):
                    tok = tr(bank[bi][0:4, t * P:(t + 1) * P], gg[:, t, 8 * d:8 * d + 4], ident, [bfree[bi], lf], t == T - 1)
                for t in range(T):
                    tok2 = tr(bank[bf][0:4, t * P:(t + 1) * P], g2_[:, t, 8 * d + 4:8 * d + 8], ident, [bfree[bf], lf],
                              t == T - 1)
                ki = a(lambda e: e.activation(ir, bank[bi][0:4, :], ACT.Copy), [tok] + core0)
                kf = a(lambda e: e.activation(Mr[d], bank[bf][0:4, :], ACT.Copy), [tok2] + core0)
                bfree[bi], bfree[bf] = ki, kf
                k = v(lambda e: e.tensor_tensor_scan(rv(fr), onerow, rv(Mr[d]), 0.0, ALU.mult, ALU.add), [kf, k1r])
                ka = v(lambda e: e.tensor_tensor(ir, ir, fr, ALU.subtract), [k, ki])
                km = v(lambda e: e.tensor_tensor_scan(rv(Mr[d]), rv(ir), rv(ir), 0.0, ALU.max, ALU.max), [ka])
                mrdy[d] = km
                kn = v(lambda e: e.tensor_tensor(fr, fr, Mr[d], ALU.add), [km])
                yield
                b = take()
                for t in range(T):
                    tr(bank[b][:, t * 4:t * 4 + 4], ir[:, t * P:(t + 1) * P], ident[p, p], [bfree[b], ka])
                    tok = tr(bank[b][:, 16 + t * 4:20 + t * 4], fr[:, t * P:(t + 1) * P], ident[p, p], [kn], t == T - 1)
                a(lambda e: e.activation(acol[:, d, :, :], bank[b][:, 0:16].rearrange("p (t h) -> p t h", t=T), ACT.Copy),
                  [tok])
                cols[d] = bfree[b] = a(lambda e: e.activation(
                    ecol[:, d, :, :], bank[b][:, 16:32].rearrange("p (t h) -> p t h", t=T), ACT.Exp, scale=-1.0), [tok])

            yield from gates(0)
            yield from gates(1)
            bMs = {}
            st_free = cols[1]
            dd_free = None
            dfree = [cols[1]] * 2
            nd = 0
            jobs = [(hh, d) for hh in range(4) for d in range(2)]

            def start(m):
                hh, d = jobs[m]
                bM = take(True)
                sel = ident[32 * d:32 * d + 4, 32 * d + hh:32 * d + hh + 1].broadcast_to([4, P])
                mtok = mm(bank[bM][:, :], sel, Mr[d], True, True, [bfree[bM], mrdy[d]], True)
                mk = CBT if d == 0 else CB
                for s in range(T):
                    c = slice(s * P, (s + 1) * P)
                    k = v(lambda e, s=s, c=c: e.scalar_tensor_tensor(Dd[:, c], bank[bM][:, c], acol[:, d, s, hh:hh + 1], mk,
                                                                     ALU.subtract, ALU.min, reverse0=True),
                          [mtok, cols[1], dd_free] + core0)
                bMs[m] = (bM, a(lambda e: e.activation(Dd, Dd, ACT.Exp), [k]))

            start(0)
            for m, (hh, d) in enumerate(jobs):
                bM, dk = bMs[m]
                for s in range(T):
                    yield
                    c0, c1_ = (s * P, SEQ) if d == 0 else (0, (s + 1) * P)
                    n = c1_ - c0
                    o0, o1 = ((s + 1) * P, SEQ) if d == 0 else (0, s * P)
                    b = take()
                    tok = mm(bank[b][:, 0:n], mqk[:, 4 + hh, s * P:(s + 1) * P], mqk[:, hh, c0:c1_], True, True,
                             [bfree[b], qk_ready], True)
                    if o1 > o0:
                        i = nd % 2
                        nd += 1
                        dv = Db[i][:, 0:o1 - o0]
                        k = a(lambda e, dv=dv, o0=o0, o1=o1, bM=bM, d=d, s=s, hh=hh: e.activation(
                            dv, bank[bM][:, o0:o1], ACT.Exp, bias=acol[:, d, s, hh:hh + 1], scale=-1.0), [dk, dfree[i]])
                        bfree[bM] = k
                        k = v(lambda e, b=b, dv=dv, o0=o0, o1=o1, c0=c0, s=s: e.scalar_tensor_tensor(
                            STm[:, s, o0:o1], bank[b][:, o0 - c0:o1 - c0], SCL, dv, ALU.mult, ALU.mult), [tok, k, st_free])
                        dfree[i] = k
                    c = slice(s * P, (s + 1) * P)
                    k = v(lambda e, b=b, c=c, c0=c0, s=s: e.scalar_tensor_tensor(
                        STm[:, s, c], bank[b][:, s * P - c0:(s + 1) * P - c0], SCL, Dd[:, c], ALU.mult, ALU.mult),
                        [tok, dk, st_free])
                    bfree[b] = k
                    sr = k
                held.discard(bM)
                dd_free = sr
                yield
                if m + 1 < len(jobs):
                    start(m + 1)
                for tt in range(2):
                    yield
                    b = take()
                    for t in (2 * tt, 2 * tt + 1):
                        src = range(0, t + 1) if d == 0 else range(t, T)
                        o = (t % 2) * 256
                        tok = mm_group(bank[b][:, o:o + 130], [(STm[:, q, t * P:(t + 1) * P], vx[:, q, hh, :]) for q in src],
                                       [bfree[b], sr, vx_ready, kz])
                    dn = den[:, m % 2, tt, :]
                    k = a(lambda e, dn=dn, b=b: e.activation(dn, bank[b][:, 128:512:256], ACT.Abs), [tok, DVE.last()])
                    k = v(lambda e, dn=dn, d=d, tt=tt, hh=hh: e.tensor_tensor(dn, dn, ecol[:, d, 2 * tt:2 * tt + 2, hh],
                                                                           ALU.max), [k, cols[1]])
                    k = v(lambda e, dn=dn: e.reciprocal(dn, dn), [k])
                    for t in (2 * tt, 2 * tt + 1):
                        o = (t % 2) * 256
                        yv = ym[:, t, hh * P:(hh + 1) * P]
                        dc = dn[:, t % 2:t % 2 + 1]
                        if d == 0:
                            hm[0] = v(lambda e, yv=yv, b=b, dc=dc, o=o: e.tensor_scalar(
                                yv, bank[b][:, o:o + P], dc, None, ALU.mult), [k])
                        else:
                            hm[0] = v(lambda e, yv=yv, b=b, dc=dc, o=o: e.scalar_tensor_tensor(
                                yv, bank[b][:, o:o + P], dc, yv, ALU.mult, ALU.add), [k])
                    bfree[b] = hm[0]
                st_free = PE.last()

        y2 = []

        def emit_2(j, ps, tok):
            y2.append(split(ps, uh[:, 0, j, :], ul[:, 0, j, :], [tok]))
            return y2[-1]

        heads = attend(PB2, PTs, qT2, kT2, lambda kb, gk: v2[:, kb, gk * 64:gk * 64 + 64], 8, 4, False,
                       [q2r, k2r, v2r] + core0, emit_2)
        mem = memory()
        live = [heads, mem, mem]
        turn_no = 0
        while live:
            gen = live[turn_no % len(live)]
            turn_no += 1
            if next(gen, background) is background:
                live = [x_ for x_ in live if x_ is not gen]
                if live:
                    live = live[:1]
        release([DVE.last(), ACTE.last(), PE.last()])
        k = None
        for t in range(T):
            for hh in range(4):
                k = a(lambda e, t=t, hh=hh: e.activation(gb[:, 0:128], ym[:, t, hh * P:(hh + 1) * P], ACT.Square,
                                                        accum_out=ssq[:, t, hh:hh + 1]), [hm[0], PE.last(), ACTE.last()])
        k = rsqrt(rs, ssq[:, :, :].rearrange("p t h -> p (t h)"), 16, 1.0 / 128, 1e-6, [k])
        gmb = A[:, 8192:8704]
        tg = load_gb(gmb, mlstm_norm_g_2[0].partition_broadcast(P), [DVE.last(), ACTE.last(), PE.last()])
        yt = [None] * T
        for t in range(T):
            for hh in range(4):
                yv = ym[:, t, hh * P:(hh + 1) * P]
                yt[t] = v(lambda e, yv=yv, t=t, hh=hh: e.scalar_tensor_tensor(
                    yv, yv, rs[:, 4 * t + hh:4 * t + hh + 1], gmb[:, hh * P:(hh + 1) * P], ALU.mult, ALU.mult), [tg, k])

        def ev_o(t, ps, tok):
            k1, yt[t] = gate_with(ym[:, t, :], ps, tok, yt[t], False)
            return k1

        gemm_tok(512, xh, xl, xr, ev_o)
        G1, G2 = A[:, 4096:5120], A[:, 5120:6144]
        for gc, G in ((GC1, G1), (GC2, G2)):
            for c in range(2):
                b = take()
                for j in range(4):
                    kk = 4 * c + j
                    tok = mm(bank[b][:, j * P:(j + 1) * P], gc[:, kk:kk + 1].broadcast_to([P, P]), ident, True, True,
                             [bfree[b], md], j == 3)
                G_ready = bfree[b] = a(lambda e, b=b, G=G, c=c: e.activation(G[:, c * 512:(c + 1) * 512], bank[b][:, :],
                                                                          ACT.Copy), [tok])
        yr = [y2[-1]] * 4
        for j in range(4):
            b = take()
            for t in range(T):
                tok = tr(bank[b][:, t * P:(t + 1) * P], ym[:, t, j * P:(j + 1) * P], ident, [bfree[b], yt[t]], t == T - 1)
            bfree[b] = split(bank[b][:, :], uh[:, 1, j, :], ul[:, 1, j, :], [tok])
            yr.append(bfree[b])
        fg = gb[:, 0:1024]
        tfg = load_gb(fg, final_norm_g_2.partition_broadcast(P), [DVE.last(), ACTE.last(), PE.last()])
        nt = [None] * T
        junk = A[:, 6144:7168]
        mo = [A[:, 7168:7680], A[:, 7680:8192]]
        mof = [DVE.last()] * 2
        xo = A[:, 0:4096].rearrange("p (t n) -> p t n", t=T)
        sq_t = [None] * T

        def ev_w(t, c, ps, tok):
            m = mo[c]
            k0 = mof[c] = v(lambda e: e.tensor_tensor(m, ps, G1[:, c * 512:(c + 1) * 512], ALU.mult), [tok, G_ready, mof[c]])
            hv = h[:, t, c * 512:(c + 1) * 512]
            ht[t] = mof[c] = v(lambda e: e.tensor_tensor(hv, hv, m, ALU.add), [k0, ht[t]])
            if c:
                sq_t[t] = rms_sum(t, ht[t], junk)
                if t:
                    nt[t - 1] = rms_row(t - 1, xo, sq_t[t - 1])
            return k0

        gemm_pair(uh[:, :, :, :].rearrange("p a f s -> p (a f) s"), ul[:, :, :, :].rearrange("p a f s -> p (a f) s"),
                  yr, ev_w)
        nt[T - 1] = rms_row(T - 1, xo, sq_t[T - 1])
        xr = to_T(xo, nt, CS2, SH2)
        facc = A[:, 8192:12288].rearrange("p (t n) -> p t n", t=T)
        ub = A[:, 0:4096].rearrange("p (i s) -> p i s", i=8)
        uf = [PE.last()] * 8
        ft = [None] * T
        urdy = {}
        nu = [0]
        u_free[0] = u_free[1] = PE.last()
        LASTF = len(FG) - 1

        def finish4(t):
            k = rms_root(t, sq_t[t])
            k = v(lambda e: e.scalar_tensor_tensor(facc[:, t, :], h[:, t, :], ln_rs[:, t:t + 1], fg, ALU.mult, ALU.mult),
                  [k, tfg, ht[t]])
            SP.put([k], lambda e: e.dma_start(out[0, t * P:(t + 1) * P, :], facc[:, t, :]).then_inc(s_out, 16), mark=False)

        def ev_down(n, t, c, ps, tok):
            fv = facc[:, t, c * 512:(c + 1) * 512]
            hv = h[:, t, c * 512:(c + 1) * 512]
            g2v = G2[:, c * 512:(c + 1) * 512]
            if n == LASTF:
                k0 = v(lambda e: e.tensor_tensor(fv, ps, g2v, ALU.mult), [tok, ht[t]])
                ht[t] = v(lambda e: e.tensor_tensor(hv, hv, fv, ALU.add), [k0])
                if c:
                    sq_t[t] = rms_sum(t, ht[t], junk)
                    if t:
                        finish4(t - 1)
                return k0
            if n == 0:
                ft[t] = v(lambda e: e.tensor_copy(fv, ps), [tok])
            else:
                ft[t] = v(lambda e: e.tensor_tensor(fv, fv, ps, ALU.add), [tok, ft[t]])
            k0 = ft[t]
            if n == LASTF - 1:
                k = v(lambda e: e.tensor_tensor(fv, fv, g2v, ALU.mult), [k0])
                ht[t] = v(lambda e: e.tensor_tensor(hv, hv, fv, ALU.add), [k, ht[t]])
            return k0

        for n in range(len(FG) + 1):
            if n < len(FG):
                for q in range(FG[n][1] // 2):
                    gt = {}

                    def ev_gate(j, ps, tok):
                        i = 2 * (nu[0] % 4) + j
                        gx = ub[:, i, :]
                        gt[j] = a(lambda e: e.activation(gx, ps, ACT.Silu), [tok, uf[i]])
                        return gt[j]

                    def ev_up(j, ps, tok, q=q, n=n):
                        i = 2 * (nu[0] % 4) + j
                        gx = ub[:, i, :]
                        k1 = v(lambda e: e.tensor_tensor(gx, gx, ps, ALU.mult), [tok, gt[j]])
                        fi = 2 * q + j
                        uf[i] = urdy[n] = split(gx, uh[:, n % 2, fi, :], ul[:, n % 2, fi, :], [k1, u_free[n % 2]])
                        return k1

                    gemm_T(xh, xl, xr, ev_gate)
                    gemm_T(xh, xl, xr, ev_up)
                    nu[0] += 1
            if n > 0:
                down(n - 1, FG[n - 1][1], urdy[n - 1], ev_down, n == len(FG))
        finish4(T - 1)
        SP.put([(s_out, 16 * T)], lambda e: None, mark=False)
        assert used[0] == len(chunks), (used[0], len(chunks))

        block = ctx.enter_context(nc.Block())

        @block.sync
        def _(e):
            for f in SP.todo:
                f(e)

        @block.gpsimd
        def _(e):
            for f in POOL.todo:
                f(e)

        @block.scalar
        def _(e):
            for f in ACTE.todo:
                f(e)

        @block.tensor
        def _(e):
            for f in PE.todo:
                f(e)

        @block.vector
        def _(e):
            for f in DVE.todo:
                f(e)


NAMES = ["x", "positions", "a_w_in", "a_w_o", "b_w_in", "b_w_a2", "b_b_a", "b_g_norm", "b_w_o", "ln_mix_g", "ln_mix_b",
         "mlp_w_up", "mlp_w_down", "ln_mlp_g", "ln_mlp_b", "c_2", "w_ada_2", "b_ada_2", "norm_mix_g_2", "w_in_2",
         "q_norm_g_2", "k_norm_g_2", "conv_w_2", "conv_b_2", "gate_b_2", "mlstm_norm_g_2", "w_out_2", "norm_ffn_g_2",
         "w_gate_2", "w_up_2", "w_down_2", "final_norm_g_2"]


def packed(inputs):
    def by_part(a):
        return np.asarray(a).reshape(-1, P).T

    pad = np.zeros((P, 4), np.float32)
    cols = [by_part(inputs["b_b_a"]), pad, by_part(inputs["c_2"]), by_part(inputs["norm_mix_g_2"]),
            by_part(inputs["norm_ffn_g_2"]), by_part(inputs["conv_w_2"]), by_part(inputs["conv_b_2"])]
    cols += [by_part(inputs[n][i]) for n in ("ln_mix_g", "ln_mix_b", "ln_mlp_g", "ln_mlp_b") for i in range(2)]
    cols.append(by_part(inputs["b_ada_2"]))
    return np.ascontiguousarray(np.concatenate(cols, 1)), np.ascontiguousarray(by_part(inputs["positions"]))


def kernel(**inputs):
    import concourse.bacc as bacc
    from concourse.bass_utils import run_bass_kernel_spmd

    nc = bacc.Bacc("TRN2", target_bir_lowering=False, num_devices=1)
    arrays, args = {}, []
    given = {n: np.ascontiguousarray(inputs[n]) for n in NAMES}
    given["cst"], given["lmask"] = constants()
    given["cols"], given["posn"] = packed(inputs)
    for name, arr in given.items():
        arrays["in_" + name] = arr
        args.append(nc.dram_tensor("in_" + name, arr.shape, mybir.dt.from_np(arr.dtype), kind="ExternalInput").ap())
    out = nc.dram_tensor("out_0", (1, SEQ, D), F, kind="ExternalOutput").ap()
    program(nc, *args, out)
    r = run_bass_kernel_spmd(nc, [arrays], core_ids=[0])
    return r.results[0]["out_0"]
```

```python
from contextlib import ExitStack

import numpy as np
import concourse.bass as bass
from concourse import mybir

F = mybir.dt.float32
R = mybir.dt.float32r
I32 = mybir.dt.int32
U8 = mybir.dt.uint8
ALU = mybir.AluOpType
ACT = mybir.ActivationFunctionType
AX = mybir.AxisListType.X

P = 128
T = 4
SEQ = 512
D = 1024
ALPHA = 4.0 ** 0.25
BIG = 1e30
NRAW = 3
NHL = 2
CH = 2048
LEVELS = [64, 32, 16, 8, 4, 2, 1]

C_ID, C_CB, C_CBT, C_ONE, C_INV, C_RC, C_RS = 0, 128, 256, 384, 512, 520, 776
C_END = 1032


def constants():
    c = np.zeros((P, C_END), np.float32)
    i = np.arange(P)
    c[:, C_ID:C_ID + P] = np.eye(P)
    c[:, C_CB:C_CB + P] = np.where(i[None, :] > i[:, None], -BIG, 0.0)
    c[:, C_CBT:C_CBT + P] = np.where(i[None, :] < i[:, None], -BIG, 0.0)
    c[:, C_ONE:C_ONE + P] = 1.0
    c[:, C_INV:C_INV + 8] = np.float32(500000.0) ** (-np.arange(0, 16, 2, dtype=np.float32) / np.float32(16))
    inv = np.float32(10000.0) ** (-np.arange(0, 32, 2, dtype=np.float32) / np.float32(32))
    for t in range(T):
        tok = t * P + i
        ar = (tok // 64).astype(np.float32)[:, None] * inv[None, :]
        ac = (tok % 64).astype(np.float32)[:, None] * inv[None, :]
        c[:, C_RC + t * 64:C_RC + t * 64 + 64] = np.concatenate([np.cos(ar), np.cos(ar), np.cos(ac), np.cos(ac)], 1)
        c[:, C_RS + t * 64:C_RS + t * 64 + 64] = np.concatenate([-np.sin(ar), np.sin(ar), -np.sin(ac), np.sin(ac)], 1)
    m = np.zeros((P, 8, P), np.float32)
    for n, s in enumerate(LEVELS):
        j, k = i[:, None], i[None, :]
        m[:, n, :] = (j // (2 * s) == k // (2 * s)) & (j % (2 * s) < s) & (k % (2 * s) >= s)
    m[:, 7, :] = np.eye(P)
    return c, m.reshape(P, 8 * P)


class Line:

    def __init__(self, sem):
        self.sem, self.n, self.todo, self.seen = sem, 0, [], {}

    def put(self, after, fn, mark=True):
        for tok in after:
            if tok is None:
                continue
            sem, v = tok
            if self.seen.get(sem.name, 0) < v:
                self.seen[sem.name] = v
                self.todo.append(lambda e, s=sem, v=v: e.wait_ge(s, v))
        if not mark:
            self.todo.append(fn)
            return None
        self.n += 1
        self.todo.append(lambda e: fn(e).then_inc(self.sem, 1))
        return (self.sem, self.n)

    def last(self):
        return (self.sem, self.n)


def program(nc, x, positions, a_w_in, a_w_o, b_w_in, b_w_a2, b_b_a, b_g_norm, b_w_o, ln_mix_g, ln_mix_b,
            mlp_w_up, mlp_w_down, ln_mlp_g, ln_mlp_b, c_2, w_ada_2, b_ada_2, norm_mix_g_2, w_in_2, q_norm_g_2,
            k_norm_g_2, conv_w_2, conv_b_2, gate_b_2, mlstm_norm_g_2, w_out_2, norm_ffn_g_2, w_gate_2, w_up_2,
            w_down_2, final_norm_g_2, cst, lmask, cols, posn, out):
    ctx = ExitStack()
    with ctx:
        def sb(name, shape, dt=F):
            return ctx.enter_context(nc.sbuf_tensor(name, shape, dt))

        def sem(name):
            return ctx.enter_context(nc.semaphore(name))

        h = sb("h", [P, T, D])
        xh = sb("xh", [P, 8, SEQ], R)
        xl = sb("xl", [P, 8, SEQ], R)
        raw = sb("raw", [P, NRAW, CH])
        wh = sb("wh", [P, NHL, CH], R)
        wl = sb("wl", [P, NHL, CH], R)
        uh = sb("uh", [P, 2, 4, SEQ], R)
        ul = sb("ul", [P, 2, 4, SEQ], R)
        C = sb("C", [P, C_END])
        LM = sb("LM", [P, 8 * P], U8)
        gb = sb("gb", [P, 2048])
        A = sb("A", [P, 13344])
        small = sb("small", [P, 648])
        stats = sb("stats", [P, T, 2, 6])
        mv = sb("mv", [P, T, 2])
        rsv = sb("rsv", [P, 64])
        rsy = sb("rsy", [P, 64])
        rsa = sb("rsa", [P, 64])
        posi = sb("posi", [P, T], I32)
        bank = [ctx.enter_context(nc.psum_tensor(f"bank{i}", [P, 512], F)) for i in range(8)]

        PE, DVE, ACTE, POOL, SP = (Line(sem(n)) for n in ("s_pe", "s_dve", "s_act", "s_pool", "s_sp"))
        s_raw = [sem(f"s_raw{i}") for i in range(NRAW)]
        s_in = sem("s_in")
        s_gb = sem("s_gb")
        s_acc = sem("s_acc")
        s_out = sem("s_out")

        ident = C[:, C_ID:C_ID + P]
        ones = C[:, C_ONE:C_ONE + P]
        CB = C[:, C_CB:C_CB + P]
        CBT = C[:, C_CBT:C_CBT + P]
        bfree = [None] * 8
        bnext = [0]

        held = set()

        def take(hold=False):
            while bnext[0] in held:
                bnext[0] = (bnext[0] + 1) % 8
            b = bnext[0]
            bnext[0] = (b + 1) % 8
            if hold:
                held.add(b)
            return b

        def v(fn, after=()):
            return DVE.put(after, fn)

        def a(fn, after=()):
            return ACTE.put(after, fn)

        def g(fn, after=()):
            return POOL.put(after, fn)

        def mm(out_, l, r, start, stop, after=(), mark=False):
            return PE.put(after, lambda e: e.matmul(out_, l, r, start=start, stop=stop), mark)

        def mm_group(out_, pairs, after=(), mark=True):
            tok = None
            for i, (l, r) in enumerate(pairs):
                tok = mm(out_, l, r, i == 0, i == len(pairs) - 1, after if i == 0 else (), mark and i == len(pairs) - 1)
            return tok

        def tr(out_, in_, idn, after=(), mark=False):
            return PE.put(after, lambda e: e.transpose(out_, in_, idn), mark)

        n_in = [0]

        def load(dst, src):
            n_in[0] += 1
            SP.put((), lambda e: e.dma_start(dst, src).then_inc(s_in, 16), mark=False)

        def col(n, w):
            return small[:, n:n + w]

        s_h = [sem(f"s_h{t}") for t in range(T)]
        SP.put((), lambda e: e.dma_start(C[:, :], cst).then_inc(s_h[0], 16), mark=False)
        for t in range(T):
            SP.put((), lambda e, t=t: e.dma_start(h[:, t, :], x[0, t * P:(t + 1) * P, :]).then_inc(s_h[t], 16), mark=False)
        H0 = [(s_h[t], 16 if t else 32) for t in range(T)]
        early_weights = len(SP.todo)
        load(posi[:, :], posn)
        load(A[:, 12288:13312], lmask)
        load(col(0, 80), cols[:, 0:80])
        load(col(256, 64), cols[:, 80:144])
        BADA, GNC = col(576, 48), col(624, 8)
        load(GNC, cols[:, 192:200])
        MNC = col(640, 4)
        load(MNC, cols[:, 200:204])
        load(BADA, cols[:, 144:192])
        BA, CC, GM, GF, CVB = col(0, 4), col(8, 8), col(16, 8), col(24, 8), col(72, 8)
        CW = col(32, 40).rearrange("p (w k) -> p w k", k=8)
        GB = col(80, 16)
        load(GB, gate_b_2[0].partition_broadcast(P))
        SH1, SC1, SH2, SC2 = col(96, 8), col(104, 8), col(112, 8), col(120, 8)
        GC1, GC2 = col(240, 8), col(248, 8)
        LNC = {(n, i): col(256 + 16 * j + 8 * i, 8) for j, n in enumerate(("mg", "mb", "fg", "fb")) for i in range(2)}
        CS1, CS2 = col(128, 8), col(136, 8)
        S0 = (s_in, 16 * n_in[0])


        chunks = []

        def plan(w, r0, nk, c0, nc_):
            chunks.append((w[r0:r0 + nk * P, c0:c0 + nc_].rearrange("(k p) n -> p k n", p=P), nk, nc_))

        def plan_tok(w, c0, n):
            if n <= 256:
                plan(w, 0, 8, c0, n)
            else:
                plan(w, 0, 4, c0, n)
                plan(w, 512, 4, c0, n)

        def plan_pair(w):
            for r0 in (0, 512):
                for c0 in (0, 512):
                    plan(w, r0, 4, c0, 512)

        wa, wb, w2 = a_w_in[0], b_w_in[0], w_in_2[0]

        ada_of = {}

        def plan_ada(n):
            ada_of[len(chunks)] = n
            plan(w_ada_2[0], (n % 8) * P, 1, (n // 8) * 2048, 2048)

        def plan_mlp(i):
            for n in range(9):
                if n < 8:
                    for q in range(2):
                        plan(mlp_w_up[i], 0, 8, n * 512 + q * 256, 256)
                        if i == 0:
                            plan_ada(2 * n + q)
                        elif q == 0:
                            plan_ada(16 + n)
                if n > 0:
                    for c in range(2):
                        plan(mlp_w_down[i], (n - 1) * 512, 4, c * 512, 512)

        plan_tok(wa, 1536, 512)
        plan(wa, 0, 8, 2048, 72)
        plan_tok(wa, 1024, 512)
        plan_tok(wa, 0, 512)
        plan_tok(wa, 512, 512)
        plan_pair(a_w_o[0])
        plan_mlp(0)
        plan(wb, 0, 8, 3072, 16)
        for n in range(4):
            plan(wb, 0, 8, n * 256, 256)
        for n in range(4):
            plan_tok(wb, 1024 + 512 * n, 512)
        plan_pair(b_w_o[0])
        plan_mlp(1)
        plan_tok(w2, 0, 512)
        plan_tok(w2, 512, 256)
        plan(w2, 0, 8, 2816, 16)
        plan_tok(w2, 1792, 512)
        for n in range(4):
            plan(w2, 0, 8, 768 + n * 256, 256)
        plan_tok(w2, 2304, 512)
        core2 = [len(chunks)]
        plan_pair(w_out_2[0])
        FG = [(0, 2), (2, 4), (6, 4), (10, 4), (14, 4), (18, 4)]
        for n in range(len(FG) + 1):
            if n < len(FG):
                f0, nf = FG[n]
                for q in range(nf // 2):
                    plan(w_gate_2[0], 0, 8, (f0 + 2 * q) * P, 256)
                    plan(w_up_2[0], 0, 8, (f0 + 2 * q) * P, 256)
            if n > 0:
                f0, nf = FG[n - 1]
                for c in range(2):
                    plan(w_down_2[0], f0 * P, nf, c * 512, 512)

        used = [0]
        prepped = [0]
        loaded = [0]
        raw_free = [None] * NRAW
        hl_free = [None] * NHL
        ready = {}
        waiting = []
        limit = [core2[0]]

        def fetch(i):
            if i >= len(chunks):
                return
            if i >= limit[0]:
                waiting.append(i)
                return
            src, nk, ncol = chunks[i]
            s = i % NRAW
            dst = raw[:, s, 0:nk * ncol].rearrange("p (k n) -> p k n", k=nk)
            SP.put([raw_free[s]], lambda e: e.dma_start(dst, src).then_inc(s_raw[s], 16), mark=False)

        def release(after):
            limit[0] = len(chunks)
            for s in range(NRAW):
                raw_free[s] = None
            SP.put(after, lambda e: None, mark=False)
            for i in list(waiting):
                fetch(i)

        def landed(i):
            return (s_raw[i % NRAW], 16 * (i // NRAW + 1))

        slot_of = {}
        nsplit = [0]

        def split_chunk(i, later=False):
            if i in ada_of:
                ada(i, ada_of[i])
                return
            src, nk, ncol = chunks[i]
            r, n = i % NRAW, nk * ncol
            s = nsplit[0] % NHL
            nsplit[0] += 1
            slot_of[i] = s
            t1 = a(lambda e: e.activation(wh[:, s, 0:n], raw[:, r, 0:n], ACT.Copy), [landed(i), hl_free[s]])

            def low():
                t2 = v(lambda e: e.tensor_tensor(wl[:, s, 0:n], raw[:, r, 0:n], wh[:, s, 0:n].bitcast(F), ALU.subtract),
                       [landed(i), t1])
                raw_free[r] = t2
                ready[i] = t2
                fetch(i + NRAW)

            if later:
                return low
            low()

        def prep_ahead():
            i = prepped[0]
            assert i == used[0] and i not in ada_of
            if i >= limit[0]:
                return lambda: None
            prepped[0] += 1
            return split_chunk(i, True)

        def next_chunk(look=True):
            i = used[0]
            while i in ada_of:
                i += 1
            used[0] = i + 1
            ahead = i + 1 if look else i
            while ahead in ada_of:
                ahead += 1
            while prepped[0] <= ahead and prepped[0] < len(chunks):
                if prepped[0] < limit[0]:
                    split_chunk(prepped[0])
                elif prepped[0] == i or limit[0] == len(chunks):
                    raise AssertionError
                else:
                    break
                prepped[0] += 1
            src, nk, ncol = chunks[i]
            s = slot_of[i]
            H = wh[:, s, 0:nk * ncol].rearrange("p (k n) -> p k n", k=nk)
            L = wl[:, s, 0:nk * ncol].rearrange("p (k n) -> p k n", k=nk)
            return H, L, ready[i], s, nk, ncol

        cond = small[:, 232:240]
        acc = A[:, 4096:6144]
        s_k = [None]
        cond_ready = []
        mod_cols = [SH1, SC1, GC1, SH2, SC2, GC2]

        def ada(i, n):
            r, kt = n // 8, n % 8
            rw = raw[:, i % NRAW, :]
            if kt == 0:
                k = v(lambda e: e.tensor_scalar(acc, rw, cond[:, 0:1], None, ALU.mult), [landed(i), PE.last(), cond_ready[0]])
            else:
                k = v(lambda e: e.scalar_tensor_tensor(acc, rw, cond[:, kt:kt + 1], acc, ALU.mult, ALU.add),
                      [landed(i), s_k[0]])
            s_k[0] = raw_free[i % NRAW] = k
            fetch(i + NRAW)
            if kt == 7:
                owed.append((r, k))

        owed = []

        def ada_sum():
            while owed:
                r, k = owed.pop()
                b = take()
                for j in range(16):
                    tok = mm(bank[b][:, j:j + 1], acc[:, j * P:(j + 1) * P], ones[:, 0:1], True, True, [bfree[b], k], j == 15)
                for q in range(2):
                    dst, bc = mod_cols[2 * r + q], BADA[:, 16 * r + 8 * q:16 * r + 8 * q + 8]
                    bfree[b] = v(lambda e, dst=dst, q=q, bc=bc: e.tensor_tensor(dst, bank[b][:, 8 * q:8 * q + 8], bc,
                                                                               ALU.add), [tok])

        done = len(SP.todo)
        for i in range(NRAW):
            fetch(i)
        SP.todo[early_weights:] = SP.todo[done:done + 2] + SP.todo[early_weights:done] + SP.todo[done + 2:]

        background = []

        def tick(n=1):
            for _ in range(n):
                for job in list(background):
                    if next(job, background) is background:
                        background.remove(job)

        def drain():
            while background:
                tick()

        def as_list(r):
            return r if isinstance(r, list) else [r] * 8

        def gemm_tok(n, hi, lo, ready_x, evac, ticks=0):
            bs = [take(True) for _ in range(T)]
            k0 = 0
            rx = as_list(ready_x)
            while k0 < 8:
                H, L, rw, s, nk, ncol = next_chunk()
                assert ncol == n, (ncol, n)
                for t in range(T):
                    for k in range(nk):
                        kk = k0 + k
                        X, Y = hi[:, kk, t * P:(t + 1) * P], lo[:, kk, t * P:(t + 1) * P]
                        o = bank[bs[t]][:, 0:n]
                        first, end = kk == 0, kk == 7
                        mm(o, X, H[:, k, :], first, False, [rw, rx[kk], bfree[bs[t]]] if first else [rw, rx[kk]])
                        mm(o, X, L[:, k, :], False, False)
                        tok = mm(o, Y, H[:, k, :], False, end, mark=(k == nk - 1))
                    if end:
                        bfree[bs[t]] = evac(t, bank[bs[t]][:, 0:n], tok)
                        held.discard(bs[t])
                    tick(ticks)
                hl_free[s] = PE.last()
                k0 += nk

        def panel_pair(X, Y, nk, out_of, first, after, evac):
            W = [next_chunk(), next_chunk(False)]
            assert W[0][4] == nk
            late = None
            for t in range(T):
                toks = []
                for c in range(2):
                    H, L, rw = W[c][0:3]
                    b = out_of(t, c)
                    for k in range(nk):
                        o = bank[b][:, :]
                        mm(o, X(k, t), H[:, k, :], first and k == 0, False, [rw, bfree[b]] + after(k) if k == 0 else after(k))
                        mm(o, X(k, t), L[:, k, :], False, False)
                        tok = mm(o, Y(k, t), H[:, k, :], False, k == nk - 1, mark=(k == nk - 1))
                    toks.append((b, tok))
                if t == T - 1:
                    for c in range(2):
                        hl_free[W[c][3]] = PE.last()
                    if prepped[0] < len(chunks):
                        late = prep_ahead()
                for c, (b, tok) in enumerate(toks):
                    bfree[b] = evac(t, c, bank[b][:, :], tok)
                    held.discard(b)
            if late:
                late()

        def gemm_pair(hi, lo, ready_x, evac):
            bs = [[take(True) for c in range(2)] for t in range(T)]
            rx = as_list(ready_x)
            for c in range(2):
                H, L, rw, s, nk, ncol = next_chunk()
                for t in range(T):
                    for k in range(nk):
                        X, Y = hi[:, k, t * P:(t + 1) * P], lo[:, k, t * P:(t + 1) * P]
                        o = bank[bs[t][c]][:, :]
                        mm(o, X, H[:, k, :], k == 0, False, [rw, rx[k], bfree[bs[t][c]]] if k == 0 else [rx[k]])
                        mm(o, X, L[:, k, :], False, False)
                        mm(o, Y, H[:, k, :], False, False, mark=(k == nk - 1 and t == T - 1))
                hl_free[s] = PE.last()
            panel_pair(lambda k, t: hi[:, 4 + k, t * P:(t + 1) * P], lambda k, t: lo[:, 4 + k, t * P:(t + 1) * P], 4,
                       lambda t, c: bs[t][c], False, lambda k: [rx[4 + k]], evac)

        def gemm_T(hi, lo, ready_x, evac, ticks=0, at_end=None):
            H, L, rw, s, nk, ncol = next_chunk()
            assert nk == 8
            rx = as_list(ready_x)
            for j in range(max(1, ncol // P)):
                w = min(P, ncol)
                b = take()
                o = bank[b][0:w, :]
                for k in range(8):
                    c = slice(j * P, j * P + w)
                    mm(o, H[:, k, c], hi[:, k, :], k == 0, False, [rw, rx[k], bfree[b]] if k == 0 else [rx[k]])
                    mm(o, L[:, k, c], hi[:, k, :], False, False)
                    tok = mm(o, H[:, k, c], lo[:, k, :], False, k == 7, mark=(k == 7))
                if (j + 1) * P >= ncol:
                    hl_free[s] = PE.last()
                    if at_end:
                        at_end()
                bfree[b] = evac(j, o, tok)
                tick(ticks)

        def split(src, dh, dl, after):
            t1 = a(lambda e: e.activation(dh, src, ACT.Copy), after)
            return v(lambda e: e.tensor_tensor(dl, src, dh.bitcast(F), ALU.subtract), [t1])

        mid = [A[:, 12288:12800], A[:, 12800:13312]]

        def to_T(src, toks, scale=None, shift=None, cols_ready=None):
            bs = [take(True) for _ in range(8)]
            out_ = []
            mf = [None, None]
            for t in range(T):
                for k in range(8):
                    tok = tr(bank[bs[k]][:, t * P:(t + 1) * P], src[:, t, k * P:(k + 1) * P], ident,
                             [bfree[bs[k]], toks[t]], mark=(t == T - 1))
                    if t < T - 1:
                        continue
                    ps = bank[bs[k]][:, :]
                    if scale is None:
                        t2 = bfree[bs[k]] = split(ps, xh[:, k, :], xl[:, k, :], [tok])
                    elif shift is None:
                        t1 = a(lambda e, ps=ps, k=k: e.activation(xh[:, k, :], ps, ACT.Copy, scale=scale[:, k:k + 1]), [tok])
                        t2 = bfree[bs[k]] = v(lambda e, ps=ps, k=k: e.scalar_tensor_tensor(
                            xl[:, k, :], ps, scale[:, k:k + 1], xh[:, k, :].bitcast(F), ALU.mult, ALU.subtract), [t1])
                    else:
                        m = mid[k % 2]
                        t1 = a(lambda e, ps=ps, m=m, k=k: e.activation(m, ps, ACT.Identity, bias=shift[:, k:k + 1],
                                                                       scale=scale[:, k:k + 1]), [tok, mf[k % 2], cols_ready])
                        bfree[bs[k]] = t1
                        if k % 2:
                            t2 = v(lambda e, m=m, k=k: e.tensor_copy(xh[:, k, :], m), [t1])
                        else:
                            t2 = a(lambda e, m=m, k=k: e.activation(xh[:, k, :], m, ACT.Copy), [t1])
                        t2 = mf[k % 2] = v(lambda e, m=m, k=k: e.tensor_tensor(xl[:, k, :], m, xh[:, k, :].bitcast(F),
                                                                               ALU.subtract), [t1, t2])
                    out_.append(t2)
            held.difference_update(bs)
            return out_

        def rsqrt(dst, src, n, scale, eps, after, c0=0):
            vv, yy, aa = rsv[:, c0:c0 + n], rsy[:, c0:c0 + n], rsa[:, c0:c0 + n]
            k = v(lambda e: e.tensor_scalar(vv, src, scale, eps, ALU.mult, ALU.add), after)
            k = v(lambda e: e.tensor_scalar(yy.bitcast(I32), vv.bitcast(I32), -0.5, 1597463007.0, ALU.mult, ALU.add), [k])
            for q in range(3):
                if n == 1:
                    k = v(lambda e: e.scalar_tensor_tensor(aa, yy, yy, vv, ALU.mult, ALU.mult), [k])
                else:
                    k = v(lambda e: e.tensor_tensor(aa, yy, yy, ALU.mult), [k])
                    k = v(lambda e: e.tensor_tensor(aa, aa, vv, ALU.mult), [k])
                k = v(lambda e: e.tensor_scalar(aa, aa, -0.5, 1.5, ALU.mult, ALU.add), [k])
                k = v(lambda e, q=q: e.tensor_tensor(dst if q == 2 else yy, yy, aa, ALU.mult), [k])
            return k

        ngb = [0]

        def load_gb(dst, src, after):
            ngb[0] += 1
            POOL.put(after, lambda e: e.dma_start(dst, src).then_inc(s_gb, 16), mark=False)
            return (s_gb, 16 * ngb[0])

        ln_rs = small[:, 144:148]
        mrs = small[:, 632:636]

        def ln_stats(t, q, tok):
            return v(lambda e: e.bn_stats(stats[:, t, q, :], h[:, t, q * 512:(q + 1) * 512]), [tok])

        def ln_rows(t, tok):
            ts = v(lambda e: e.bn_aggr(mv[:, t, :], stats[:, t, :, :].rearrange("p a b -> p (a b)")), [tok])
            k = rsqrt(ln_rs[:, t:t + 1], mv[:, t, 1:2], 1, 1.0, 1e-5, [ts], 32 + t)
            k = v(lambda e: e.scalar_tensor_tensor(mrs[:, t:t + 1], mv[:, t, 0:1], -1.0, ln_rs[:, t:t + 1],
                                                   ALU.mult, ALU.mult), [k])
            return a(lambda e: e.activation(h[:, t, :], h[:, t, :], ACT.Identity, bias=mrs[:, t:t + 1],
                                            scale=ln_rs[:, t:t + 1]), [k, tok])

        def ln_load(gd, bd):
            free = [POOL.last()]
            load_gb(gb[:, 0:D], gd.partition_broadcast(P), free + [DVE.last(), ACTE.last(), PE.last()])
            return load_gb(gb[:, D:2 * D], bd.partition_broadcast(P), ())

        def ln_finish(nt, tg, gain, shift):
            xr_ = to_T(h, nt, gain, shift)
            read = PE.last()
            toks = []
            for t in range(T):
                k = g(lambda e, t=t: e.tensor_tensor(h[:, t, :], h[:, t, :], gb[:, 0:D], ALU.mult), [tg, read, nt[t]])
                toks.append(g(lambda e, t=t: e.tensor_tensor(h[:, t, :], h[:, t, :], gb[:, D:2 * D], ALU.add), [k]))
            return xr_, toks

        def residual_out(hi_ready, ht):
            toks = [None] * T

            def evac(t, c, ps, tok):
                hv = h[:, t, c * 512:(c + 1) * 512]
                k = v(lambda e: e.scalar_tensor_tensor(hv, hv, ALPHA, ps, ALU.mult, ALU.add), [tok, ht[t]])
                toks[t] = ln_stats(t, c, k)
                if c:
                    toks[t] = ln_rows(t, toks[t])
                return k

            gemm_pair(xh, xl, hi_ready, evac)
            return toks

        u_free = [None, None]

        def down(n, nf, u_ready, evac, last=False):
            bsel = n % 2
            if last:
                panel_pair(lambda f, t: uh[:, bsel, f, t * P:(t + 1) * P], lambda f, t: ul[:, bsel, f, t * P:(t + 1) * P], nf,
                           lambda t, c: take(), True, lambda f: [u_ready], lambda t, c, ps, tok: evac(n, t, c, ps, tok))
                ada_sum()
                u_free[bsel] = PE.last()
                return
            for c in range(2):
                H, L, rw, s, nk, ncol = next_chunk()
                assert nk == nf
                for t in range(T):
                    b = take()
                    for f in range(nf):
                        X = uh[:, bsel, f, t * P:(t + 1) * P]
                        Y = ul[:, bsel, f, t * P:(t + 1) * P]
                        mm(bank[b][:, :], X, H[:, f, :], f == 0, False, [rw, u_ready, bfree[b]] if f == 0 else ())
                        mm(bank[b][:, :], X, L[:, f, :], False, False)
                        tok = mm(bank[b][:, :], Y, H[:, f, :], False, f == nf - 1, mark=(f == nf - 1))
                    bfree[b] = evac(n, t, c, bank[b][:, :], tok)
                hl_free[s] = PE.last()
            ada_sum()
            u_free[bsel] = PE.last()

        def mlp(x_ready, ht, finish=None):
            toks = [None] * T
            urdy = {}
            rb = A[:, 0:2048].rearrange("p (n s) -> p n s", n=4)
            prev = [None] * 4

            def evac_down(n, t, c, ps, tok):
                hv = h[:, t, c * 512:(c + 1) * 512]
                if n == 0:
                    toks[t] = v(lambda e: e.scalar_tensor_tensor(hv, hv, ALPHA, ps, ALU.mult, ALU.add), [tok, ht[t]])
                else:
                    toks[t] = v(lambda e: e.tensor_tensor(hv, hv, ps, ALU.add), [tok, toks[t]])
                k = toks[t]
                if n == 7:
                    toks[t] = ln_stats(t, c, k)
                    if c:
                        toks[t] = (finish or ln_rows)(t, toks[t])
                return k

            for n in range(9):
                if n < 8:
                    for q in range(2):
                        def evac(j, ps, tok, q=q, n=n):
                            i = 2 * q + j
                            r = rb[:, i, :]
                            t1 = a(lambda e: e.activation(r, ps, ACT.Relu), [tok, prev[i]])
                            t2 = v(lambda e: e.tensor_tensor(r, r, r, ALU.mult), [t1])
                            prev[i] = urdy[n] = split(r, uh[:, n % 2, i, :], ul[:, n % 2, i, :], [t2, u_free[n % 2]])
                            return t1
                        gemm_T(xh, xl, x_ready, evac)
                if n > 0:
                    down(n - 1, 4, urdy[n - 1], evac_down, n == 8)
            return toks

        xr = to_T(h, H0)
        for i in range(2):
            split_chunk(i)
        prepped[0] = 2
        v(lambda e: e.tensor_copy(LM[:, :], A[:, 12288:13312]), [S0])
        pf = small[:, 148:152]
        ang = small[:, 152:184]
        nn = small[:, 184:216]
        rot = sb("rot", [P, 2, T, 16])
        cosd, sind = rot[:, 0, :, :], rot[:, 1, :, :]
        t0 = v(lambda e: e.tensor_copy(pf, posi[:, :]), [S0] + H0)
        a3 = ang.rearrange("p (t k) -> p t k", t=T)
        n3 = nn.rearrange("p (t k) -> p t k", t=T)
        t0 = v(lambda e: e.tensor_tensor(a3, pf.unsqueeze(2).broadcast_to([P, T, 8]),
                                         C[:, C_INV:C_INV + 8].unsqueeze(1).broadcast_to([P, T, 8]), ALU.mult), [t0])
        MAGIC = 12582912.0
        t0 = v(lambda e: e.tensor_scalar(nn, ang, float(np.float32(1 / (2 * np.pi))), MAGIC, ALU.mult, ALU.add), [t0])
        t0 = v(lambda e: e.tensor_scalar(nn, nn, MAGIC, None, ALU.subtract), [t0])
        c1 = 6.28125
        c2 = float(np.float32(np.round((2 * np.pi - c1) * 2 ** 21) / 2 ** 21))
        c3 = float(np.float32(2 * np.pi - c1 - c2))
        for cc in (c1, c2, c3):
            t0 = v(lambda e, cc=cc: e.scalar_tensor_tensor(ang, nn, -cc, ang, ALU.mult, ALU.add), [t0])
        t0 = v(lambda e: e.tensor_scalar(ang, ang, 3.1415925, -3.1415925, ALU.min, ALU.max), [t0])
        t1 = a(lambda e: e.activation(sind[:, :, 8:16], a3, ACT.Sin), [t0])
        t2 = a(lambda e: e.activation(n3, a3, ACT.Sin, scale=0.5), [t0, t1])
        t3 = v(lambda e: e.tensor_tensor(nn, nn, nn, ALU.mult), [t2])
        t3 = v(lambda e: e.tensor_scalar(cosd[:, :, 0:8], n3, -2.0, 1.0, ALU.mult, ALU.add), [t3])
        t3 = v(lambda e: e.tensor_scalar(cosd[:, :, 8:16], n3, -2.0, 1.0, ALU.mult, ALU.add), [t3])
        rot_ready = v(lambda e: e.tensor_scalar(sind[:, :, 0:8], sind[:, :, 8:16], -1.0, None, ALU.mult), [t1])

        t1 = a(lambda e: e.activation(cond, CC, ACT.Exp, scale=-1.0), [S0])
        t1 = v(lambda e: e.tensor_scalar(cond, cond, 1.0, None, ALU.add), [t1])
        t1 = v(lambda e: e.reciprocal(cond, cond), [t1])
        cond_ready.append(v(lambda e: e.tensor_tensor(cond, cond, CC, ALU.mult), [t1]))

        def rotary(view, nh, after, v=v):
            ta = gb[:, 0:nh * 16 * T].rearrange("p (t g k) -> p t g k", t=T, k=16)
            tb = gb[:, 512:512 + nh * 16 * T].rearrange("p (t g k) -> p t g k", t=T, k=16)
            cv = cosd.unsqueeze(2).broadcast_to([P, T, nh, 16])
            sv = sind.unsqueeze(2).broadcast_to([P, T, nh, 16])
            x1 = v(lambda e: e.tensor_tensor(ta, view[:, :, :, 0:16], cv, ALU.mult), after)
            x2 = v(lambda e: e.tensor_tensor(tb[:, :, :, 0:8], view[:, :, :, 8:16], sv[:, :, :, 0:8], ALU.mult), after)
            x3 = v(lambda e: e.tensor_tensor(tb[:, :, :, 8:16], view[:, :, :, 0:8], sv[:, :, :, 8:16], ALU.mult), after)
            return v(lambda e: e.tensor_tensor(view[:, :, :, 0:16], ta, tb, ALU.add), [x1, x2, x3])

        def turn(view, nt, dst, after, scale=None):
            last = []
            for j in range(nt):
                b = take()
                for t in range(T):
                    tok = tr(bank[b][:, t * P:(t + 1) * P], view[:, t, j * P:(j + 1) * P], ident,
                             [bfree[b]] + list(after), mark=(t == T - 1))
                d = dst[:, j, :]
                bfree[b] = a(lambda e, b=b, d=d: e.activation(d, bank[b][:, :], ACT.Copy), [tok])
                last.append(bfree[b])
            return last[-1]


        qT = A[:, 0:4096].rearrange("p (j s) -> p j s", j=8)
        iqT = A[:, 0:2048].rearrange("p (j s) -> p j s", j=4)
        ikT = A[:, 2048:2560].rearrange("p (j s) -> p j s", j=1)
        kT = A[:, 4096:6144].rearrange("p (j s) -> p j s", j=4)
        vt = A[:, 6144:7168].rearrange("p (t n) -> p t n", t=T)
        bias = A[:, 7168:9216].rearrange("p (t n) -> p t n", t=T)
        tmp = A[:, 9216:11264].rearrange("p (t n) -> p t n", t=T)
        kd = A[:, 11264:13312].rearrange("p (t n) -> p t n", t=T)
        iw = sb("iw", [P, T, 8])

        ev = []

        def ev_tmp(t, ps, tok):
            k = a(lambda e: e.activation(tmp[:, t, :], ps, ACT.Copy), [tok])
            ev.append(k)
            return k

        gemm_tok(512, xh, xl, xr, ev_tmp)
        riq = rotary(tmp.rearrange("p t (g k) -> p t g k", k=64), 8, [rot_ready, ev[-1]])
        kd1 = gb[:, 1536:2048].rearrange("p (t n) -> p t n", t=T)
        ev = []

        ikf = A[0:72, 11264:11776]

        def ev_ik(j, ps, tok):
            ev.append(a(lambda e: e.activation(ikf, ps, ACT.Copy), [tok]))
            return ev[-1]

        gemm_T(xh, xl, xr, ev_ik)
        b = take()
        for t in range(T):
            tok = tr(bank[b][:, t * 72:(t + 1) * 72], ikf[:, t * P:(t + 1) * P], ident[0:72, 0:72], [bfree[b], ev[-1]], t == T - 1)
        pi = bank[b][:, 0:72 * T].rearrange("p (t n) -> p t n", t=T)
        for q in range(2):
            a(lambda e, q=q: e.activation(kd1[:, :, q * 64:(q + 1) * 64], pi[:, :, 0:64], ACT.Copy), [tok])
        iw_ready = bfree[b] = a(lambda e: e.activation(iw[:, :, :], pi[:, :, 64:72], ACT.Copy, scale=8.0 ** -0.5))
        ev.append(iw_ready)
        iq_ready = turn(tmp, 4, iqT, [riq])
        rt = rotary(kd1.rearrange("p t (g k) -> p t g k", k=64), 2, [ev[-1], riq])
        ik_ready = turn(kd1, 1, ikT, [rt])

        cur = gb[:, 1024:1536]
        rel = [A[:, 11264 + 512 * i:11776 + 512 * i] for i in range(4)]
        rel_free = [None] * 4
        n_rel = 0
        sc_done = {}
        for t in range(1, T):
            n = P * (t + 1)
            prev_t = None
            for hh in range(8):
                b = take()
                half = slice(64 * (hh % 2), 64 * (hh % 2) + 64)
                tok = mm(bank[b][:, 0:n], iqT[half, hh // 2, t * P:(t + 1) * P], ikT[half, 0, 0:n], True, True,
                         [bfree[b], iq_ready, ik_ready], True)
                i = n_rel % 4
                r = rel[i]
                t1 = a(lambda e, b=b, n=n, r=r: e.activation(r[:, 0:n], bank[b][:, 0:n], ACT.Relu, scale=0.125),
                       [tok, rel_free[i]])
                bfree[b] = t1
                s_ = bias[:, t, 0:n]
                w_ = iw[:, t, hh:hh + 1]
                if hh == 0:
                    prev_t = v(lambda e, s_=s_, r=r, n=n, w_=w_: e.tensor_scalar(s_, r[:, 0:n], w_, None, ALU.mult),
                               [t1, iw_ready])
                else:
                    prev_t = v(lambda e, s_=s_, r=r, n=n, w_=w_: e.scalar_tensor_tensor(
                        s_, r[:, 0:n], w_, s_, ALU.mult, ALU.add), [t1, prev_t])
                rel_free[i] = prev_t
                n_rel += 1
            sd = bias[:, t, t * P:(t + 1) * P]
            sc_done[t] = v(lambda e, sd=sd: e.tensor_tensor(sd, sd, CB, ALU.add), [prev_t])
        scored = sc_done[T - 1]
        m8 = sb("m8", [P, 8])
        bias_ready = [None] * T
        bias_ready[0] = v(lambda e: e.tensor_copy(bias[:, 0, 0:P], CB))

        def top_k():
            for t in range(1, T):
                n = P * (t + 1)
                s_ = bias[:, t, 0:n]
                w_ = cur[:, 0:n]
                k = sc_done[t]
                src = s_
                for r in range(16):
                    k = v(lambda e, src=src: e.max(m8[:, :], src), [k])
                    k = v(lambda e, src=src, w_=w_: e.match_replace(w_, m8[:, :], src, -3e38), [k])
                    src = w_
                    yield
                k = v(lambda e, s_=s_, w_=w_: e.tensor_tensor(s_, w_, s_, ALU.is_equal), [k])
                bias_ready[t] = v(lambda e, s_=s_: e.tensor_scalar(s_, s_, -BIG, None, ALU.mult), [k])

        background.append(top_k())
        ev = []

        def ev_kv(t, ps, tok):
            kv_ = kd[:, t, :].rearrange("p (g q k) -> p g q k", g=4, q=2)
            pk = ps[:, 0:256].rearrange("p (g k) -> p g k", g=4)
            for q in range(2):
                a(lambda e, q=q: e.activation(kv_[:, :, q, :], pk, ACT.Copy), [tok, scored])
            k = a(lambda e: e.activation(vt[:, t, :], ps[:, 256:512], ACT.Copy))
            ev.append(k)
            return k

        gemm_tok(512, xh, xl, xr, ev_kv, 3)
        v_ready = ev[-1]
        rk = rotary(kd.rearrange("p t (g k) -> p t g k", k=64), 8, [ev[-1], ik_ready, DVE.last()], g)
        q_turned, k_turned = [], []

        def turns(jobs):
            for src, dst, tok, out_ in jobs:
                for _ in range(3):
                    yield
                out_.append(turn(src, 4, dst, [tok]))

        background.append(turns([(kd, kT, rk, k_turned)]))
        for c in range(2):
            ev = []

            def ev_q(t, ps, tok):
                k = a(lambda e: e.activation(tmp[:, t, :], ps, ACT.Copy), [tok])
                ev.append(k)
                return k

            gemm_tok(512, xh, xl, xr, ev_q, 2)
            assert not c or len(q_turned) == 1
            rt = rotary(tmp.rearrange("p t (g k) -> p t g k", k=64), 8, [ev[-1], rk, rt], v if c else g)
            if c == 0:
                background.append(turns([(tmp, qT[:, 0:4, :], rt, q_turned)]))
        drain()

        att = sb("att", [P, 3, 16, T])

        def attend(bufs, PTs, qv, kv_, vv_, nheads, grp, causal, ready_, emit_o, pt_ready=()):
            nmx, sm, rc = (att[:, q, 0:nheads, :] for q in range(3))
            N = nheads * T
            TL, LAG = (3, 5) if causal else (2, 4)
            NB = len(bufs)
            bfr = [None] * NB
            st = [{} for _ in range(N)]
            pt_tok = {}
            pt_free = [()] * len(PTs)
            ob = [None]

            def scores_(i):
                hd, t = i // T, i % T
                half = slice(64 * (hd % 2), 64 * (hd % 2) + 64)
                n = P * (t + 1) if causal else SEQ
                b = take()
                pb = bufs[i % NB][:, 0:n]
                nm = nmx[:, hd, t:t + 1]
                tok = mm(bank[b][:, 0:n], qv[half, hd // 2, t * P:(t + 1) * P], kv_[half, hd // grp, 0:n], True, True,
                         [bfree[b]] + ready_(hd), True)
                if causal:
                    k = v(lambda e: e.tensor_tensor_reduce(pb, bank[b][:, 0:n], bias[:, t, 0:n], -0.125, 3e38,
                                                           ALU.add, ALU.min, nm), [tok, bfr[i % NB], bias_ready[t]])
                else:
                    fac = q_rms[:, t * nheads + hd:t * nheads + hd + 1]
                    k = v(lambda e: e.tensor_scalar(pb, bank[b][:, 0:n], fac, 3e38, ALU.mult, ALU.min, accum_out=nm),
                          [tok, bfr[i % NB]])
                bfree[b] = k
                st[i]["e"] = a(lambda e: e.activation(pb, pb, ACT.Exp, bias=nm, scale=-1.0,
                                                      accum_out=sm[:, hd, t:t + 1]), [k])

            def norm_(i):
                hd, t = i // T, i % T
                n = P * (t + 1) if causal else SEQ
                pb = bufs[i % NB][:, 0:n]
                k = v(lambda e: e.reciprocal(rc[:, hd, t:t + 1], sm[:, hd, t:t + 1]), [st[i]["e"]])
                st[i]["n"] = v(lambda e: e.tensor_scalar(pb, pb, rc[:, hd, t:t + 1], None, ALU.mult), [k])

            def turn_(i):
                hd, t = i // T, i % T
                n = P * (t + 1) if causal else SEQ
                pb = bufs[i % NB]
                b = take()
                for kb in range(n // P):
                    tok = tr(bank[b][:, kb * P:(kb + 1) * P], pb[:, kb * P:(kb + 1) * P], ident,
                             [bfree[b], st[i]["n"]], mark=(kb == n // P - 1))
                bfr[i % NB] = tok
                d = PTs[hd % len(PTs)][:, 0:n // P, t * P:(t + 1) * P]
                s_ = bank[b][:, 0:n].rearrange("p (k q) -> p k q", q=P)
                after = [tok, *pt_free[hd % len(PTs)]]
                if hd == 1:
                    after += list(pt_ready)
                if i % 2:
                    k = v(lambda e: e.tensor_copy(d, s_), after)
                else:
                    k = a(lambda e: e.activation(d, s_, ACT.Copy), after)
                bfree[b] = k
                pt_tok[i] = k

            def out_(hd):
                half = slice(64 * (hd % 2), 64 * (hd % 2) + 64)
                PT = PTs[hd % len(PTs)]
                if hd % 2 == 0:
                    ob[0] = take(True)
                o = bank[ob[0]]
                for kb in range(T):
                    c0 = kb * P if causal else 0
                    tok = mm(o[half, c0:SEQ], vv_(kb, hd // grp), PT[:, kb, c0:SEQ], kb == 0, kb == T - 1,
                             [pt_tok[hd * T + q] for q in range(T)] + [bfree[ob[0]] if hd % 2 == 0 else None],
                             mark=(kb == T - 1))
                pt_free[hd % len(PTs)] = (tok,)
                if hd % 2:
                    held.discard(ob[0])
                    bfree[ob[0]] = emit_o(hd // 2, o[:, :], tok)

            for i in range(N + LAG + 1):
                if i < N:
                    scores_(i)
                if 0 <= i - 1 < N:
                    norm_(i - 1)
                if 0 <= i - TL < N:
                    turn_(i - TL)
                if i >= LAG and (i - LAG) % T == T - 1 and (i - LAG) // T < nheads:
                    out_((i - LAG) // T)
                yield

        oo = []

        def emit_a(j, ps, tok):
            k = split(ps, xh[:, j, :], xl[:, j, :], [tok])
            oo.append(k)
            return k

        bufs = [gb[:, 512 * i:512 * (i + 1)] for i in range(4)]
        topped = DVE.last()
        for step, _ in enumerate(attend(bufs, [kd, tmp], qT, kT, lambda kb, gk: vt[:, kb, gk * 64:gk * 64 + 64], 16, 4,
                                        True, lambda hd: [q_turned[hd // 8], k_turned[0], v_ready, topped], emit_a)):
            if step == 3:
                q_turned.append(turn(tmp, 4, qT[:, 4:8, :], [rt]))
        tg = ln_load(ln_mix_g[0], ln_mix_b[0])
        nt = residual_out(oo, H0)
        xr, ht = ln_finish(nt, tg, LNC["mg", 0], LNC["mb", 0])
        tg = ln_load(ln_mlp_g[0], ln_mlp_b[0])
        nt = mlp(xr, ht)
        wa2 = A[0:16, 2048:2560]
        ta2 = load_gb(wa2, b_w_a2[0], [PE.last(), tg])
        xr, ht = ln_finish(nt, tg, LNC["fg", 0], LNC["fb", 0])

        gq = A[:, 0:2048].rearrange("p (h s) -> p h s", h=4)
        gk_ = A[:, 2048:4096].rearrange("p (h s) -> p h s", h=4)
        gv = A[:, 4096:8192].rearrange("p (t n) -> p t n", t=T)
        bb = A[:, 8192:10240].rearrange("p (h s) -> p h s", h=4)
        wb = [A[:, 10240 + 512 * i:10752 + 512 * i].rearrange("p (h s) -> p h s", h=4) for i in range(4)]
        ATs = [x_.rearrange("p (h s) -> p h s", h=4) for x_ in (A[:, 12288:12800], A[:, 12800:13312], gb[:, 0:512],
                                                              gb[:, 512:1024])]
        ST = gb[:, 1024:2048].rearrange("p (h n) -> p h n", h=4)
        zz = A[:, 4096:6144].rearrange("p (h s) -> p h s", h=4)
        z2 = A[:, 6144:8192].rearrange("p (h s) -> p h s", h=4)
        alow = A[0:16, 12288:12800]
        al = []

        def ev_al(j, ps, tok):
            al.append(a(lambda e: e.activation(alow, ps, ACT.Copy), [tok]))
            return al[-1]

        gemm_T(xh, xl, xr, ev_al)
        zt = None
        for q in range(4):
            b = take()
            tok = mm(bank[b][:, :], wa2[:, q * P:(q + 1) * P], alow, True, True, [al[0], ta2, bfree[b]], True)
            bfree[b] = v(lambda e, b=b, q=q: e.tensor_scalar(zz[:, q, :], bank[b][:, :], BA[:, q:q + 1], None, ALU.add),
                         [tok, S0])
        zt = DVE.last()
        t1 = a(lambda e: e.activation(z2, zz, ACT.Abs), [zt])
        t1 = a(lambda e: e.activation(z2, z2, ACT.Exp, scale=-1.0), [t1])
        t1 = v(lambda e: e.tensor_scalar(z2, z2, 1.0, None, ALU.add), [t1])
        t1 = a(lambda e: e.activation(z2, z2, ACT.Ln), [t1])
        t1 = v(lambda e: e.scalar_tensor_tensor(zz, zz, 0.0, z2, ALU.min, ALU.subtract), [t1])
        for q in range(4):
            for c in range(4):
                b_ready = v(lambda e, q=q, c=c: e.tensor_tensor_scan(
                    bb[:, q, c * P:(c + 1) * P], ones, zz[:, q, c * P:(c + 1) * P], 0.0, ALU.mult, ALU.add), [t1])
        qk_r = []
        for n in range(4):
            def ev_qk(j, ps, tok, n=n):
                i = 2 * n + j
                dst = gq[:, i, :] if i < 4 else gk_[:, i - 4, :]
                sc = 128.0 ** -0.5 if i < 4 else 1.0
                qk_r.append(a(lambda e: e.activation(dst, ps, ACT.Copy, scale=sc), [tok]))
                return qk_r[-1]
            gemm_T(xh, xl, xr, ev_qk)
        ssq = sb("ssq", [P, T, 4])
        ebl = sb("ebl", [P, 4, 4])
        qk_done = qk_r[-1]
        gb_free = [POOL.last(), DVE.last()]
        at = [None] * 4

        def levels():
            units = [(c, n) for c in range(4) for n in range(8)]
            st = [{} for _ in units]
            wfree = [None] * 4

            def blk(x4, s):
                return x4.rearrange("p h (n two s) -> p h n two s", two=2, s=s)

            def sub_(i):
                c, n = units[i]
                if n == 7:
                    return
                s = LEVELS[n]
                cs = slice(c * P, (c + 1) * P)
                bv = blk(bb[:, :, cs], s)
                ref = bv[:, :, :, 0, s - 1:s].broadcast_to([P, 4, 64 // s, s])
                w_ = blk(wb[i % 4], s)
                k = [wfree[i % 4], b_ready]
                g(lambda e: e.tensor_tensor(w_[:, :, :, 1, :], bv[:, :, :, 1, :], ref, ALU.subtract), k)
                k = g(lambda e: e.tensor_tensor(w_[:, :, :, 0, :], ref, bv[:, :, :, 0, :], ALU.subtract), k)
                st[i]["e"] = a(lambda e: e.activation(wb[i % 4], wb[i % 4], ACT.Exp, scale=0.0625), [k])

            def mul_(i):
                c, n = units[i]
                if n == 7:
                    return
                s = LEVELS[n]
                cs = slice(c * P, (c + 1) * P)
                w_, q4, k4 = blk(wb[i % 4], s), blk(gq[:, :, cs], s), blk(gk_[:, :, cs], s)
                v(lambda e: e.tensor_tensor(w_[:, :, :, 1, :], w_[:, :, :, 1, :], q4[:, :, :, 1, :], ALU.mult),
                  [st[i]["e"], qk_done])
                st[i]["m"] = v(lambda e: e.tensor_tensor(w_[:, :, :, 0, :], w_[:, :, :, 0, :], k4[:, :, :, 0, :],
                                                         ALU.mult), [st[i]["e"], qk_done])

            def pe_(i):
                c, n = units[i]
                cs = slice(c * P, (c + 1) * P)
                b = take(True)
                for q in range(4):
                    l, r = (gk_[:, q, cs], gq[:, q, cs]) if n == 7 else (wb[i % 4][:, q, :], wb[i % 4][:, q, :])
                    tok = mm(bank[b][:, q * P:(q + 1) * P], l, r, True, True,
                             [bfree[b], qk_done if n == 7 else st[i]["m"]], q == 3)
                wfree[i % 4] = tok
                st[i]["p"], st[i]["b"] = tok, b

            def put_(i):
                c, n = units[i]
                b = st[i]["b"]
                AT = ATs[c]
                if n == 0:
                    at[c] = v(lambda e: e.memset(AT, 0.0), gb_free + [al[0], ta2, PE.last()])
                mk = LM[:, n * P:(n + 1) * P].unsqueeze(1).broadcast_to([P, 4, P])
                pv = bank[b][:, :].rearrange("p (h s) -> p h s", h=4)
                at[c] = bfree[b] = v(lambda e: e.copy_predicated(AT, mk, pv), [st[i]["p"], at[c]])
                held.discard(b)

            N = len(units)
            for i in range(N + 4):
                if i < N:
                    sub_(i)
                if 0 <= i - 2 < N:
                    mul_(i - 2)
                if 0 <= i - 3 < N:
                    pe_(i - 3)
                if 0 <= i - 4 < N:
                    put_(i - 4)
                yield

        rs = small[:, 216:232]
        sqj = small[:, 320:576]
        rp = [uh[:, :, :, :].rearrange("p a f s -> p (a f s)"), ul[:, :, :, :].rearrange("p a f s -> p (a f s)")]
        vr, rr = [], {}
        y_half = {}
        zt_ = {}

        def core():
            st_ready = None
            lvl = PE.last()
            ch = [{} for _ in range(4)]

            def decays(c):
                cs = slice(c * P, (c + 1) * P)
                QE, KD = wb[c % 2], wb[2 + c % 2]
                prev_ = [lvl] if c < 2 else [ch[c - 2]["o"], ch[c - 2]["s"], ch[c - 2]["sq"]]
                t1 = a(lambda e: e.activation(QE, bb[:, :, cs], ACT.Exp, scale=0.0625), prev_)
                bl = bb[:, :, c * P + 127:c * P + 128]
                t2 = v(lambda e: e.tensor_tensor(KD, bl.broadcast_to([P, 4, P]), bb[:, :, cs], ALU.subtract), prev_)
                t2 = a(lambda e: e.activation(KD, KD, ACT.Exp, scale=0.0625), [t2])
                ch[c]["l"] = a(lambda e: e.activation(ebl[:, c, :].unsqueeze(2), bl, ACT.Exp, scale=0.0625))
                yield
                ch[c]["q"] = v(lambda e: e.tensor_tensor(QE, QE, gq[:, :, cs], ALU.mult), [t1])
                ch[c]["kd"] = v(lambda e: e.tensor_tensor(KD, KD, gk_[:, :, cs], ALU.mult), [t2])
                yield
                b = take()
                for q in range(4):
                    tok = tr(bank[b][:, q * P:(q + 1) * P], KD[:, q, :], ident, [bfree[b], ch[c]["kd"]], q == 3)
                bfree[b] = ch[c]["k"] = a(lambda e: e.activation(
                    KD, bank[b][:, :].rearrange("p (h s) -> p h s", h=4), ACT.Copy), [tok])

            dec = decays(0)
            for _ in dec:
                yield
                yield
            for c in range(4):
                QE, KD, AT = wb[c % 2], wb[2 + c % 2], ATs[c]
                made = []
                for f in range(2):
                    qs = (2 * f, 2 * f + 1)
                    b = None
                    if c < 3:
                        b = take(True)
                        for q in qs:
                            stok = mm_group(bank[b][:, (q % 2) * 256:(q % 2) * 256 + 256],
                                            [(KD[:, q, :], gv[:, c, q * 256:(q + 1) * 256])],
                                            [bfree[b], ch[c]["k"], vr[-1]])
                        ch[c]["s"] = stok
                    ob = take(True)
                    for q in qs:
                        prs = [(AT[:, q, :], gv[:, c, q * 256:(q + 1) * 256])]
                        if c:
                            prs.append((QE[:, q, :], ST[:, q, :]))
                        otok = mm_group(bank[ob][:, (q % 2) * 256:(q % 2) * 256 + 256], prs,
                                        [bfree[ob], at[c], ch[c]["q"], st_ready, vr[-1]])
                    ch[c]["o"] = otok
                    yield
                    if f and c < 3:
                        dec = decays(c + 1)
                        next(dec)
                    for q in qs if c < 3 else ():
                        o = bank[b][:, (q % 2) * 256:(q % 2) * 256 + 256]
                        if c == 0:
                            bfree[b] = v(lambda e, q=q, o=o: e.tensor_copy(ST[:, q, :], o), [stok] + gb_free)
                        else:
                            bfree[b] = v(lambda e, q=q, o=o, c=c: e.scalar_tensor_tensor(
                                ST[:, q, :], ST[:, q, :], ebl[:, c, q:q + 1], o, ALU.mult, ALU.add),
                                [stok, otok, ch[c]["l"]])
                        made.append(bfree[b])
                    held.discard(b)
                    for q in qs:
                        o = bank[ob][:, (q % 2) * 256:(q % 2) * 256 + 256]
                        dst = gv[:, c, q * 256:(q + 1) * 256]
                        k1 = a(lambda e, dst=dst, o=o: e.activation(dst, o, ACT.Copy), [otok])
                        k2 = a(lambda e, dst=dst, q=q, c=c: e.activation(
                            sqj, dst, ACT.Square, accum_out=ssq[:, c, q:q + 1]), [k1, ACTE.last()])
                        bfree[ob] = k1
                    held.discard(ob)
                st_ready = made[-1] if made else None
                ch[c]["sq"] = k2
                otoks[c] = otok
                yield
                if c < 3:
                    next(dec)
                yield
                rr[c] = rsqrt(rs[:, 4 * c:4 * c + 4], ssq[:, c, :], 4, 1.0 / 256, 1e-6, [k2, DVE.last()], 4 * c)
                yield
                for _ in dec:
                    pass
                yield
                if c:
                    halves(c - 1, 0)
                yield
            yield
            halves(3, 0)

        def halves(t, n, parts=(0, 1)):
            sl = slice(t * 1024 + n * 512, t * 1024 + n * 512 + 512)
            z = ATs[t].rearrange("p h s -> p (h s)")
            if 0 in parts:
                k = v(lambda e: e.tensor_tensor(z, rp[0][:, sl].bitcast(F), rp[1][:, sl].bitcast(F), ALU.add),
                      [r_done[t, n], rr[t], y_half.get((t, 0)), otoks[t]])
                zt_[t] = a(lambda e: e.activation(z, z, ACT.Silu), [k])
            if 1 not in parts:
                return
            k = zt_[t]
            for q in (2 * n, 2 * n + 1):
                o = gv[:, t, q * 256:(q + 1) * 256]
                y_half[t, n] = v(lambda e, o=o, q=q: e.scalar_tensor_tensor(
                    o, o, rs[:, t * 4 + q:t * 4 + q + 1], z[:, (q % 2) * 256:(q % 2) * 256 + 256], ALU.mult, ALU.mult),
                    [k, rr[t]])

        r_done = {}
        otoks = {}

        def both():
            yield from levels()
            yield from core()

        background.append(both())
        for n in range(2):
            def ev_v(t, ps, tok, n=n):
                vr.append(a(lambda e: e.activation(gv[:, t, n * 512:(n + 1) * 512], ps, ACT.Copy), [tok, b_ready]))
                return vr[-1]
            gemm_tok(512, xh, xl, xr, ev_v, 2)
        uf_ = [PE.last()]
        for n in range(2):
            def ev_r(t, ps, tok, n=n):
                sl = slice(t * 1024 + n * 512, t * 1024 + n * 512 + 512)
                r_done[t, n] = split(ps, rp[0][:, sl], rp[1][:, sl], [tok] + uf_)
                return r_done[t, n]
            gemm_tok(512, xh, xl, xr, ev_r, 2)
        drain()
        for part in range(2):
            for t in range(T):
                halves(t, 1, (part,))
        yt = [y_half[t, 1] for t in range(T)]
        xr = to_T(gv, yt, GNC)
        tg = ln_load(ln_mix_g[1], ln_mix_b[1])
        nt = residual_out(xr, ht)
        xr, ht = ln_finish(nt, tg, LNC["mg", 1], LNC["mb", 1])

        def rms_sum(t, tok, junk):
            return a(lambda e: e.activation(junk, h[:, t, :], ACT.Square, accum_out=ssq[:, t, 0:1]), [tok, ACTE.last()])

        def rms_root(t, k):
            return rsqrt(ln_rs[:, t:t + 1], ssq[:, t, 0:1], 1, 1.0 / D, 1e-6, [k], 32 + t)

        def rms_row(t, dst, k):
            k = rms_root(t, k)
            return a(lambda e: e.activation(dst[:, t, :], h[:, t, :], ACT.Copy, scale=ln_rs[:, t:t + 1]), [k])

        xn = A[:, 6144:10240].rearrange("p (t n) -> p t n", t=T)
        tg = ln_load(ln_mlp_g[1], ln_mlp_b[1])
        xn_t = [None] * T
        sq_t = [None] * T

        gain_t = [None] * T

        def shift3(t):
            ht2[t] = v(lambda e: e.tensor_tensor(h[:, t, :], h[:, t, :], gb[:, D:2 * D], ALU.add), [gain_t[t]])
            sq_t[t] = rms_sum(t, ht2[t], A[:, 10240:11264])

        def finish3(t, tok):
            k = ln_rows(t, tok)
            e_ = v if t == T - 1 else g
            if t:
                shift3(t - 1)
            if t > 1:
                xn_t[t - 2] = rms_row(t - 2, xn, sq_t[t - 2])
            gain_t[t] = e_(lambda e: e.tensor_tensor(h[:, t, :], h[:, t, :], gb[:, 0:D], ALU.mult), [k, tg])
            return gain_t[t]

        ht2 = [None] * T
        nt = mlp(xr, ht, finish3)
        ht = ht2
        md = DVE.last()
        t1 = v(lambda e: e.tensor_scalar(CS1, SC1, 1.0, None, ALU.add), [md])
        cs1 = v(lambda e: e.tensor_tensor(CS1, CS1, GM, ALU.mult), [t1])
        t1 = v(lambda e: e.tensor_scalar(CS2, SC2, 1.0, None, ALU.add), [md])
        cs2 = v(lambda e: e.tensor_tensor(CS2, CS2, GF, ALU.mult), [t1])
        shift3(T - 1)
        for t in (T - 2, T - 1):
            xn_t[t] = rms_row(t, xn, sq_t[t])
        xr = to_T(xn, xn_t, CS1, SH1, cs1)

        ym = A[:, 0:2048].rearrange("p (t n) -> p t n", t=T)
        qT2 = A[:, 2048:4096].rearrange("p (j s) -> p j s", j=4)
        kT2 = A[:, 4096:5120].rearrange("p (j s) -> p j s", j=2)
        v2 = A[:, 5120:5632].rearrange("p (t n) -> p t n", t=T)
        mqk = A[:, 5632:9728].rearrange("p (j s) -> p j s", j=8)
        vx = A[:, 9728:11808].rearrange("p (t h n) -> p t h n", t=T, h=4)
        tm = A[:, 7680:9728].rearrange("p (t n) -> p t n", t=T)
        tm2 = A[:, 0:2048].rearrange("p (t n) -> p t n", t=T)
        kd2 = A[:, 11808:12832].rearrange("p (t n) -> p t n", t=T)
        gqn, gkn = col(320, 64), col(384, 64)
        load_gb(gqn, q_norm_g_2[0].partition_broadcast(P), [md])
        tgq = load_gb(gkn, k_norm_g_2[0].partition_broadcast(P), ())
        s32 = sb("s32", [P, 16])

        def norm_rope(x4, w4, nh, gain, tab, after, done, col_of):
            x1, w1 = x4.rearrange("p t g k -> p (t g k)"), w4.rearrange("p t g k -> p (t g k)")
            k = a(lambda e: e.activation(w1, x1, ACT.Square), after)
            ct, st_ = tab[:, 0:256], tab[:, 256:512]
            tf = [DVE.last(), ACTE.last(), PE.last()]
            kc = v(lambda e: e.tensor_tensor(ct.rearrange("p (t k) -> p t k", t=T),
                                             C[:, C_RC:C_RC + 256].rearrange("p (t k) -> p t k", t=T),
                                             gain.unsqueeze(1).broadcast_to([P, T, 64]), ALU.mult), [tgq] + tf)
            g4 = gain.rearrange("p (r a k) -> p r a k", r=2, a=2)
            s5 = st_.rearrange("p (t r a k) -> p t r a k", t=T, r=2, a=2)
            c5 = C[:, C_RS:C_RS + 256].rearrange("p (t r a k) -> p t r a k", t=T, r=2, a=2)
            for q in range(2):
                ks = v(lambda e, q=q: e.tensor_tensor(s5[:, :, :, q, :], c5[:, :, :, q, :],
                                                      g4[:, :, 1 - q, :].unsqueeze(1).broadcast_to([P, T, 2, 16]),
                                                      ALU.mult), [tgq] + tf)
            yield
            k = v(lambda e: e.tensor_reduce(col_of.rearrange("p (t g) -> p t g", t=T), w4, AX, ALU.add), [k])
            yield
            kr = rsqrt(col_of, col_of, T * nh, 1.0 / 64, 1e-6, [k])
            k3 = None
            for t in range(T):
                yield
                rcv = ct[:, t * 64:t * 64 + 64].unsqueeze(1).broadcast_to([P, nh, 64])
                xv = x4[:, t].rearrange("p g (r a k) -> p g r a k", r=2, a=2)
                wv = w4[:, t].rearrange("p g (r a k) -> p g r a k", r=2, a=2)
                for q in range(2):
                    sv = s5[:, t, :, q, :].unsqueeze(1).broadcast_to([P, nh, 2, 16])
                    k1 = v(lambda e, wv=wv, xv=xv, sv=sv, q=q: e.tensor_tensor(wv[:, :, :, q, :], xv[:, :, :, 1 - q, :], sv,
                                                                             ALU.mult), [k, ks])
                k2 = v(lambda e, t=t, rcv=rcv: e.tensor_tensor(x4[:, t], x4[:, t], rcv, ALU.mult), [k1, kc])
                k3 = v(lambda e, t=t: e.tensor_tensor(x4[:, t], x4[:, t], w4[:, t], ALU.add), [k1, k2])
            if nh == 8:
                k3 = v(lambda e: e.tensor_scalar(col_of, col_of, -0.125, None, ALU.mult), [kr])
            else:
                yield
                rsb = col_of.rearrange("p (t g) -> p t g", t=T).unsqueeze(3).broadcast_to([P, T, nh, 64])
                k3 = v(lambda e: e.tensor_tensor(x4, x4, rsb, ALU.mult), [kr, k3])
            done.append(k3)

        ev = []

        def ev_q2(t, ps, tok):
            ev.append(a(lambda e: e.activation(tm[:, t, :], ps, ACT.Copy), [tok]))
            return ev[-1]

        gemm_tok(512, xh, xl, xr, ev_q2)
        q2_ev = ev[-1]
        qd, kdn = [], []
        q_rms = sb("q_rms", [P, 32])
        gg = sb("gg", [P, T, 16])
        g2_ = sb("g2_", [P, T, 16])
        acol = sb("acol", [P, 2, T, 4])
        ecol = sb("ecol", [P, 2, T, 4])
        den = sb("den", [P, 2, 2, 2])
        Mr = [A[32 * d:32 * d + 4, 12832:13344] for d in range(2)]
        ev = []

        ggf = A[0:16, 12832:13344]
        gr = []
        evk = []
        turned = []
        mrdy = [None, None]
        cols = [None, None]

        def small_jobs():
            yield from norm_rope(tm.rearrange("p t (g k) -> p t g k", k=64), tm2.rearrange("p t (g k) -> p t g k", k=64),
                                 8, gqn, gb[:, 1032:1544], [q2_ev], qd, q_rms[:, :])
            yield
            yield
            turned.append(turn(tm, 4, qT2, qd))
            yield from norm_rope(kd2.rearrange("p t (g k) -> p t g k", k=64),
                                 A[:, 0:1024].rearrange("p (t g k) -> p t g k", t=T, k=64), 4, gkn, gb[:, 1032:1544], [evk[-1], qd[0]], kdn, s32[:, 0:16])
            yield
            yield
            turned.append(turn(kd2, 2, kT2, kdn))
            b = take()
            for t in range(T):
                tok = tr(bank[b][:, t * 16:(t + 1) * 16], ggf[:, t * P:(t + 1) * P], ident[0:16, 0:16],
                         [bfree[b], gr[0]], t == T - 1)
            k = bfree[b] = v(lambda e: e.tensor_tensor(gg[:, :, :], bank[b][:, 0:16 * T].rearrange("p (t n) -> p t n", t=T),
                                                       GB.unsqueeze(1).broadcast_to([P, T, 16]), ALU.add), [tok, S0])
            k = a(lambda e: e.activation(g2_[:, :, :], gg[:, :, :], ACT.Abs), [k])
            k = a(lambda e: e.activation(g2_[:, :, :], g2_[:, :, :], ACT.Exp, scale=-1.0), [k])
            yield
            k = v(lambda e: e.tensor_scalar(g2_[:, :, :], g2_[:, :, :], 1.0, None, ALU.add), [k])
            k = a(lambda e: e.activation(g2_[:, :, :], g2_[:, :, :], ACT.Ln), [k])
            yield
            lf = v(lambda e: e.scalar_tensor_tensor(g2_[:, :, :], gg[:, :, :], 0.0, g2_[:, :, :], ALU.min, ALU.subtract),
                   [k])
            yield

            def gates(d):
                p = slice(32 * d, 32 * d + 4)
                free = [DVE.last(), ACTE.last(), PE.last()]
                ir, fr, onerow = A[p, 0:512], A[p, 512:1024], A[p, 1024:1536]
                rv = (lambda ap: ap) if d == 0 else (lambda ap: ap[:, ::-1])
                k1r = v(lambda e: e.memset(onerow, 1.0), free)
                bi, bf = take(), take()
                for t in range(T):
                    tok = tr(bank[bi][0:4, t * P:(t + 1) * P], gg[:, t, 8 * d:8 * d + 4], ident, [bfree[bi], lf], t == T - 1)
                for t in range(T):
                    tok2 = tr(bank[bf][0:4, t * P:(t + 1) * P], g2_[:, t, 8 * d + 4:8 * d + 8], ident, [bfree[bf], lf],
                              t == T - 1)
                ki = a(lambda e: e.activation(ir, bank[bi][0:4, :], ACT.Copy), [tok] + free)
                kf = a(lambda e: e.activation(Mr[d], bank[bf][0:4, :], ACT.Copy), [tok2] + free)
                bfree[bi], bfree[bf] = ki, kf
                yield
                k = v(lambda e: e.tensor_tensor_scan(rv(fr), onerow, rv(Mr[d]), 0.0, ALU.mult, ALU.add), [kf, k1r])
                ka = v(lambda e: e.tensor_tensor(ir, ir, fr, ALU.subtract), [k, ki])
                km = v(lambda e: e.tensor_tensor_scan(rv(Mr[d]), rv(ir), rv(ir), 0.0, ALU.max, ALU.max), [ka])
                mrdy[d] = km
                kn = v(lambda e: e.tensor_tensor(fr, fr, Mr[d], ALU.add), [km])
                yield
                yield
                b = take()
                for t in range(T):
                    tr(bank[b][:, t * 4:t * 4 + 4], ir[:, t * P:(t + 1) * P], ident[p, p], [bfree[b], ka])
                    tok = tr(bank[b][:, 16 + t * 4:20 + t * 4], fr[:, t * P:(t + 1) * P], ident[p, p], [kn], t == T - 1)
                a(lambda e: e.activation(acol[:, d, :, :], bank[b][:, 0:16].rearrange("p (t h) -> p t h", t=T), ACT.Copy),
                  [tok])
                cols[d] = bfree[b] = a(lambda e: e.activation(
                    ecol[:, d, :, :], bank[b][:, 16:32].rearrange("p (t h) -> p t h", t=T), ACT.Exp, scale=-1.0), [tok])

            yield from gates(0)
            yield from gates(1)

        background.append(small_jobs())

        def ev_k2(t, ps, tok):
            kk = kd2[:, t, :].rearrange("p (g q k) -> p g q k", g=2, q=2)
            pk = ps[:, 0:128].rearrange("p (g k) -> p g k", g=2)
            for q in range(2):
                a(lambda e, q=q: e.activation(kk[:, :, q, :], pk, ACT.Copy), [tok])
            evk.append(a(lambda e: e.activation(v2[:, t, :], ps[:, 128:256], ACT.Copy), [tok]))
            return evk[-1]

        gemm_tok(256, xh, xl, xr, ev_k2, 1)

        ev = []

        def ev_g(j, ps, tok):
            ev.append(a(lambda e: e.activation(ggf, ps, ACT.Copy), [tok]))
            return ev[-1]

        gemm_T(xh, xl, xr, ev_g, 2)
        gr.append(ev[-1])
        ev = []

        def ev_v2(t, ps, tok):
            ev.append(a(lambda e: e.activation(vx[:, t, :, 0:128], ps.rearrange("p (h n) -> p h n", h=4), ACT.Copy), [tok]))
            return ev[-1]

        vx1 = v(lambda e: e.memset(vx[:, :, :, 128:130], 1.0), [PE.last(), ACTE.last()])
        gemm_tok(512, xh, xl, xr, ev_v2, 2)
        vx_ready = ev[-1]
        Wo = []
        pads = [gb[:, 0:516], gb[:, 514:1030]]
        kz = v(lambda e: e.memset(gb[:, 0:1030], 0.0), [ht[-1]])
        pfr = [kz, kz]
        cvt, owed_silu = [], []

        def silu_owed():
            while owed_silu:
                yo, ko = owed_silu.pop(0)
                cvt.append(a(lambda e: e.activation(yo, yo, ACT.Silu), [ko]))

        for n in range(4):
            def ev_c(j, ps, tok, n=n):
                i = 2 * n + j
                assert turned or i < 4
                pad, y_ = pads[i % 2], mqk[:, i, :]
                k0 = a(lambda e: e.activation(pad[:, 2:514], ps, ACT.Copy), [tok, pfr[i % 2]])
                k = a(lambda e: e.activation(y_, pad[:, 0:512], ACT.Identity, bias=CVB[:, i:i + 1], scale=CW[:, 0, i:i + 1]),
                      [k0, S0])
                silu_owed()
                for w in range(1, 5):
                    k = v(lambda e, w=w: e.scalar_tensor_tensor(y_, pad[:, w:w + 512], CW[:, w, i:i + 1], y_,
                                                               ALU.mult, ALU.add), [k])
                pfr[i % 2] = k
                owed_silu.append((y_, k))
                return k0
            gemm_T(xh, xl, xr, ev_c, 2, (lambda: Wo.extend([next_chunk(), next_chunk(False)])) if n == 3 else None)
        silu_owed()
        while len(turned) < 2:
            tick()
        rest = list(background)
        background.clear()
        qk_ready = cvt[-1]
        q2r, k2r = turned
        v2r = evk[-1]
        core0 = [DVE.last(), ACTE.last(), PE.last()]
        rawf = raw[:, :, :].rearrange("p a n -> p (a n)")
        STm = rawf[:, 2048:4096].rearrange("p (b s) -> p b s", b=T)
        PTs = [rawf[:, 0:2048].rearrange("p (b s) -> p b s", b=T), gb[:, 0:2048].rearrange("p (b s) -> p b s", b=T)]
        PB2 = [rawf[:, 4096 + 512 * i:4608 + 512 * i] for i in range(3)]
        Dd = rawf[:, 5632:6144]
        Db = [A[:, 11808:12320], A[:, 12320:12832]]
        SCL = 128.0 ** -0.5
        hm = [None]
        oh = uh[:, 1, :, :]
        ol = ul[:, 1, :, :]
        o_t = [None] * T
        sq_h = [None]

        def gate_products():
            for t in range(T):
                b = take(True)
                for k in range(8):
                    H, L, rw = Wo[k // 4][0:3]
                    X, Y = xh[:, k, t * P:(t + 1) * P], xl[:, k, t * P:(t + 1) * P]
                    mm(bank[b][:, :], X, H[:, k % 4, :], k == 0, False, [rw, bfree[b]])
                    mm(bank[b][:, :], X, L[:, k % 4, :], False, False)
                    tok = mm(bank[b][:, :], Y, H[:, k % 4, :], False, k == 7, mark=(k == 7))
                    if k == 7:
                        o_t[t] = bfree[b] = split(bank[b][:, :], oh[:, t, :], ol[:, t, :], [tok])
                        held.discard(b)
                    yield
            for w in Wo:
                hl_free[w[3]] = PE.last()

        def memory():
            for job in rest:
                yield from job
            bMs = {}
            st_free = cols[1]
            dd_free = None
            dfree = [cols[1]] * 2
            nd = 0
            jobs = [(hh, d) for hh in range(4) for d in range(2)]

            def start(m):
                hh, d = jobs[m]
                bM = take(True)
                sel = ident[32 * d:32 * d + 4, 32 * d + hh:32 * d + hh + 1].broadcast_to([4, P])
                mtok = mm(bank[bM][:, :], sel, Mr[d], True, True, [bfree[bM], mrdy[d]], True)
                mk = CBT if d == 0 else CB
                for s in range(T):
                    c = slice(s * P, (s + 1) * P)
                    k = v(lambda e, s=s, c=c: e.scalar_tensor_tensor(Dd[:, c], bank[bM][:, c], acol[:, d, s, hh:hh + 1], mk,
                                                                     ALU.subtract, ALU.min, reverse0=True),
                          [mtok, cols[1], dd_free] + core0)
                bMs[m] = (bM, a(lambda e: e.activation(Dd, Dd, ACT.Exp), [k]))

            start(0)
            for m, (hh, d) in enumerate(jobs):
                bM, dk = bMs[m]
                for s in range(T):
                    yield
                    c0, c1_ = (s * P, SEQ) if d == 0 else (0, (s + 1) * P)
                    n = c1_ - c0
                    o0, o1 = ((s + 1) * P, SEQ) if d == 0 else (0, s * P)
                    b = take()
                    tok = mm(bank[b][:, 0:n], mqk[:, 4 + hh, s * P:(s + 1) * P], mqk[:, hh, c0:c1_], True, True,
                             [bfree[b], qk_ready], True)
                    if o1 > o0:
                        i = nd % 2
                        nd += 1
                        dv = Db[i][:, 0:o1 - o0]
                        k = a(lambda e, dv=dv, o0=o0, o1=o1, bM=bM, d=d, s=s, hh=hh: e.activation(
                            dv, bank[bM][:, o0:o1], ACT.Exp, bias=acol[:, d, s, hh:hh + 1], scale=-1.0), [dk, dfree[i]])
                        bfree[bM] = k
                        k = v(lambda e, b=b, dv=dv, o0=o0, o1=o1, c0=c0, s=s: e.scalar_tensor_tensor(
                            STm[:, s, o0:o1], bank[b][:, o0 - c0:o1 - c0], SCL, dv, ALU.mult, ALU.mult), [tok, k, st_free])
                        dfree[i] = k
                    c = slice(s * P, (s + 1) * P)
                    k = v(lambda e, b=b, c=c, c0=c0, s=s: e.scalar_tensor_tensor(
                        STm[:, s, c], bank[b][:, s * P - c0:(s + 1) * P - c0], SCL, Dd[:, c], ALU.mult, ALU.mult),
                        [tok, dk, st_free])
                    bfree[b] = k
                    sr = k
                held.discard(bM)
                dd_free = sr
                yield
                if m + 1 < len(jobs):
                    start(m + 1)
                for tt in range(2):
                    yield
                    b = take()
                    for t in (2 * tt, 2 * tt + 1):
                        src = range(0, t + 1) if d == 0 else range(t, T)
                        o = (t % 2) * 256
                        tok = mm_group(bank[b][:, o:o + 130], [(STm[:, q, t * P:(t + 1) * P], vx[:, q, hh, :]) for q in src],
                                       [bfree[b], sr, vx_ready, vx1])
                    dn = den[:, m % 2, tt, :]
                    k = a(lambda e, dn=dn, b=b: e.activation(dn, bank[b][:, 128:512:256], ACT.Abs), [tok, DVE.last()])
                    k = v(lambda e, dn=dn, d=d, tt=tt, hh=hh: e.tensor_tensor(dn, dn, ecol[:, d, 2 * tt:2 * tt + 2, hh],
                                                                           ALU.max), [k, cols[1]])
                    k = v(lambda e, dn=dn: e.reciprocal(dn, dn), [k])
                    for t in (2 * tt, 2 * tt + 1):
                        o = (t % 2) * 256
                        yv = ym[:, t, hh * P:(hh + 1) * P]
                        dc = dn[:, t % 2:t % 2 + 1]
                        if d == 0:
                            hm[0] = v(lambda e, yv=yv, b=b, dc=dc, o=o: e.tensor_scalar(
                                yv, bank[b][:, o:o + P], dc, None, ALU.mult), [k])
                        else:
                            hm[0] = v(lambda e, yv=yv, b=b, dc=dc, o=o: e.scalar_tensor_tensor(
                                yv, bank[b][:, o:o + P], dc, yv, ALU.mult, ALU.add), [k])
                    bfree[b] = hm[0]
                    if d:
                        for t in (2 * tt, 2 * tt + 1):
                            sq_h[0] = a(lambda e, t=t, hh=hh: e.activation(
                                sqj[:, 128:256], ym[:, t, hh * P:(hh + 1) * P], ACT.Square,
                                accum_out=ssq[:, t, hh:hh + 1]), [hm[0], ACTE.last()])
                st_free = PE.last()

        y2 = []

        def emit_2(j, ps, tok):
            y2.append(split(ps, uh[:, 0, j, :], ul[:, 0, j, :], [tok]))
            return y2[-1]

        heads = attend(PB2, PTs, qT2, kT2, lambda kb, gk: v2[:, kb, gk * 64:gk * 64 + 64], 8, 4, False,
                       lambda hd: [q2r, k2r, v2r, Wo[1][2]], emit_2, core0)
        mem = memory()
        products = gate_products()
        live = [heads, mem, products, mem]
        while live:
            for gen in list(live):
                if gen in live and next(gen, background) is background:
                    live = [x_ for x_ in live if x_ is not gen]
        release([DVE.last(), ACTE.last(), PE.last()])
        free = [PE.last(), ACTE.last(), DVE.last()]
        yt = [None] * T
        for t in range(T):
            z = gb[:, t * 512:(t + 1) * 512]
            k1 = v(lambda e, z=z, t=t: e.tensor_tensor(z, oh[:, t, :].bitcast(F), ol[:, t, :].bitcast(F), ALU.add),
                   [o_t[t]] + free)
            yt[t] = a(lambda e, z=z: e.activation(z, z, ACT.Sigmoid), [k1])
        k = rsqrt(rs, ssq[:, :, :].rearrange("p t h -> p (t h)"), 16, 1.0 / 128, 1e-6, [sq_h[0], DVE.last()])
        for t in range(T):
            z = gb[:, t * 512:(t + 1) * 512]
            for hh in range(4):
                yv = ym[:, t, hh * P:(hh + 1) * P]
                k1 = v(lambda e, yv=yv, t=t, hh=hh, z=z: e.scalar_tensor_tensor(
                    yv, yv, rs[:, 4 * t + hh:4 * t + hh + 1], z[:, hh * P:(hh + 1) * P], ALU.mult, ALU.mult), [k, yt[t]])
            yt[t] = k1
        G1, G2 = A[:, 4096:5120], A[:, 5120:6144]
        for gc, G in ((GC1, G1), (GC2, G2)):
            for c in range(2):
                b = take()
                for j in range(4):
                    kk = 4 * c + j
                    tok = mm(bank[b][:, j * P:(j + 1) * P], gc[:, kk:kk + 1].broadcast_to([P, P]), ident, True, True,
                             [bfree[b], md], j == 3)
                G_ready = bfree[b] = a(lambda e, b=b, G=G, c=c: e.activation(G[:, c * 512:(c + 1) * 512], bank[b][:, :],
                                                                          ACT.Copy), [tok])
        assert prepped[0] == used[0]
        split_chunk(prepped[0])
        prepped[0] += 1
        yr = [y2[-1]] * 4
        bs = [take(True) for _ in range(4)]
        for t in range(T):
            for j in range(4):
                tok = tr(bank[bs[j]][:, t * P:(t + 1) * P], ym[:, t, j * P:(j + 1) * P], ident, [bfree[bs[j]], yt[t]], t == T - 1)
                if t == T - 1:
                    ps, c = bank[bs[j]][:, :], MNC[:, j:j + 1]
                    t1 = a(lambda e, ps=ps, c=c, j=j: e.activation(uh[:, 1, j, :], ps, ACT.Copy, scale=c), [tok])
                    bfree[bs[j]] = v(lambda e, ps=ps, c=c, j=j: e.scalar_tensor_tensor(
                        ul[:, 1, j, :], ps, c, uh[:, 1, j, :].bitcast(F), ALU.mult, ALU.subtract), [t1])
                    yr.append(bfree[bs[j]])
        held.difference_update(bs)
        fg = gb[:, 0:1024]
        tfg = load_gb(fg, final_norm_g_2.partition_broadcast(P), [DVE.last(), ACTE.last(), PE.last()])
        nt = [None] * T
        junk = A[:, 6144:7168]
        mo = [A[:, 7168:7680], A[:, 7680:8192]]
        mof = [DVE.last()] * 2
        xo = A[:, 0:4096].rearrange("p (t n) -> p t n", t=T)
        sq_t = [None] * T

        def ev_w(t, c, ps, tok):
            m = mo[c]
            k0 = mof[c] = v(lambda e: e.tensor_tensor(m, ps, G1[:, c * 512:(c + 1) * 512], ALU.mult), [tok, G_ready, mof[c]])
            hv = h[:, t, c * 512:(c + 1) * 512]
            ht[t] = mof[c] = v(lambda e: e.tensor_tensor(hv, hv, m, ALU.add), [k0, ht[t]])
            if c:
                sq_t[t] = rms_sum(t, ht[t], junk)
                if t:
                    nt[t - 1] = rms_row(t - 1, xo, sq_t[t - 1])
            return k0

        gemm_pair(uh[:, :, :, :].rearrange("p a f s -> p (a f) s"), ul[:, :, :, :].rearrange("p a f s -> p (a f) s"),
                  yr, ev_w)
        nt[T - 1] = rms_row(T - 1, xo, sq_t[T - 1])
        xr = to_T(xo, nt, CS2, SH2)
        facc = A[:, 8192:12288].rearrange("p (t n) -> p t n", t=T)
        ub = A[:, 0:4096].rearrange("p (i s) -> p i s", i=8)
        uf = [PE.last()] * 8
        ft = [None] * T
        urdy = {}
        nu = [0]
        u_free[0] = u_free[1] = PE.last()
        LASTF = len(FG) - 1

        def finish4(t):
            k = rms_root(t, sq_t[t])
            k = v(lambda e: e.scalar_tensor_tensor(facc[:, t, :], h[:, t, :], ln_rs[:, t:t + 1], fg, ALU.mult, ALU.mult),
                  [k, tfg, ht[t]])
            SP.put([k], lambda e: e.dma_start(out[0, t * P:(t + 1) * P, :], facc[:, t, :]).then_inc(s_out, 16), mark=False)

        def ev_down(n, t, c, ps, tok):
            fv = facc[:, t, c * 512:(c + 1) * 512]
            hv = h[:, t, c * 512:(c + 1) * 512]
            g2v = G2[:, c * 512:(c + 1) * 512]
            if n == LASTF:
                k0 = v(lambda e: e.tensor_tensor(fv, ps, g2v, ALU.mult), [tok, ht[t]])
                ht[t] = v(lambda e: e.tensor_tensor(hv, hv, fv, ALU.add), [k0])
                if c:
                    sq_t[t] = rms_sum(t, ht[t], junk)
                    if t:
                        finish4(t - 1)
                return k0
            if n == 0:
                ft[t] = v(lambda e: e.tensor_copy(fv, ps), [tok])
            else:
                ft[t] = v(lambda e: e.tensor_tensor(fv, fv, ps, ALU.add), [tok, ft[t]])
            k0 = ft[t]
            if n == LASTF - 1:
                k = v(lambda e: e.tensor_tensor(fv, fv, g2v, ALU.mult), [k0])
                ht[t] = v(lambda e: e.tensor_tensor(hv, hv, fv, ALU.add), [k, ht[t]])
            return k0

        for n in range(len(FG) + 1):
            if n < len(FG):
                for q in range(FG[n][1] // 2):
                    gt = {}

                    def ev_gate(j, ps, tok):
                        i = 2 * (nu[0] % 4) + j
                        gx = ub[:, i, :]
                        gt[j] = a(lambda e: e.activation(gx, ps, ACT.Silu), [tok, uf[i]])
                        return gt[j]

                    def ev_up(j, ps, tok, q=q, n=n):
                        i = 2 * (nu[0] % 4) + j
                        gx = ub[:, i, :]
                        k1 = v(lambda e: e.tensor_tensor(gx, gx, ps, ALU.mult), [tok, gt[j]])
                        fi = 2 * q + j
                        uf[i] = urdy[n] = split(gx, uh[:, n % 2, fi, :], ul[:, n % 2, fi, :], [k1, u_free[n % 2]])
                        return k1

                    gemm_T(xh, xl, xr, ev_gate)
                    gemm_T(xh, xl, xr, ev_up)
                    nu[0] += 1
            if n > 0:
                down(n - 1, FG[n - 1][1], urdy[n - 1], ev_down, n == len(FG))
        finish4(T - 1)
        SP.put([(s_out, 16 * T)], lambda e: None, mark=False)
        assert used[0] == len(chunks), (used[0], len(chunks))

        block = ctx.enter_context(nc.Block())

        @block.sync
        def _(e):
            for f in SP.todo:
                f(e)

        @block.gpsimd
        def _(e):
            for f in POOL.todo:
                f(e)

        @block.scalar
        def _(e):
            for f in ACTE.todo:
                f(e)

        @block.tensor
        def _(e):
            for f in PE.todo:
                f(e)

        @block.vector
        def _(e):
            for f in DVE.todo:
                f(e)


NAMES = ["x", "positions", "a_w_in", "a_w_o", "b_w_in", "b_w_a2", "b_b_a", "b_g_norm", "b_w_o", "ln_mix_g", "ln_mix_b",
         "mlp_w_up", "mlp_w_down", "ln_mlp_g", "ln_mlp_b", "c_2", "w_ada_2", "b_ada_2", "norm_mix_g_2", "w_in_2",
         "q_norm_g_2", "k_norm_g_2", "conv_w_2", "conv_b_2", "gate_b_2", "mlstm_norm_g_2", "w_out_2", "norm_ffn_g_2",
         "w_gate_2", "w_up_2", "w_down_2", "final_norm_g_2"]


def packed(inputs):
    def by_part(a):
        return np.asarray(a).reshape(-1, P).T

    pad = np.zeros((P, 4), np.float32)
    cols = [by_part(inputs["b_b_a"]), pad, by_part(inputs["c_2"]), by_part(inputs["norm_mix_g_2"]),
            by_part(inputs["norm_ffn_g_2"]), by_part(inputs["conv_w_2"]), by_part(inputs["conv_b_2"])]
    cols += [by_part(inputs[n][i]) for n in ("ln_mix_g", "ln_mix_b", "ln_mlp_g", "ln_mlp_b") for i in range(2)]
    cols += [by_part(inputs["b_ada_2"])] + [by_part(inputs["b_g_norm"])] * 4 + [by_part(inputs["mlstm_norm_g_2"])]
    return np.ascontiguousarray(np.concatenate(cols, 1)), np.ascontiguousarray(by_part(inputs["positions"]))


def kernel(**inputs):
    import concourse.bacc as bacc
    from concourse.bass_utils import run_bass_kernel_spmd

    nc = bacc.Bacc("TRN2", target_bir_lowering=False, num_devices=1)
    arrays, args = {}, []
    given = {n: np.ascontiguousarray(inputs[n]) for n in NAMES}
    given["cst"], given["lmask"] = constants()
    given["cols"], given["posn"] = packed(inputs)
    for name, arr in given.items():
        arrays["in_" + name] = arr
        args.append(nc.dram_tensor("in_" + name, arr.shape, mybir.dt.from_np(arr.dtype), kind="ExternalInput").ap())
    out = nc.dram_tensor("out_0", (1, SEQ, D), F, kind="ExternalOutput").ap()
    program(nc, *args, out)
    r = run_bass_kernel_spmd(nc, [arrays], core_ids=[0])
    return r.results[0]["out_0"]
```
